# Optimizing a Trainium2 kernel written in Bass

```python
import math
import jax, jax.numpy as jnp
from jax import lax
import numpy as np

D_MODEL = 1024
BATCH = 1
SEQ = 128
DEPTH = 2
DEC_BATCH = 1
DEC_SEQ = 256
PAST_LEN = 128

GRID_W = 64
ROPE_BASE = 10000.0
EPS = 1e-6
Q_BLOCK = 128
MLA_HEADS = 8
MLA_NOPE = 64
MLA_ROPE = 32
MLA_V = 64
MLA_Q_RANK = 384
MLA_KV_RANK = 256
GQA_HEADS = 8
GQA_KV_HEADS = 2
GQA_DIM = 64
DIFF_HEADS = 4
DIFF_DIM = 64
DIFF_V = 2 * DIFF_DIM
N_EXPERTS = 16
EXPERT_FF = 1024
CAPACITY_FACTOR = 2
N_BRANCH = 3
IN_SIZES = (MLA_Q_RANK, MLA_KV_RANK, MLA_ROPE,
            GQA_HEADS * GQA_DIM, GQA_KV_HEADS * GQA_DIM, GQA_KV_HEADS * GQA_DIM,
            DIFF_HEADS * 2 * DIFF_DIM, DIFF_HEADS * 2 * DIFF_DIM, DIFF_HEADS * DIFF_V,
            D_MODEL, D_MODEL, D_MODEL)
IN_COLS = sum(IN_SIZES)

kernel_name = 'hybrid_diffusion_mla_gqa_diffattn_ec_step'

def rmsnorm(x, g):
    xf = x.astype(jnp.float32)
    y = xf * lax.rsqrt(jnp.mean(xf * xf, axis=-1, keepdims=True) + EPS)
    return (y * g.astype(jnp.float32)).astype(x.dtype)

def rope_1d(x, pos):
    half = x.shape[-1] // 2
    freqs = ROPE_BASE ** (-jnp.arange(half, dtype=jnp.float32) / half)
    ang = pos[:, None] * freqs[None, :]
    cos = jnp.cos(ang)[:, None, :].astype(x.dtype)
    sin = jnp.sin(ang)[:, None, :].astype(x.dtype)
    x1, x2 = x[..., :half], x[..., half:]
    return jnp.concatenate([x1 * cos - x2 * sin, x1 * sin + x2 * cos], axis=-1)

def rope_2d(x, row, col):
    half = x.shape[-1] // 2
    return jnp.concatenate([rope_1d(x[..., :half], row), rope_1d(x[..., half:], col)], axis=-1)

def attend(q, k, v):
    b, tq, h, dk = q.shape
    g = k.shape[2]
    rep = h // g
    dv = v.shape[-1]
    scale = dk ** -0.5
    qb = q.reshape(b, tq // Q_BLOCK, Q_BLOCK, g, rep, dk).transpose(1, 0, 2, 3, 4, 5)

    def one_block(qblk):
        s = jnp.einsum('bqgrd,bkgd->bgrqk', qblk, k, preferred_element_type=jnp.float32) * scale
        p = jax.nn.softmax(s, axis=-1).astype(v.dtype)
        return jnp.einsum('bgrqk,bkge->bqgre', p, v)

    o = lax.map(one_block, qb)
    return o.transpose(1, 0, 2, 3, 4, 5).reshape(b, tq, h * dv)

def attention_branches(h, p, lam_init, pos, ctx):
    b, t, _ = h.shape
    z = h @ p['w_in']
    splits = [int(s) for s in np.cumsum(IN_SIZES)[:-1]]
    (c_q, c_kv, k_pe, gq, gk, gv, dq, dk, dv, g_mla, g_gqa, g_diff) = jnp.split(z, splits, axis=-1)
    c_kv = rmsnorm(c_kv, p['mla_kv_norm'])
    k_pe = k_pe[:, :, None, :]
    q = (rmsnorm(c_q, p['mla_q_norm']) @ p['mla_w_uq']).reshape(b, t, MLA_HEADS, MLA_NOPE + MLA_ROPE)
    gq = rmsnorm(gq.reshape(b, t, GQA_HEADS, GQA_DIM), p['gqa_q_norm'])
    gk = rmsnorm(gk.reshape(b, t, GQA_KV_HEADS, GQA_DIM), p['gqa_k_norm'])
    gv = gv.reshape(b, t, GQA_KV_HEADS, GQA_DIM)
    dq = dq.reshape(b, t, DIFF_HEADS, 2 * DIFF_DIM)
    dk = dk.reshape(b, t, DIFF_HEADS, 2 * DIFF_DIM)
    dv = dv.reshape(b, t, DIFF_HEADS, DIFF_V)
    own = (c_kv, k_pe[:, :, 0, :], gk, gv, dk, dv)

    if pos is None:
        ckv_all, kpe_all, gk_all, gv_all, dk_all, dv_all = c_kv, k_pe, gk, gv, dk, dv
    else:
        row, col = pos

        def rot(u):
            return rope_2d(u, row, col)

        def rot_pair(u):
            return jnp.concatenate([rot(u[..., :DIFF_DIM]), rot(u[..., DIFF_DIM:])], axis=-1)

        def cat(a, u):
            return jnp.concatenate([a, u], axis=1)

        q = jnp.concatenate([q[..., :MLA_NOPE], rot(q[..., MLA_NOPE:])], axis=-1)
        gq = rot(gq)
        dq = rot_pair(dq)
        ctx_ckv, ctx_kpe, ctx_gk, ctx_gv, ctx_dk, ctx_dv = ctx
        ckv_all = cat(ctx_ckv, c_kv)
        kpe_all = cat(ctx_kpe[:, :, None, :], rot(k_pe))
        gk_all = cat(ctx_gk, rot(gk))
        gv_all = cat(ctx_gv, gv)
        dk_all = cat(ctx_dk, rot_pair(dk))
        dv_all = cat(ctx_dv, dv)

    k_nope = jnp.einsum('btr,rhd->bthd', ckv_all, p['mla_w_uk'])
    k_mla = jnp.concatenate([k_nope, jnp.broadcast_to(kpe_all, k_nope.shape[:-1] + (MLA_ROPE,))], axis=-1)
    v_mla = jnp.einsum('btr,rhd->bthd', ckv_all, p['mla_w_uv'])
    o_mla = attend(q, k_mla, v_mla)
    o_gqa = attend(gq, gk_all, gv_all)
    lam = (jnp.exp(jnp.sum(p['diff_lam_q1'].astype(jnp.float32) * p['diff_lam_k1'].astype(jnp.float32)))
           - jnp.exp(jnp.sum(p['diff_lam_q2'].astype(jnp.float32) * p['diff_lam_k2'].astype(jnp.float32)))
           + lam_init).astype(h.dtype)
    a1 = attend(dq[..., :DIFF_DIM], dk_all[..., :DIFF_DIM], dv_all)
    a2 = attend(dq[..., DIFF_DIM:], dk_all[..., DIFF_DIM:], dv_all)
    o_diff = rmsnorm((a1 - lam * a2).reshape(b, t, DIFF_HEADS, DIFF_V), p['diff_subln']) * (1.0 - lam_init)
    o_diff = o_diff.reshape(b, t, DIFF_HEADS * DIFF_V)
    merged = (jax.nn.sigmoid(g_mla) * (o_mla @ p['w_br_mla'])
              + jax.nn.sigmoid(g_gqa) * (o_gqa @ p['w_br_gqa'])
              + jax.nn.sigmoid(g_diff) * (o_diff @ p['w_br_diff']))
    return merged @ p['w_out'], own

def expert_choice_ffn(h, p):
    b, t, d = h.shape
    n = b * t
    cap = CAPACITY_FACTOR * n // N_EXPERTS
    xs = h.reshape(n, d)
    aff = jax.nn.softmax((xs @ p['w_router']).astype(jnp.float32), axis=-1)
    gate, idx = lax.top_k(aff.T, cap)
    xe = xs[idx]
    hg = jnp.einsum('ecd,edf->ecf', xe, p['w_gate'])
    hu = jnp.einsum('ecd,edf->ecf', xe, p['w_up'])
    ye = jnp.einsum('ecf,efd->ecd', jax.nn.silu(hg) * hu, p['w_down']) * gate[..., None].astype(h.dtype)
    out = jnp.zeros_like(xs).at[idx.reshape(-1)].add(ye.reshape(-1, d))
    return out.reshape(b, t, d)

def trunk_layer(x, cond, p, lam_init, pos, ctx):
    mod = (jax.nn.silu(cond) @ p['w_ada'] + p['b_ada']).reshape(-1, 1, 6 * D_MODEL)
    shift1, scale1, gate1, shift2, scale2, gate2 = jnp.split(mod, 6, axis=-1)
    h = rmsnorm(x, p['norm1']) * (1.0 + scale1) + shift1
    y, own = attention_branches(h, p, lam_init, pos, ctx)
    x = x + gate1 * y
    h = rmsnorm(x, p['norm2']) * (1.0 + scale2) + shift2
    x = x + gate2 * expert_choice_ffn(h, p)
    return x, own

def setup_inputs(seed: int = 0) -> dict:
    key = jax.random.key(seed)
    ks = iter(jax.random.split(key, 48))

    def nrm(shape, scale):
        return jax.random.normal(next(ks), shape, jnp.float32) * scale

    def gain(shape):
        return 1.0 + nrm(shape, 0.05)

    D = D_MODEL
    return {
        'x_prompt': nrm((BATCH, SEQ, D), 1.0),
        'x_sample': nrm((DEC_BATCH, DEC_SEQ, D), 1.0),
        'cache_mla_ckv': nrm((DEC_BATCH, DEPTH, PAST_LEN, MLA_KV_RANK), 1.0),
        'cache_mla_kpe': nrm((DEC_BATCH, DEPTH, PAST_LEN, MLA_ROPE), 1.0),
        'cache_gqa_k': nrm((DEC_BATCH, DEPTH, PAST_LEN, GQA_KV_HEADS, GQA_DIM), 1.0),
        'cache_gqa_v': nrm((DEC_BATCH, DEPTH, PAST_LEN, GQA_KV_HEADS, GQA_DIM), 1.0),
        'cache_diff_k': nrm((DEC_BATCH, DEPTH, PAST_LEN, DIFF_HEADS, 2 * DIFF_DIM), 1.0),
        'cache_diff_v': nrm((DEC_BATCH, DEPTH, PAST_LEN, DIFF_HEADS, DIFF_V), 1.0),
        'c': nrm((DEC_BATCH, D), 1.0),
        'c_ctx': nrm((D,), 1.0),
        'w_ada': nrm((DEPTH, D, 6 * D), 0.5 * D ** -0.5),
        'b_ada': nrm((DEPTH, 6 * D), 0.02),
        'norm1': gain((DEPTH, D)),
        'norm2': gain((DEPTH, D)),
        'w_in': nrm((DEPTH, D, IN_COLS), D ** -0.5),
        'mla_q_norm': gain((DEPTH, MLA_Q_RANK)),
        'mla_kv_norm': gain((DEPTH, MLA_KV_RANK)),
        'mla_w_uq': nrm((DEPTH, MLA_Q_RANK, MLA_HEADS * (MLA_NOPE + MLA_ROPE)), MLA_Q_RANK ** -0.5),
        'mla_w_uk': nrm((DEPTH, MLA_KV_RANK, MLA_HEADS, MLA_NOPE), MLA_KV_RANK ** -0.5),
        'mla_w_uv': nrm((DEPTH, MLA_KV_RANK, MLA_HEADS, MLA_V), MLA_KV_RANK ** -0.5),
        'gqa_q_norm': gain((DEPTH, GQA_DIM)),
        'gqa_k_norm': gain((DEPTH, GQA_DIM)),
        'diff_lam_q1': nrm((DEPTH, DIFF_DIM), 0.1),
        'diff_lam_k1': nrm((DEPTH, DIFF_DIM), 0.1),
        'diff_lam_q2': nrm((DEPTH, DIFF_DIM), 0.1),
        'diff_lam_k2': nrm((DEPTH, DIFF_DIM), 0.1),
        'diff_subln': gain((DEPTH, DIFF_V)),
        'w_br_mla': nrm((DEPTH, MLA_HEADS * MLA_V, D), (MLA_HEADS * MLA_V) ** -0.5),
        'w_br_gqa': nrm((DEPTH, GQA_HEADS * GQA_DIM, D), (GQA_HEADS * GQA_DIM) ** -0.5),
        'w_br_diff': nrm((DEPTH, DIFF_HEADS * DIFF_V, D), (DIFF_HEADS * DIFF_V) ** -0.5),
        'w_out': nrm((DEPTH, D, D), D ** -0.5),
        'w_router': nrm((DEPTH, D, N_EXPERTS), D ** -0.5),
        'w_gate': nrm((DEPTH, N_EXPERTS, D, EXPERT_FF), D ** -0.5),
        'w_up': nrm((DEPTH, N_EXPERTS, D, EXPERT_FF), D ** -0.5),
        'w_down': nrm((DEPTH, N_EXPERTS, EXPERT_FF, D), EXPERT_FF ** -0.5),
        'final_norm': gain((D,)),
    }

def reference(x_prompt, x_sample, cache_mla_ckv, cache_mla_kpe, cache_gqa_k, cache_gqa_v,
              cache_diff_k, cache_diff_v, c, c_ctx, w_ada, b_ada, norm1, norm2, w_in,
              mla_q_norm, mla_kv_norm, mla_w_uq, mla_w_uk, mla_w_uv, gqa_q_norm, gqa_k_norm,
              diff_lam_q1, diff_lam_k1, diff_lam_q2, diff_lam_k2, diff_subln,
              w_br_mla, w_br_gqa, w_br_diff, w_out, w_router, w_gate, w_up, w_down, final_norm):
    rows = x_sample.shape[1] // GRID_W
    row_pos = jnp.repeat(jnp.arange(rows, dtype=jnp.float32), GRID_W)
    col_pos = jnp.tile(jnp.arange(GRID_W, dtype=jnp.float32), rows)
    xp, xs = x_prompt, x_sample
    l_ckv, l_kpe, l_gk, l_gv, l_dk, l_dv = [], [], [], [], [], []
    for l in range(DEPTH):
        p = {
            'w_ada': w_ada[l], 'b_ada': b_ada[l], 'norm1': norm1[l], 'norm2': norm2[l],
            'w_in': w_in[l], 'mla_q_norm': mla_q_norm[l], 'mla_kv_norm': mla_kv_norm[l],
            'mla_w_uq': mla_w_uq[l], 'mla_w_uk': mla_w_uk[l], 'mla_w_uv': mla_w_uv[l],
            'gqa_q_norm': gqa_q_norm[l], 'gqa_k_norm': gqa_k_norm[l],
            'diff_lam_q1': diff_lam_q1[l], 'diff_lam_k1': diff_lam_k1[l],
            'diff_lam_q2': diff_lam_q2[l], 'diff_lam_k2': diff_lam_k2[l], 'diff_subln': diff_subln[l],
            'w_br_mla': w_br_mla[l], 'w_br_gqa': w_br_gqa[l], 'w_br_diff': w_br_diff[l],
            'w_out': w_out[l], 'w_router': w_router[l],
            'w_gate': w_gate[l], 'w_up': w_up[l], 'w_down': w_down[l],
        }
        lam_init = 0.8 - 0.6 * math.exp(-0.3 * l)
        xp, own = trunk_layer(xp, c_ctx, p, lam_init, None, None)
        l_ckv.append(own[0]); l_kpe.append(own[1]); l_gk.append(own[2])
        l_gv.append(own[3]); l_dk.append(own[4]); l_dv.append(own[5])
        ctx = (cache_mla_ckv[:, l], cache_mla_kpe[:, l], cache_gqa_k[:, l],
               cache_gqa_v[:, l], cache_diff_k[:, l], cache_diff_v[:, l])
        xs, _ = trunk_layer(xs, c, p, lam_init, (row_pos, col_pos), ctx)
    y_prompt = rmsnorm(xp, final_norm)
    y_sample = rmsnorm(xs, final_norm)
    new_mla_ckv = jnp.stack(l_ckv, axis=1)
    new_mla_kpe = jnp.stack(l_kpe, axis=1)
    new_gqa_k = jnp.stack(l_gk, axis=1)
    new_gqa_v = jnp.stack(l_gv, axis=1)
    new_diff_k = jnp.stack(l_dk, axis=1)
    new_diff_v = jnp.stack(l_dv, axis=1)
    return (y_prompt, y_sample, new_mla_ckv, new_mla_kpe, new_gqa_k, new_gqa_v, new_diff_k, new_diff_v)


_drawn_inputs = setup_inputs


def setup_inputs(seed=0):
    import zlib

    import numpy as np

    out = dict(_drawn_inputs(seed))
    spreads = {}
    factors = {'cache_mla_ckv': 4.597,
     'cache_mla_kpe': 7.274,
     'cache_gqa_k': 5.598,
     'cache_gqa_v': 4.268,
     'norm2': 3.711,
     'mla_q_norm': 8.0,
     'gqa_q_norm': 8.0,
     'diff_lam_q1': 5.573,
     'diff_lam_k1': 5.943,
     'diff_lam_q2': 7.806,
     'diff_lam_k2': 8.0,
     'diff_subln': 6.395}
    for name, (base, spread) in spreads.items():
        noise = np.random.default_rng([zlib.crc32(name.encode()), seed]).standard_normal(out[name].shape)
        drawn = base * np.exp(spread * noise) if base else spread * noise
        out[name] = __import__('jax').numpy.asarray(drawn.astype(out[name].dtype))
    for name, factor in factors.items():
        out[name] = (out[name] * factor).astype(out[name].dtype)
    return out
```

```python
from contextlib import ExitStack
import math

import numpy as np
import concourse.bass as bass
from concourse import mybir

F32 = mybir.dt.float32
ALU = mybir.AluOpType
ACT = mybir.ActivationFunctionType
AX = mybir.AxisListType.X

P = 128
D = 1024
KC = D // P
DEPTH = 2
NT = 3
TOK = NT * P
NKEY = 4 * P
EPS = 1e-6
QR, KVR, ROPE, NOPE = 384, 256, 32, 64
QD = NOPE + ROPE
NE, FF = 16, 1024
CAP_S, CAP_P = 32, 16
CAP = CAP_S + CAP_P
XW = 64
ATT = 2976
SLOTS = 8
SLOT = 2048
UNITS = 256
ATT_UNITS = 64
GE = 4
NG = NE // GE
GROUP_UNITS = 12 * GE
USES = UNITS // SLOTS
BF = 512

ZA_W, ZG_W, ZD_W = 672, 768, 1536
Z_KV, Z_PE = QR, QR + KVR
G_K, G_V = 512, 640
D_K, D_V = 512, 1024

C_ID = 0
C_SEL = C_ID + P
C_ONE = C_SEL + 4 * P
C_COS = C_ONE + P
C_IOTA = C_COS + 2 * 192
C_LAM = C_IOTA + CAP_S
C_W = C_LAM + 2 * DEPTH


def lam_init(layer):
    return 0.8 - 0.6 * math.exp(-0.3 * layer)


def constants():
    c = np.zeros((P, C_W), np.float32)
    c[:, C_ID:C_ID + P] = np.eye(P)
    for which in range(2):
        for s in range(2):
            at = C_SEL + (2 * which + s) * P
            c[32 * (1 + 2 * which) + s, at:at + P] = 1.0
    c[:, C_ONE:C_ONE + P] = 1.0
    token = np.arange(2 * P)
    axes = ((token // 64).astype(np.float32), (token % 64).astype(np.float32))
    at = C_COS
    tables = []
    for width in (64, 32):
        half = width // 4
        freqs = (np.float32(10000.0) ** (-np.arange(half, dtype=np.float32) / np.float32(half))).astype(np.float32)
        cos, sin = [], []
        for pos in axes:
            ang = (pos[:, None] * freqs[None, :]).astype(np.float32)
            co, si = np.cos(ang), np.sin(ang)
            cos += [co, co]
            sin += [-si, si]
        tables += [np.concatenate(cos, 1), np.concatenate(sin, 1)]
    table = np.concatenate(tables, 1).astype(np.float32)
    for t in range(2):
        c[:, at + 192 * t:at + 192 * (t + 1)] = table[t * P:(t + 1) * P]
    c[:, C_IOTA:C_IOTA + CAP_S] = np.arange(1, CAP_S + 1)
    for layer in range(DEPTH):
        c[:, C_LAM + 2 * layer] = lam_init(layer)
        c[:, C_LAM + 2 * layer + 1] = 1.0 - lam_init(layer)
    return c


class Signal:

    def __init__(self, handle, per, base):
        self.s, self.per, self.base = handle, per, base

    def at(self, layer, n):
        return layer * self.per + (n + self.base)

    def in_group(self, layer, g, n):
        return layer * self.per + g * (self.per // NG) + (n + self.base)


JOBS = [("mla", h) for h in range(8)] + [("gqa", i) for i in range(4)] + [("diff", h) for h in range(4)]
NJ = len(JOBS)
MAPS = []
OUTS = []
for _j, (_kind, _) in enumerate(JOBS):
    MAPS += [(_j, m) for m in range(1 if _kind == "mla" else 2)]
    OUTS += [(_j, m) for m in range(2 if _kind == "gqa" else 1)]
MAP_AT = {jm: n for n, jm in enumerate(MAPS)}
OUT_AT = {jm: n for n, jm in enumerate(OUTS)}
SCALE = {"mla": QD ** -0.5, "gqa": 64 ** -0.5, "diff": 64 ** -0.5}

FILL = [[] for _ in range(NJ + 1)]
for _t in range(NT):
    FILL[_t] += [("c1", _t, h) for h in range(2)]
for _c in range(KC):
    FILL[3 + _c // 2].append(("gate0", _c))
for _n in range(12):
    FILL[8 + _n // 4].append(("c2", _n))
for _c in range(KC):
    FILL[11 + _c // 4].append(("br0", _c))
for _c in range(KC):
    FILL[13 + _c // 3] += [("gate1", _c), ("br1", _c)]

USERS = [("c0", t, h) for t in range(NT) for h in range(2)]
USERS += [("q", t, h) for t in range(NT) for h in range(2)] + [("v", t) for t in range(4)]
for _i in range(NJ + 1):
    if _i >= 1:
        USERS.append(("pv", _i - 1))
    USERS += FILL[_i]
USERS += [("gate2", c) for c in range(KC)] + [("br2", c) for c in range(KC)]
USERS += [("out", t, h) for t in range(NT) for h in range(2)]
USER_AT = {u: n for n, u in enumerate(USERS)}
BY_DVE = {"v", "br0", "br1", "br2", "out"}


def evacuated(n):
    dve = USERS[n][0] in BY_DVE
    return sum((u[0] in BY_DVE) == dve for u in USERS[:n + 1])


N_DVE_USERS = sum(u[0] in BY_DVE for u in USERS)
N_ACT_USERS = len(USERS) - N_DVE_USERS

PLAN = [("ada", i, k) for i in range(3) for k in range(KC)]
PLAN += [("c0", u) for u in range(4)] + [("uq", 0), ("uq", 1)]
PLAN += [("c1", u) for u in range(4)] + [("gate0", u) for u in range(4)]
PLAN += [("c2", u) for u in range(8)] + [("br0", 0), ("br0", 1)]
PLAN += [("gate1", 0), ("br1", 0), ("gate1", 1), ("gate1", 2), ("br1", 1), ("gate1", 3)]
PLAN += [("gate2", u) for u in range(4)] + [("br2", 0), ("br2", 1)] + [("wout", u) for u in range(4)]
assert len(PLAN) == ATT_UNITS
UNIT = {u: n for n, u in enumerate(PLAN)}

DVE_LINKS = 100
POOL_LINKS = 24


def backbone(nc, a):
    ctx = ExitStack()
    with ctx:
        arena = ctx.enter_context(nc.sbuf_tensor("arena", [P, 36800], F32))
        ring = ctx.enter_context(nc.sbuf_tensor("ring", [P, SLOTS, SLOT], F32))
        PS = ctx.enter_context(nc.psum_tensor("banks", [P, 8, BF], F32))

        def at(start, *shape):
            n = int(np.prod(shape))
            v = arena[:, start:start + n]
            names = "abcd"[:len(shape)]
            if len(shape) == 1:
                return v
            return v.rearrange(f"p ({' '.join(names)}) -> p {' '.join(names)}",
                               **{x: s for x, s in zip(names, shape)})

        hT = at(0, KC, TOK)
        XN = at(3072, NT, D)
        MG = at(3072, KC, TOK)
        ZA = at(6144, NT, ZA_W)
        ZG = at(8160, NT, ZG_W)
        QQ = at(10464, NT, 768)
        QAB = at(10464, 2, 2, TOK)
        VM = at(12768, 4, 512)
        CKT = at(14816, 2, NKEY)
        UKV = at(15840, 2, 2, 512)
        ZD = at(12768, NT, ZD_W)
        QM = at(17888, 2, TOK)
        SG1 = at(17888, 2, TOK)
        KT = at(18656, 2, NKEY)
        PB = at(19680, 2, 896)
        CQT = at(19680, 3, TOK)
        PT = at(21472, 2, 896)
        OT0 = at(23264, 4, TOK)
        OT1 = at(6144, 4, TOK)
        OT2 = at(8160, 4, TOK)
        SQD = at(19680, 4, TOK)
        RSD = at(21472, 4, TOK)
        RT1 = at(24800, 640)
        RT2 = at(25440, 640)
        TMP = at(24800, 2, BF)
        SQG = at(3072, NT, 640)
        G1 = at(12768, 2, D)
        SG2 = at(14816, KC, TOK)
        CTX_CKV = at(26080, KVR)
        CTX_KPE = at(26336, ROPE)
        CTX_GK = at(26368, 128)
        CTX_GV = at(26496, 128)
        CTX_DK = at(26624, 512)
        CTX_DV = at(27136, 512)
        YS = at(0, 2, D)
        CTMP = at(2048, 2, BF)
        SGE = at(3072, BF)
        AC = at(3584, BF)
        AT = at(4096, 4, P)
        DD = at(6144, NT, NE, CAP_S)
        DG = at(7680, NT, NE, CAP_S)
        DGT = at(9216, NG, NT * P)
        XB = at(10752, 2, KC, XW)
        DGB = at(11776, NT * P)
        G2 = at(12160, 2, D)
        AFT = at(14208, TOK)[0:NE]
        WK = at(14592, TOK)[0:NE]
        MK = at(14976, TOK)[0:NE]
        SN = at(15360, TOK)[0:NE]
        XE = at(17888, KC, NE, CAP)
        AFF = at(24032, NT, NE)
        POS = at(24080, NT, NE)
        LG = at(24128, NT, NE)
        M8 = at(24176, 8)[0:NE]
        X = at(27648, NT, D)
        MODR = at(30720, 1536)
        BR = at(32256, 1536)
        MODC = at(33792, 2, 4, 12)
        AA = at(33888, 2, 2, KC)
        CST = at(33920, C_W)
        o = 33920 + C_W
        GNQ = at(o, QR)
        GNK = at(o + 384, KVR)
        GGQ = at(o + 640, 64)
        GGK = at(o + 704, 64)
        LAMV = at(o + 768, 4, 64)
        NR = at(o + 1024, P)[0:16]
        NCOL = at(o + 1152, 2, KC)
        SUB = at(o + 1168, 1)
        WR = at(o + 1172, KC, NE)
        SC = at(o + 1300, KC, 2)
        CR = NR
        SIGC = at(o + 1316, 16)
        ST = at(o + 1332, 3)
        RS = at(o + 1336, 3)
        ST2 = at(o + 1340, 6)
        R2 = at(o + 1346, 6)
        STG = at(o + 1352, 30)
        RG = at(o + 1382, 30)
        MX = at(o + 1412, 2, 3)
        NB = at(o + 1418, 2, 3)
        SM = at(o + 1424, 2, 3)
        RC = at(o + 1430, 2, 3)
        LP = at(o + 1436, 2, 64)
        LE = at(o + 1564, 2)
        LAM = at(o + 1566, 1)
        LIC = at(o + 1567, 2)
        KPR = at(o + 1569, 2, ROPE)
        assert o + 1633 <= 36800
        IDT = CST[:, C_ID:C_ID + P]
        ONES = CST[:, C_ONE:C_ONE + P]
        IOTA = CST[:, C_IOTA:C_IOTA + CAP_S]
        GSTAT = ST2

        def sem(name, per=0, base=0):
            return Signal(ctx.enter_context(nc.semaphore(name)), per, base)

        filled = [sem(f"filled{i}", 16 * USES) for i in range(SLOTS)]
        used = [sem(f"used{i}", USES, 1) for i in range(SLOTS)]
        const_in, cond_in, x_in = sem("const_in"), sem("cond_in"), sem("x_in")
        cond_t, cond_sig, cond_ok = sem("cond_t"), sem("cond_sig"), sem("cond_ok")
        early_in = sem("early_in", 6 * 16)
        late_in = sem("late_in", 18 * 16)
        ada_mm = sem("ada_mm", 3)
        mod_row, mod_col = sem("mod_row", 3), sem("mod_col", 3)
        mod_t = sem("mod_t", 4)
        ncol_ok, aa_ok = sem("ncol_ok", 1), sem("aa_ok", 1)
        ss_ok, root_ok, ms_ok, xn_ok = sem("ss_ok", 2), sem("root_ok", 2), sem("ms_ok", 2), sem("xn_ok", 6)
        ht_mm, ht_act, ht_dve = sem("ht_mm", 16), sem("ht_act", 8), sem("ht_dve", 8)
        user_mm = sem("user_mm", len(USERS))
        user_act, user_dve = sem("user_act", N_ACT_USERS), sem("user_dve", N_DVE_USERS)
        sq2_ok, ms2_ok, root2_ok, za_ok = sem("sq2_ok", 1), sem("ms2_ok", 1), sem("root2_ok", 1), sem("za_ok", 1)
        kpe_ok, qrope_ok = sem("kpe_ok", 1), sem("qrope_ok", 1)
        tr_mm, tr_act, tr_dve = sem("tr_mm", 3), sem("tr_act", 1), sem("tr_dve", 2)
        prep_mm, prep_act, prep_dve = sem("prep_mm", NJ), sem("prep_act", NJ), sem("prep_dve", NJ)
        score_mm, max_ok, exp_ok = sem("score_mm", len(MAPS)), sem("max_ok", len(MAPS)), sem("exp_ok", len(MAPS))
        prob_ok = sem("prob_ok", len(OUTS))
        pt_mm, pt_act, pt_dve = sem("pt_mm", len(OUTS)), sem("pt_act", len(OUTS)), sem("pt_dve", len(OUTS))
        sqg_ok, msg_ok, rootg_ok, rg_ok, gq_ok = (sem("sqg_ok", 1), sem("msg_ok", 1), sem("rootg_ok", 1),
                                                  sem("rg_ok", 1), sem("gq_ok", 1))
        zero_ok, dq_ok = sem("zero_ok", 1), sem("dq_ok", 1)
        lamp_ok, lame_ok = sem("lamp_ok", 1), sem("lame_ok", 1)
        stored_a, stored_g, stored_d = sem("stored_a", 32), sem("stored_g", 32), sem("stored_d", 32)
        sqd_ok, sqd_mm, msd_ok, rootd_ok, ot2_ok = (sem("sqd_ok", 1), sem("sqd_mm", 1), sem("msd_ok", 1),
                                                    sem("rootd_ok", 1), sem("ot2_ok", 1))
        gb_mm, gb_ok = sem("gb_mm", 2), sem("gb_ok", 2)
        x1_ok, xg_ok, silu_ok = sem("x1_ok", 1), sem("xg_ok", NG, 1), sem("silu_ok", NE)
        router_mm, logit_ok, aexp_ok, aff_ok = (sem("router_mm", 1, 1), sem("logit_ok", 1), sem("aexp_ok", 1),
                                                sem("aff_ok", 1))
        aff_t, pos_ok, pos_t, disp_ok = sem("aff_t", 1), sem("pos_ok", 1), sem("pos_t", 1), sem("disp_ok", 1)
        gather_mm, gather_act, gather_dve = sem("gather_mm", 16), sem("gather_act", 8), sem("gather_dve", 8)
        dgt_mm, dgt_ok = sem("dgt_mm", 1), sem("dgt_ok", 1)
        xb_ok = sem("xb_ok", NE)
        gu_mm = sem("gu_mm", 2 * NE)
        sig_ok, ac_ok, at_mm, at_ok = sem("sig_ok", NE), sem("ac_ok", NE, 1), sem("at_mm", NE, 1), sem("at_ok", NE)
        y_mm, y_ok = sem("y_mm", NE), sem("y_ok", NE, 1)
        comb_mm, comb_ok, dgb_ok = sem("comb_mm", 6 * NG, 1), sem("comb_ok", 6 * NG, 1), sem("dgb_ok", NG)
        dve_chain, pool_chain, act_chain = sem("dve_chain", DVE_LINKS), sem("pool_chain", POOL_LINKS), sem("act_chain", 0)
        fn_in, y_out = sem("fn_in"), sem("y_out")
        fin_ss, fin_ms, fin_root, fin_ok = sem("fin_ss"), sem("fin_ms"), sem("fin_root"), sem("fin_ok")

        passed = sem("passed")

        def apart(eng):
            eng.sem_inc(passed.s, 1)

        block = ctx.enter_context(nc.Block())

        @block.sync
        def _(sp):
            sp.dma_start(CST, a["constants"]).then_inc(const_in.s, 16)
            sp.dma_start(CR[0:8], a["c_ctx"].rearrange("(k p) -> k p", p=P)).then_inc(cond_in.s, 16)
            sp.dma_start(CR[8:16], a["c"].rearrange("b (k p) -> (b k) p", p=P)).then_inc(cond_in.s, 16)
            sp.dma_start(X[:, 0], a["x_prompt"].rearrange("b p d -> (b p) d")).then_inc(x_in.s, 16)
            sp.dma_start(X[:, 1:3], a["x_sample"].rearrange("b (t p) d -> p (b t) d", p=P)).then_inc(x_in.s, 16)
            w_ada = a["w_ada"].rearrange("l (k p) (j i n) -> l k i p j n", p=P, j=4, i=3)
            w_in = a["w_in"].rearrange("l (k p) n -> l p k n", p=P)
            w_uq = a["mla_w_uq"].rearrange("l (k p) n -> l p k n", p=P)
            w_br = [a[f"w_br_{n}"].rearrange("l (k p) n -> l p k n", p=P) for n in ("mla", "gqa", "diff")]
            w_out = a["w_out"].rearrange("l (k p) n -> l p k n", p=P)
            w_exp = [a[n].rearrange("l e (k p) n -> l e p k n", p=P) for n in ("w_gate", "w_up", "w_down")]

            def source(l, unit):
                kind, u = unit[0], unit[1]
                if kind == "ada":
                    return w_ada[l, unit[2], u]
                if kind == "c0":
                    return w_in[l, :, 2 * u:2 * u + 2, 0:ZA_W]
                if kind == "c1":
                    return w_in[l, :, 2 * u:2 * u + 2, ZA_W:ZA_W + ZG_W]
                if kind == "c2":
                    c = ZA_W + ZG_W + 768 * (u // 4)
                    return w_in[l, :, 2 * (u % 4):2 * (u % 4) + 2, c:c + 768]
                if kind == "uq":
                    return w_uq[l, :, 2 * u:min(2 * u + 2, 3), :]
                if kind.startswith("gate"):
                    c = ATT + D * int(kind[4]) + 256 * u
                    return w_in[l, :, :, c:c + 256]
                if kind.startswith("br"):
                    return w_br[int(kind[2])][l, :, :, 512 * u:512 * u + 512]
                return w_out[l, :, 2 * u:2 * u + 2, :]

            with sp.Fori(0, DEPTH) as l:
                for n, unit in enumerate(PLAN):
                    src = source(l, unit)
                    _, parts, cols = src.shape
                    dst = ring[:, n % SLOTS, 0:parts * cols].rearrange("p (k n) -> p k n", k=parts)
                    sp.wait_ge(used[n % SLOTS].s, used[n % SLOTS].at(l, n // SLOTS))
                    sp.dma_start(dst, src).then_inc(filled[n % SLOTS].s, 16)
                with sp.Fori(0, NG) as g:
                    for e in range(GE):
                        for m in range(3):
                            for u in range(4):
                                n = 12 * e + 4 * m + u
                                src = w_exp[m][l, bass.ds(g * GE + e, 1), :, 2 * u:2 * u + 2, :]
                                sp.wait_ge(used[n % SLOTS].s,
                                           l * USES + g * (GROUP_UNITS // SLOTS) + ((ATT_UNITS + n) // SLOTS + 1))
                                sp.dma_start(ring[:, n % SLOTS, :].rearrange("p (k n) -> p k n", k=2),
                                             src.rearrange("e p k n -> (e p) k n")).then_inc(filled[n % SLOTS].s, 16)
            sp.wait_ge(xg_ok.s, DEPTH * NG + 1)
            sp.dma_start(at(0, D), a["final_norm"].rearrange("(o n) -> o n", o=1).to_broadcast([P, D]))\
              .then_inc(fn_in.s, 16)
            sp.wait_ge(fin_ok.s, NT)
            sp.dma_start(a["y_prompt"].rearrange("b p d -> (b p) d"), XN[:, 0]).then_inc(y_out.s, 16)
            sp.dma_start(a["y_sample"].rearrange("b (t p) d -> p (b t) d", p=P), XN[:, 1:3]).then_inc(y_out.s, 16)
            sp.wait_ge(y_out.s, 32)
            sp.wait_ge(stored_a.s, 32 * DEPTH)
            sp.wait_ge(stored_g.s, 32 * DEPTH)
            sp.wait_ge(stored_d.s, 32 * DEPTH)

        @block.gpsimd
        def _(pool):
            links = [0]

            def link(ins, l):
                links[0] += 1
                ins.then_inc(pool_chain.s, 1)
                pool.wait_ge(pool_chain.s, pool_chain.at(l, links[0]))

            def rotate(l, z, heads, width, t):
                c0 = C_COS + 192 * t + (0 if width == 64 else 128)
                half = width // 4
                cos = CST[:, c0:c0 + width].rearrange("p (o n) -> p o n", o=1).to_broadcast([P, heads, width])
                sin = CST[:, c0 + width:c0 + 2 * width].rearrange("p (x h n) -> p x h n", x=2, h=2)
                t1 = RT1[:, 0:heads * width].rearrange("p (a n) -> p a n", a=heads)
                t2 = RT2[:, 0:heads * width].rearrange("p (a n) -> p a n", a=heads)
                t2v = RT2[:, 0:heads * width].rearrange("p (a x h n) -> p a x h n", a=heads, x=2, h=2)
                pool.tensor_tensor(t1, z, cos, ALU.mult)
                for h in range(2):
                    for x in range(2):
                        src = z[:, :, (2 * x + 1 - h) * half:(2 * x + 2 - h) * half]
                        sx = sin[:, x, h, :].rearrange("p (o n) -> p o n", o=1).to_broadcast([P, heads, half])
                        ins = pool.tensor_tensor(t2v[:, :, x, h, :], src, sx, ALU.mult)
                link(ins, l)
                return pool.tensor_tensor(z, t1, t2, ALU.add)

            def row(ap, n):
                return ap.rearrange("(o n) -> o n", o=1).to_broadcast([P, n])

            pool.wait_ge(const_in.s, 16)
            pool.wait_ge(cond_t.s, 1)
            with pool.Fori(0, DEPTH) as l:
                links[0] = 0
                pool.wait_ge(router_mm.s, router_mm.at(l, 0))
                b_ada = a["b_ada"].rearrange("l (j n) -> l j n", j=4)
                for j in range(4):
                    pool.dma_start(BR[32 * j:32 * j + 2], b_ada[l, j].rearrange("(o n) -> o n", o=1)
                                   .to_broadcast([2, 1536])).then_inc(early_in.s, 16)
                pool.dma_start(NR[0:8], a["norm1"].rearrange("l (k p) -> l k p", p=P)[l]).then_inc(early_in.s, 16)
                pool.dma_start(NR[8:16], a["norm2"].rearrange("l (k p) -> l k p", p=P)[l]).then_inc(early_in.s, 16)
                for dst, name, n in ((GNQ, "mla_q_norm", QR), (GNK, "mla_kv_norm", KVR), (GGQ, "gqa_q_norm", 64),
                                     (GGK, "gqa_k_norm", 64), (LAMV[:, 0], "diff_lam_q1", 64),
                                     (LAMV[:, 1], "diff_lam_q2", 64), (LAMV[:, 2], "diff_lam_k1", 64),
                                     (LAMV[:, 3], "diff_lam_k2", 64)):
                    pool.dma_start(dst, row(a[name][l], n)).then_inc(late_in.s, 16)
                pool.dma_start(SUB, a["diff_subln"][l].rearrange("(p o) -> p o", o=1)).then_inc(late_in.s, 16)
                pool.dma_start(WR, a["w_router"].rearrange("l (k p) e -> l p k e", p=P)[l]).then_inc(late_in.s, 16)
                for m, name in enumerate(("mla_w_uk", "mla_w_uv")):
                    pool.dma_start(UKV[:, m], a[name].rearrange("l (k p) h d -> l p k (h d)", p=P)[l])\
                        .then_inc(late_in.s, 16)
                for dst, name, form in ((CTX_CKV, "cache_mla_ckv", "b l p r -> l (b p) r"),
                                        (CTX_KPE, "cache_mla_kpe", "b l p r -> l (b p) r"),
                                        (CTX_GK, "cache_gqa_k", "b l p h d -> l (b p) (h d)"),
                                        (CTX_GV, "cache_gqa_v", "b l p h d -> l (b p) (h d)"),
                                        (CTX_DK, "cache_diff_k", "b l p h d -> l (b p) (h d)"),
                                        (CTX_DV, "cache_diff_v", "b l p h d -> l (b p) (h d)")):
                    pool.dma_start(dst, a[name].rearrange(form)[l]).then_inc(late_in.s, 16)
                pool.wait_ge(user_act.s, user_act.at(l, evacuated(USER_AT["c0", 2, 1])))
                for t in range(2):
                    apart(pool)
                    link(pool.tensor_copy(KPR[:, t:t + 1], ZA[:, 1 + t:2 + t, Z_PE:Z_PE + ROPE]), l)
                    ins = rotate(l, KPR[:, t:t + 1], 1, ROPE, t)
                    if t == 0:
                        link(ins, l)
                    else:
                        ins.then_inc(kpe_ok.s, 1)
                pool.wait_ge(za_ok.s, za_ok.at(l, 1))
                apart(pool)
                pool.dma_start(a["new_ckv"].rearrange("b l p r -> l (b p) r")[l],
                               ZA[:, 0, Z_KV:Z_KV + KVR]).then_inc(stored_a.s, 16)
                pool.dma_start(a["new_kpe"].rearrange("b l p r -> l (b p) r")[l],
                               ZA[:, 0, Z_PE:Z_PE + ROPE]).then_inc(stored_a.s, 16)
                pool.wait_ge(user_act.s, user_act.at(l, evacuated(USER_AT["q", 2, 1])))
                pool.wait_ge(kpe_ok.s, kpe_ok.at(l, 1))
                for t in range(2):
                    z = QQ[:, 1 + t].rearrange("p (h d) -> p h d", h=8)[:, :, NOPE:QD]
                    ins = rotate(l, z, 8, ROPE, t)
                    if t == 0:
                        link(ins, l)
                    else:
                        ins.then_inc(qrope_ok.s, 1)
                pool.wait_ge(rg_ok.s, rg_ok.at(l, 1))
                pool.wait_ge(qrope_ok.s, qrope_ok.at(l, 1))
                for t in range(NT):
                    z = ZG[:, t, 0:640].rearrange("p (h d) -> p h d", h=10)
                    rg = RG[:, 10 * t:10 * t + 10].rearrange("p (h o) -> p h o", o=1).to_broadcast([P, 10, 64])
                    link(pool.tensor_tensor(z, z, rg, ALU.mult), l)
                    pool.tensor_tensor(z[:, 0:8], z[:, 0:8],
                                       GGQ.rearrange("p (o n) -> p o n", o=1).to_broadcast([P, 8, 64]), ALU.mult)
                    link(pool.tensor_tensor(z[:, 8:10], z[:, 8:10],
                                            GGK.rearrange("p (o n) -> p o n", o=1).to_broadcast([P, 2, 64]),
                                            ALU.mult), l)
                    if t >= 1:
                        ins = rotate(l, z, 10, 64, t - 1)
                        if t == 1:
                            link(ins, l)
                        else:
                            ins.then_inc(gq_ok.s, 1)
                pool.wait_ge(gq_ok.s, gq_ok.at(l, 1))
                apart(pool)
                pool.dma_start(a["new_gk"].rearrange("b l p h d -> l (b p) (h d)")[l],
                               ZG[:, 0, G_K:G_K + 128]).then_inc(stored_g.s, 16)
                pool.dma_start(a["new_gv"].rearrange("b l p h d -> l (b p) (h d)")[l],
                               ZG[:, 0, G_V:G_V + 128]).then_inc(stored_g.s, 16)
                pool.wait_ge(prep_mm.s, prep_mm.at(l, 8))
                apart(pool)
                pool.memset(QAB[64:128, :, 0], 0.0)
                pool.memset(QAB[0:64, :, 1], 0.0).then_inc(zero_ok.s, 1)
                pool.wait_ge(user_act.s, user_act.at(l, evacuated(USER_AT["c2", 11])))
                for t in range(2):
                    for part in range(2):
                        z = ZD[:, 1 + t, 512 * part:512 * part + 512].rearrange("p (h d) -> p h d", h=8)
                        ins = rotate(l, z, 8, 64, t)
                        if (t, part) != (1, 1):
                            link(ins, l)
                        else:
                            ins.then_inc(dq_ok.s, 1)
                pool.dma_start(a["new_dk"].rearrange("b l p h d -> l (b p) (h d)")[l],
                               ZD[:, 0, D_K:D_K + 512]).then_inc(stored_d.s, 16)
                pool.dma_start(a["new_dv"].rearrange("b l p h d -> l (b p) (h d)")[l],
                               ZD[:, 0, D_V:D_V + 512]).then_inc(stored_d.s, 16)
                assert links[0] == POOL_LINKS, ("POOL_LINKS", links[0])

        @block.scalar
        def _(act):
            def norm_root(l, n):
                for t in range(NT):
                    ins = nc.scalar.activation(XN[:, t], X[:, t], ACT.Square, accum_out=ST[:, t:t + 1])
                ins.then_inc(ss_ok.s, 1)
                act.wait_ge(ms_ok.s, ms_ok.at(l, n + 1))
                nc.scalar.activation(RS, RS, ACT.Sqrt).then_inc(root_ok.s, 1)

            def ht_even(l, n):
                for c in range(0, KC, 2):
                    act.wait_ge(ht_mm.s, ht_mm.at(l, 8 * n + c + 1))
                    ps = PS[:, 4 + c % 4]
                    for s, lo, hi in ((0, 0, P), (1, P, TOK)):
                        v = 24 * n + c
                        ins = nc.scalar.activation(hT[:, c, lo:hi], ps[:, lo:hi], ACT.Identity,
                                                   scale=AA[:, n, s, c:c + 1],
                                                   bias=MODC[:, s, v // 12, v % 12:v % 12 + 1])
                    ins.then_inc(ht_act.s, 1)

            def user(l, key, write):
                n = USER_AT[key]
                act.wait_ge(user_mm.s, user_mm.at(l, n + 1))
                write(PS[:, 6 + n % 2]).then_inc(user_act.s, 1)

            def exps(l, j):
                kind, _ = JOBS[j]
                for m in range(1 if kind == "mla" else 2):
                    n = MAP_AT[j, m]
                    act.wait_ge(max_ok.s, max_ok.at(l, n + 1))
                    if n >= 2:
                        before = MAPS[n - 2]
                        act.wait_ge(pt_mm.s, pt_mm.at(l, OUT_AT.get(before, OUT_AT[before[0], 0]) + 1))
                    b = n % 2
                    for r, (lo, hi, bank, c) in enumerate(((0, 384, 0, 0), (384, 512, 0, 384), (512, 896, 1, 0))):
                        ins = nc.scalar.activation(PB[:, b, lo:hi], PS[:, 2 * m + bank, c:c + hi - lo], ACT.Exp,
                                                   scale=SCALE[kind], bias=NB[:, b, r:r + 1],
                                                   accum_out=SM[:, b, r:r + 1])
                    ins.then_inc(exp_ok.s, 1)

            def prep(l, j):
                kind, i = JOBS[j]
                act.wait_ge(prep_mm.s, prep_mm.at(l, j + 1))
                if kind == "mla":
                    ins = nc.scalar.copy(QM[0:QD, j % 2], PS[0:QD, 5, 0:TOK])
                else:
                    ins = nc.scalar.copy(QAB[0:64, j % 2, 0], PS[0:64, 5, 0:TOK])
                ins.then_inc(prep_act.s, 1)

            def values(l, j):
                kind, i = JOBS[j]
                n = USER_AT["pv", j]
                ps = PS[:, 6 + n % 2]
                act.wait_ge(user_mm.s, user_mm.at(l, n + 1))
                if kind == "mla":
                    r = 64 * (i % 2)
                    ins = nc.scalar.copy(OT0[r:r + 64, i // 2], ps[r:r + 64, 0:TOK])
                elif kind == "gqa":
                    if i == 0:
                        act.wait_ge(stored_a.s, stored_a.at(l, 32))
                    ins = nc.scalar.copy(OT1[:, i], ps[:, 0:TOK])
                else:
                    if i == 0:
                        act.wait_ge(stored_g.s, stored_g.at(l, 32))
                    ins = nc.scalar.copy(OT2[:, i], ps[:, 0:TOK])
                ins.then_inc(user_act.s, 1)

            def fill(l, key):
                kind = key[0]
                if kind == "c1":
                    user(l, key, lambda ps: nc.scalar.copy(ZG[:, key[1], 384 * key[2]:384 * key[2] + 384],
                                                           ps[:, 0:384]))
                elif kind == "c2":
                    half, t, q = key[1] // 6, key[1] % 6 // 2, key[1] % 2
                    c = 768 * half + 384 * q
                    user(l, key, lambda ps: nc.scalar.copy(ZD[:, t, c:c + 384], ps[:, 0:384]))
                elif kind == "gate0":
                    user(l, key, lambda ps: nc.scalar.activation(MG[:, key[1]], ps[:, 0:TOK], ACT.Tanh, scale=0.5))
                elif kind == "gate1":
                    if key[1] >= 2:
                        act.wait_ge(user_dve.s, user_dve.at(l, evacuated(USER_AT["br1", key[1] - 2])))
                    user(l, key, lambda ps: nc.scalar.activation(SG1[:, key[1] % 2], ps[:, 0:TOK], ACT.Tanh,
                                                                 scale=0.5))
                elif kind == "gate2":
                    user(l, key, lambda ps: nc.scalar.activation(SG2[:, key[1]], ps[:, 0:TOK], ACT.Tanh, scale=0.5))

            act.sem_inc(y_ok.s, 1)
            act.wait_ge(cond_t.s, 1)
            nc.scalar.activation(SIGC, PS[:, 0, 0:16], ACT.Sigmoid).then_inc(cond_sig.s, 1)
            act.wait_ge(x_in.s, 32)
            with act.Fori(0, DEPTH) as l:
                act.wait_ge(xg_ok.s, xg_ok.at(l, 0))
                norm_root(l, 0)
                act.wait_ge(aa_ok.s, aa_ok.at(l, 1))
                ht_even(l, 0)
                for t in range(NT):
                    for h in range(2):
                        user(l, ("c0", t, h), lambda ps: nc.scalar.copy(ZA[:, t, 336 * h:336 * h + 336],
                                                                        ps[:, 0:336]))
                    act.wait_ge(user_act.s, user_act.at(l, evacuated(USER_AT["c0", t, 1])))
                    nc.scalar.activation(SQG[:, t, 0:QR], ZA[:, t, 0:QR], ACT.Square, accum_out=ST2[:, t:t + 1])
                    ins = nc.scalar.activation(SQG[:, t, QR:640], ZA[:, t, Z_KV:Z_KV + KVR], ACT.Square,
                                               accum_out=ST2[:, 3 + t:4 + t])
                ins.then_inc(sq2_ok.s, 1)
                act.wait_ge(ms2_ok.s, ms2_ok.at(l, 1))
                nc.scalar.activation(R2, R2, ACT.Sqrt).then_inc(root2_ok.s, 1)
                act.wait_ge(tr_mm.s, tr_mm.at(l, 1))
                nc.scalar.copy(CQT, PS[:, 0:3, 0:TOK]).then_inc(tr_act.s, 1)
                for t in range(NT):
                    for h in range(2):
                        user(l, ("q", t, h), lambda ps: nc.scalar.copy(QQ[:, t, 384 * h:384 * h + 384],
                                                                       ps[:, 0:384]))
                act.wait_ge(lamp_ok.s, lamp_ok.at(l, 1))
                nc.scalar.activation(LE, LE, ACT.Exp).then_inc(lame_ok.s, 1)
                prep(l, 0)
                for i in range(NJ + 1):
                    if i < NJ:
                        exps(l, i)
                    if i + 1 < NJ:
                        prep(l, i + 1)
                    if i >= 1:
                        values(l, i - 1)
                    if i == 3:
                        act.wait_ge(msg_ok.s, msg_ok.at(l, 1))
                        nc.scalar.activation(RG, RG, ACT.Sqrt).then_inc(rootg_ok.s, 1)
                    for key in FILL[i]:
                        fill(l, key)
                    if i == 2:
                        act.wait_ge(user_act.s, user_act.at(l, evacuated(USER_AT["c1", 2, 1])))
                        nc.scalar.activation(SQG, ZG[:, :, 0:640], ACT.Square).then_inc(sqg_ok.s, 1)
                    if i < NJ:
                        for m in range(2 if JOBS[i][0] == "gqa" else 1):
                            n = OUT_AT[i, m]
                            act.wait_ge(pt_mm.s, pt_mm.at(l, n + 1))
                            if n >= 2:
                                act.wait_ge(user_mm.s, user_mm.at(l, USER_AT["pv", OUTS[n - 2][0]] + 1))
                            nc.scalar.copy(PT[:, n % 2, 0:384], PS[:, 4, 0:384]).then_inc(pt_act.s, 1)
                act.wait_ge(user_act.s, user_act.at(l, evacuated(USER_AT["pv", NJ - 1])))
                nc.scalar.activation(SQD, OT2, ACT.Square).then_inc(sqd_ok.s, 1)
                act.wait_ge(stored_d.s, stored_d.at(l, 32))
                for c in range(KC):
                    fill(l, ("gate2", c))
                act.wait_ge(msd_ok.s, msd_ok.at(l, 1))
                nc.scalar.activation(RSD, RSD, ACT.Sqrt).then_inc(rootd_ok.s, 1)
                act.wait_ge(gb_mm.s, gb_mm.at(l, 1))
                nc.scalar.mul(G1, PS[:, 0:4, :].rearrange("p (s h) n -> p s (h n)", s=2), 0.5).then_inc(gb_ok.s, 1)
                act.wait_ge(x1_ok.s, x1_ok.at(l, 1))
                norm_root(l, 1)
                ht_even(l, 1)
                act.wait_ge(gb_mm.s, gb_mm.at(l, 2))
                nc.scalar.copy(G2, PS[:, 4:8, :].rearrange("p (s h) n -> p s (h n)", s=2)).then_inc(gb_ok.s, 1)
                act.wait_ge(logit_ok.s, logit_ok.at(l, 1))
                nc.scalar.activation(LG, LG, ACT.Exp).then_inc(aexp_ok.s, 1)
                for c in range(KC):
                    n = 2 * c
                    act.wait_ge(gather_mm.s, gather_mm.at(l, n + 1))
                    v = 24 + c
                    nc.scalar.activation(XE[:, c, :, 0:CAP_S],
                                         PS[:, n % 4, :].rearrange("p (e s) -> p e s", e=NE), ACT.Identity,
                                         scale=AA[:, 1, 1, c:c + 1], bias=MODC[:, 1, v // 12, v % 12:v % 12 + 1])\
                        .then_inc(gather_act.s, 1)
                with act.Fori(0, NG) as g:
                    for e in range(GE):
                        act.wait_ge(gu_mm.s, gu_mm.in_group(l, g, 2 * e + 1))
                        act.wait_ge(ac_ok.s, ac_ok.in_group(l, g, e))
                        nc.scalar.activation(SGE, PS[:, e % 2], ACT.Sigmoid).then_inc(sig_ok.s, 1)
                        act.wait_ge(at_mm.s, at_mm.in_group(l, g, e + 1))
                        nc.scalar.copy(AT, PS[:, 4].rearrange("p (q n) -> p q n", q=4)).then_inc(at_ok.s, 1)
                        act.wait_ge(y_mm.s, y_mm.in_group(l, g, e + 1))
                        if e == 0:
                            act.wait_ge(comb_mm.s, comb_mm.in_group(l, g, 0))
                        for h in range(2):
                            nc.scalar.copy(YS[32 * e:32 * e + 32, 0, BF * h:BF * h + BF],
                                           PS[64 * h:64 * h + 32, 5])
                            ins = nc.scalar.copy(YS[32 * e:32 * e + 16, 1, BF * h:BF * h + BF],
                                                 PS[64 * h + 32:64 * h + 48, 5])
                        ins.then_inc(y_ok.s, 1)
            act.wait_ge(xg_ok.s, DEPTH * NG + 1)
            for t in range(NT):
                ins = nc.scalar.activation(XN[:, t], X[:, t], ACT.Square, accum_out=ST[:, t:t + 1])
            ins.then_inc(fin_ss.s, 1)
            act.wait_ge(fin_ms.s, 1)
            nc.scalar.activation(RS, RS, ACT.Sqrt).then_inc(fin_root.s, 1)

        @block.vector
        def _(dve):
            links = [0]

            def link(ins, l):
                links[0] += 1
                ins.then_inc(dve_chain.s, 1)
                dve.wait_ge(dve_chain.s, dve_chain.at(l, links[0]))

            def norm_rows(l, n):
                dve.wait_ge(ss_ok.s, ss_ok.at(l, n + 1))
                nc.vector.tensor_scalar(RS, ST, 1.0 / D, EPS, ALU.mult, ALU.add).then_inc(ms_ok.s, 1)
                dve.wait_ge(root_ok.s, root_ok.at(l, n + 1))
                link(nc.vector.reciprocal(RS, RS), l)
                for t in range(NT):
                    nc.vector.tensor_scalar(XN[:, t], X[:, t], RS[:, t:t + 1], None, ALU.mult).then_inc(xn_ok.s, 1)

            def ht_odd(l, n):
                for c in range(1, KC, 2):
                    dve.wait_ge(ht_mm.s, ht_mm.at(l, 8 * n + c + 1))
                    ps = PS[:, 4 + c % 4]
                    for s, lo, hi in ((0, 0, P), (1, P, TOK)):
                        v = 24 * n + c
                        ins = nc.vector.tensor_scalar(hT[:, c, lo:hi], ps[:, lo:hi], AA[:, n, s, c:c + 1],
                                                      MODC[:, s, v // 12, v % 12:v % 12 + 1], ALU.mult, ALU.add)
                    ins.then_inc(ht_dve.s, 1)

            def maxima(l, j):
                kind, _ = JOBS[j]
                for m in range(1 if kind == "mla" else 2):
                    n = MAP_AT[j, m]
                    b = n % 2
                    dve.wait_ge(score_mm.s, score_mm.at(l, n + 1))
                    if n >= 2:
                        dve.wait_ge(exp_ok.s, exp_ok.at(l, n - 1))
                    for r, (w, bank, c) in enumerate(((384, 0, 0), (128, 0, 384), (384, 1, 0))):
                        ins = nc.vector.reduce_max(MX[:, b, r:r + 1], PS[:, 2 * m + bank, c:c + w], AX)
                    link(ins, l)
                    nc.vector.tensor_scalar(NB[:, b], MX[:, b], -SCALE[kind], None, ALU.mult).then_inc(max_ok.s, 1)

            def prep(l, j):
                kind, i = JOBS[j]
                dve.wait_ge(prep_mm.s, prep_mm.at(l, j + 1))
                if kind == "mla":
                    ins = nc.vector.tensor_copy(KT[0:NOPE, j % 2], PS[0:NOPE, 4])
                else:
                    if kind == "diff":
                        nc.vector.tensor_copy(KT[:, j % 2], PS[:, 4])
                    elif i == 0:
                        for g in range(2):
                            for r in range(2):
                                nc.vector.tensor_copy(KT[64 * r:64 * r + 64, g], PS[64 * g:64 * g + 64, 4])
                    ins = nc.vector.tensor_copy(QAB[64:128, j % 2, 1], PS[64:128, 5, 0:TOK])
                ins.then_inc(prep_dve.s, 1)

            def normalise(l, j):
                kind, _ = JOBS[j]
                rows = ((0, 384), (384, 512), (512, 896))
                for m in range(1 if kind == "mla" else 2):
                    n = MAP_AT[j, m]
                    b = n % 2
                    dve.wait_ge(exp_ok.s, exp_ok.at(l, n + 1))
                    link(nc.vector.reciprocal(RC[:, b], SM[:, b]), l)
                    if kind == "diff" and m == 1:
                        link(nc.vector.tensor_scalar(RC[:, b], RC[:, b], LAM, None, ALU.mult), l)
                        for r, (lo, hi) in enumerate(rows):
                            ins = nc.vector.scalar_tensor_tensor(
                                out=PB[:, 0, lo:hi], in0=PB[:, 1, lo:hi], scalar=RC[:, b, r:r + 1],
                                in1=PB[:, 0, lo:hi], op0=ALU.mult, op1=ALU.add)
                    else:
                        for r, (lo, hi) in enumerate(rows):
                            ins = nc.vector.tensor_scalar(PB[:, b, lo:hi], PB[:, b, lo:hi], RC[:, b, r:r + 1],
                                                          None, ALU.mult)
                    if kind == "diff" and m == 0:
                        link(ins, l)
                    else:
                        ins.then_inc(prob_ok.s, 1)

            def branch(l, key):
                kind, c = key
                n = USER_AT[key]
                dve.wait_ge(user_mm.s, user_mm.at(l, n + 1))
                dve.wait_ge(user_act.s, user_act.at(l, evacuated(USER_AT["gate" + kind[2], c])))
                ps = PS[:, 6 + n % 2, 0:TOK]
                gate = {"br0": MG[:, c], "br1": SG1[:, c % 2], "br2": SG2[:, c]}[kind]
                if kind == "br0":
                    nc.vector.scalar_tensor_tensor(out=gate, in0=gate, scalar=1.0, in1=ps, op0=ALU.add,
                                                   op1=ALU.mult).then_inc(user_dve.s, 1)
                else:
                    link(nc.vector.scalar_tensor_tensor(out=gate, in0=gate, scalar=1.0, in1=ps, op0=ALU.add,
                                                        op1=ALU.mult), l)
                    nc.vector.tensor_tensor(MG[:, c], MG[:, c], gate, ALU.add).then_inc(user_dve.s, 1)

            for free in (xg_ok, ac_ok, comb_ok):
                dve.sem_inc(free.s, 1)
            dve.wait_ge(const_in.s, 16)
            nc.vector.memset(MODR, 0.0)
            dve.wait_ge(cond_sig.s, 1)
            nc.vector.tensor_tensor(SC.rearrange("p k s -> p s k"),
                                    PS[:, 0, 0:16].rearrange("p (s k) -> p s k", s=2),
                                    SIGC.rearrange("p (s k) -> p s k", s=2), ALU.mult).then_inc(cond_ok.s, 1)
            with dve.Fori(0, DEPTH) as l:
                links[0] = 0
                norm_rows(l, 0)
                dve.wait_ge(mod_t.s, mod_t.at(l, 1))
                nc.vector.tensor_copy(NCOL, PS[:, 3, 0:16].rearrange("p (n k) -> p n k", n=2)).then_inc(ncol_ok.s, 1)

                def mod_rows(i):
                    dve.wait_ge(ada_mm.s, ada_mm.at(l, i + 1))
                    for j in range(4):
                        r = slice(32 * j, 32 * j + 2)
                        ins = nc.vector.tensor_tensor(MODR[r, BF * i:BF * i + BF], PS[r, i],
                                                      BR[r, BF * i:BF * i + BF], ALU.add)
                    ins.then_inc(mod_row.s, 1)

                def mod_cols(i):
                    dve.wait_ge(mod_t.s, mod_t.at(l, 2 + i))
                    for s in range(2):
                        src = PS[:, 3].rearrange("p (q j r) -> p j q r", q=4, j=4)[:, :, :, s]
                        ins = nc.vector.tensor_copy(MODC[:, s, :, 4 * i:4 * i + 4], src)
                    ins.then_inc(mod_col.s, 1)

                dve.wait_ge(early_in.s, early_in.at(l, 96))
                mod_rows(0)
                mod_rows(1)
                mod_cols(0)
                mod_rows(2)
                mod_cols(1)
                mod_cols(2)
                dve.wait_ge(mod_col.s, mod_col.at(l, 3))
                for n in range(2):
                    for s in range(2):
                        scale = MODC[:, s].rearrange("p j q -> p (j q)")[:, 24 * n + 8:24 * n + 16]
                        ins = nc.vector.scalar_tensor_tensor(out=AA[:, n, s], in0=scale, scalar=1.0,
                                                             in1=NCOL[:, n], op0=ALU.add, op1=ALU.mult)
                ins.then_inc(aa_ok.s, 1)
                dve.wait_ge(aa_ok.s, aa_ok.at(l, 1))
                ht_odd(l, 0)
                dve.wait_ge(late_in.s, late_in.at(l, 18 * 16))
                dve.wait_ge(sq2_ok.s, sq2_ok.at(l, 1))
                nc.vector.tensor_scalar(R2[:, 0:3], ST2[:, 0:3], 1.0 / QR, EPS, ALU.mult, ALU.add)
                nc.vector.tensor_scalar(R2[:, 3:6], ST2[:, 3:6], 1.0 / KVR, EPS, ALU.mult, ALU.add)\
                    .then_inc(ms2_ok.s, 1)
                dve.wait_ge(root2_ok.s, root2_ok.at(l, 1))
                link(nc.vector.reciprocal(R2, R2), l)
                for t in range(NT):
                    for col, w, gain, r in ((0, QR, GNQ, t), (Z_KV, KVR, GNK, 3 + t)):
                        z = ZA[:, t, col:col + w]
                        ins = nc.vector.scalar_tensor_tensor(out=z, in0=z, scalar=R2[:, r:r + 1], in1=gain,
                                                             op0=ALU.mult, op1=ALU.mult)
                ins.then_inc(za_ok.s, 1)
                link(nc.vector.tensor_tensor(LP, LAMV[:, 0:2], LAMV[:, 2:4], ALU.mult), l)
                nc.vector.reduce_sum(LE, LP, AX).then_inc(lamp_ok.s, 1)
                nc.vector.tensor_copy(LIC, CST[:, bass.ds(l * 2 + C_LAM, 2)])
                dve.wait_ge(tr_mm.s, tr_mm.at(l, 2))
                nc.vector.tensor_copy(CKT, PS[:, 3:5, :]).then_inc(tr_dve.s, 1)
                dve.wait_ge(tr_mm.s, tr_mm.at(l, 3))
                nc.vector.tensor_copy(KT[NOPE:QD, 0], PS[0:ROPE, 5])
                nc.vector.tensor_copy(KT[NOPE:QD, 1], PS[0:ROPE, 5]).then_inc(tr_dve.s, 1)
                for t in range(4):
                    n = USER_AT["v", t]
                    dve.wait_ge(user_mm.s, user_mm.at(l, n + 1))
                    nc.vector.tensor_copy(VM[:, t], PS[:, 6 + n % 2]).then_inc(user_dve.s, 1)
                dve.wait_ge(lame_ok.s, lame_ok.at(l, 1))
                link(nc.vector.tensor_tensor(LAM, LE[:, 1:2], LE[:, 0:1], ALU.subtract), l)
                link(nc.vector.tensor_tensor(LAM, LAM, LIC[:, 0:1], ALU.subtract), l)
                nc.vector.tensor_tensor(SUB, SUB, LIC[:, 1:2], ALU.mult)
                prep(l, 0)
                for i in range(NJ + 1):
                    if i < NJ:
                        maxima(l, i)
                    if i + 1 < NJ:
                        prep(l, i + 1)
                    if i < NJ:
                        normalise(l, i)
                    if i == 3:
                        dve.wait_ge(sqg_ok.s, sqg_ok.at(l, 1))
                        link(nc.vector.reduce_sum(STG, SQG.rearrange("p t (h d) -> p (t h) d", d=64), AX), l)
                        nc.vector.tensor_scalar(RG, STG, 1.0 / 64, EPS, ALU.mult, ALU.add).then_inc(msg_ok.s, 1)
                        dve.wait_ge(rootg_ok.s, rootg_ok.at(l, 1))
                        nc.vector.reciprocal(RG, RG).then_inc(rg_ok.s, 1)
                    for key in FILL[i]:
                        if key[0] in ("br0", "br1"):
                            branch(l, key)
                    if i < NJ:
                        for m in range(2 if JOBS[i][0] == "gqa" else 1):
                            n = OUT_AT[i, m]
                            dve.wait_ge(pt_mm.s, pt_mm.at(l, n + 1))
                            if n >= 2:
                                dve.wait_ge(user_mm.s, user_mm.at(l, USER_AT["pv", OUTS[n - 2][0]] + 1))
                            nc.vector.tensor_copy(PT[:, n % 2, 384:896], PS[:, 5]).then_inc(pt_dve.s, 1)
                dve.wait_ge(sqd_mm.s, sqd_mm.at(l, 1))
                nc.vector.tensor_scalar(RSD, PS[:, 0:4, 0:TOK], 1.0 / 128, EPS, ALU.mult, ALU.add)\
                    .then_inc(msd_ok.s, 1)
                dve.wait_ge(rootd_ok.s, rootd_ok.at(l, 1))
                link(nc.vector.reciprocal(RSD, RSD), l)
                nc.vector.scalar_tensor_tensor(out=OT2, in0=OT2, scalar=SUB, in1=RSD, op0=ALU.mult,
                                               op1=ALU.mult).then_inc(ot2_ok.s, 1)
                for c in range(KC):
                    branch(l, ("br2", c))
                dve.wait_ge(gb_ok.s, gb_ok.at(l, 1))
                for t in range(NT):
                    for h in range(2):
                        n = USER_AT["out", t, h]
                        dve.wait_ge(user_mm.s, user_mm.at(l, n + 1))
                        x = X[:, t, BF * h:BF * h + BF]
                        nc.vector.tensor_tensor(TMP[:, h], PS[:, 6 + n % 2], G1[:, min(t, 1), BF * h:BF * h + BF],
                                                ALU.mult).then_inc(user_dve.s, 1)
                        dve.wait_ge(user_dve.s, user_dve.at(l, evacuated(n)))
                        ins = nc.vector.tensor_tensor(x, x, TMP[:, h], ALU.add)
                ins.then_inc(x1_ok.s, 1)
                dve.wait_ge(x1_ok.s, x1_ok.at(l, 1))
                norm_rows(l, 1)
                ht_odd(l, 1)
                dve.wait_ge(router_mm.s, router_mm.at(l, 1))
                ps = PS[:, 0, 0:NT * NE].rearrange("p (t e) -> p t e", t=NT)
                link(nc.vector.reduce_max(ST, ps, AX), l)
                st = ST.rearrange("p (t o) -> p t o", o=1).to_broadcast([P, NT, NE])
                nc.vector.tensor_tensor(LG, ps, st, ALU.subtract).then_inc(logit_ok.s, 1)
                dve.wait_ge(aexp_ok.s, aexp_ok.at(l, 1))
                link(nc.vector.reduce_sum(ST, LG, AX), l)
                link(nc.vector.reciprocal(RS, ST), l)
                nc.vector.tensor_tensor(AFF, LG, RS.rearrange("p (t o) -> p t o", o=1).to_broadcast([P, NT, NE]),
                                        ALU.mult).then_inc(aff_ok.s, 1)
                dve.wait_ge(aff_t.s, aff_t.at(l, 1))
                link(nc.vector.tensor_copy(WK, PS[0:NE, 1, 0:TOK]), l)
                for lo, hi, rounds in ((0, P, CAP_P // 8), (P, TOK, CAP_S // 8)):
                    for _ in range(rounds):
                        apart(dve)
                        link(nc.vector.max(M8, WK[:, lo:hi]), l)
                        apart(dve)
                        link(nc.vector.match_replace(WK[:, lo:hi], M8, WK[:, lo:hi], -1.0), l)
                nc.vector.memset(AFT, 1.0)
                link(nc.vector.tensor_scalar(MK, WK, 0.0, None, ALU.is_lt), l)
                for lo, hi in ((0, P), (P, TOK)):
                    ins = nc.vector.tensor_tensor_scan(SN[:, lo:hi], AFT[:, lo:hi], MK[:, lo:hi], 0.0,
                                                       ALU.mult, ALU.add)
                link(ins, l)
                nc.vector.tensor_tensor(SN, SN, MK, ALU.mult).then_inc(pos_ok.s, 1)
                dve.wait_ge(pos_t.s, pos_t.at(l, 1))
                link(nc.vector.tensor_copy(POS, PS[:, 2, 0:NT * NE].rearrange("p (t e) -> p t e", t=NT)), l)
                for t in range(NT):
                    pos = POS[:, t].rearrange("p (e o) -> p e o", o=1).to_broadcast([P, NE, CAP_S])
                    iota = IOTA.rearrange("p (o s) -> p o s", o=1).to_broadcast([P, NE, CAP_S])
                    ins = nc.vector.tensor_tensor(DD[:, t], pos, iota, ALU.is_equal)
                link(ins, l)
                for t in range(NT):
                    aff = AFF[:, t].rearrange("p (e o) -> p e o", o=1).to_broadcast([P, NE, CAP_S])
                    ins = nc.vector.tensor_tensor(DG[:, t], DD[:, t], aff, ALU.mult)
                ins.then_inc(disp_ok.s, 1)
                for c in range(KC):
                    n = 2 * c + 1
                    dve.wait_ge(gather_mm.s, gather_mm.at(l, n + 1))
                    v = 24 + c
                    nc.vector.tensor_scalar(XE[:, c, :, CAP_S:CAP],
                                            PS[:, n % 4, 0:NE * CAP_P].rearrange("p (e s) -> p e s", e=NE),
                                            AA[:, 1, 0, c:c + 1], MODC[:, 0, v // 12, v % 12:v % 12 + 1],
                                            ALU.mult, ALU.add).then_inc(gather_dve.s, 1)
                dve.wait_ge(dgt_mm.s, dgt_mm.at(l, 1))
                nc.vector.tensor_copy(DGT, PS[:, 4:7, :].rearrange("p a b -> p (a b)")
                                      .rearrange("p (g n) -> p g n", g=NG)).then_inc(dgt_ok.s, 1)
                nc.vector.memset(XB[:, :, :, CAP:XW], 0.0)
                nc.vector.memset(YS[:, 1], 0.0)
                dve.wait_ge(gather_act.s, gather_act.at(l, 8))
                dve.wait_ge(gather_dve.s, gather_dve.at(l, 8))
                dve.wait_ge(dgt_ok.s, dgt_ok.at(l, 1))
                dve.wait_ge(gb_ok.s, gb_ok.at(l, 2))
                apart(dve)
                with dve.Fori(0, NG) as g:
                    dve.wait_ge(comb_mm.s, comb_mm.in_group(l, g, 0))
                    nc.vector.tensor_copy(DGB, DGT.rearrange("p g n -> p (g n)")[:, bass.ds(g * (NT * P), NT * P)])\
                        .then_inc(dgb_ok.s, 1)

                    def tokens(e):
                        xe = XE[:, :, bass.ds(g * GE + e, 1), :].rearrange("p k e s -> p k (e s)")
                        nc.vector.tensor_copy(XB[:, e % 2, :, 0:CAP], xe).then_inc(xb_ok.s, 1)

                    tokens(0)
                    for e in range(GE):
                        if e + 1 < GE:
                            if e >= 1:
                                dve.wait_ge(gu_mm.s, gu_mm.in_group(l, g, 2 * e))
                            tokens(e + 1)
                        dve.wait_ge(sig_ok.s, sig_ok.in_group(l, g, e + 1))
                        dve.wait_ge(at_mm.s, at_mm.in_group(l, g, e))
                        nc.vector.tensor_tensor(AC, PS[:, e % 2], SGE, ALU.mult).then_inc(silu_ok.s, 1)
                        dve.wait_ge(silu_ok.s, silu_ok.in_group(l, g, e + 1))
                        dve.wait_ge(gu_mm.s, gu_mm.in_group(l, g, 2 * e + 2))
                        nc.vector.tensor_tensor(AC, AC, PS[:, 2 + e % 2], ALU.mult).then_inc(ac_ok.s, 1)
                    for n in range(6):
                        t, h = n // 2, n % 2
                        x = X[:, t, BF * h:BF * h + BF]
                        dve.wait_ge(comb_mm.s, comb_mm.in_group(l, g, n + 1))
                        nc.vector.tensor_tensor(CTMP[:, h], PS[:, 6 + h], G2[:, min(t, 1), BF * h:BF * h + BF],
                                                ALU.mult).then_inc(comb_ok.s, 1)
                        dve.wait_ge(comb_ok.s, comb_ok.in_group(l, g, n + 1))
                        ins = nc.vector.tensor_tensor(x, x, CTMP[:, h], ALU.add)
                    ins.then_inc(xg_ok.s, 1)
                    dve.wait_ge(xg_ok.s, xg_ok.in_group(l, g, 1))
                assert links[0] == DVE_LINKS, ("DVE_LINKS", links[0])
            dve.wait_ge(fin_ss.s, 1)
            nc.vector.tensor_scalar(RS, ST, 1.0 / D, EPS, ALU.mult, ALU.add).then_inc(fin_ms.s, 1)
            dve.wait_ge(fin_root.s, 1)
            nc.vector.reciprocal(RS, RS).then_inc(fin_ms.s, 1)
            dve.wait_ge(fin_ms.s, 2)
            dve.wait_ge(fn_in.s, 16)
            for t in range(NT):
                nc.vector.scalar_tensor_tensor(out=XN[:, t], in0=X[:, t], scalar=RS[:, t:t + 1], in1=at(0, D),
                                               op0=ALU.mult, op1=ALU.mult).then_inc(fin_ok.s, 1)

        @block.tensor
        def _(pe):
            def arrived(l, n):
                pe.wait_ge(filled[n % SLOTS].s, (l * USES + n // SLOTS + 1) * 16)

            owed = []

            def settle(ins):
                if owed:
                    ins.then_inc(used[owed.pop()].s, 1)
                return ins

            def user_bank(l, key):
                n = USER_AT[key]
                if n >= 2:
                    freed = user_dve if USERS[n - 2][0] in BY_DVE else user_act
                    pe.wait_ge(freed.s, freed.at(l, evacuated(n - 2)))
                return PS[:, 6 + n % 2]

            def turn(out, src, rows=P):
                return pe.transpose(out, src, IDT[0:rows, 0:rows])

            def norm_turn(l, n):
                pe.wait_ge(xn_ok.s, xn_ok.at(l, NT * (n + 1)))
                for c in range(KC):
                    if c >= 4:
                        freed = ht_dve if c % 2 else ht_act
                        pe.wait_ge(freed.s, freed.at(l, 4 * n + (c - 4) // 2 + 1))
                    for t in range(NT):
                        ins = turn(PS[:, 4 + c % 4, P * t:P * t + P], XN[:, t, P * c:P * c + P])
                        if (c, t) == (0, 0):
                            settle(ins)
                    ins.then_inc(ht_mm.s, 1)

            def project(l, key, units, stride, width, col, t, last):
                ps = user_bank(l, key)
                for k in range(KC):
                    n = units[k // 2]
                    if k % 2 == 0:
                        arrived(l, n)
                    c0 = (k % 2) * stride + col
                    ins = pe.matmul(ps[:, 0:width], hT[:, k, P * t:P * t + P], ring[:, n % SLOTS, c0:c0 + width],
                                    start=k == 0, stop=k == KC - 1)
                    if k == 0:
                        settle(ins)
                    if last and k % 2 and k < KC - 1:
                        ins.then_inc(used[n % SLOTS].s, 1)
                ins.then_inc(user_mm.s, 1)
                if last:
                    owed.append(n % SLOTS)

            def gate(l, b, c):
                ps = user_bank(l, (f"gate{b}", c))
                n = UNIT[f"gate{b}", c // 2]
                arrived(l, n)
                w = ring[:, n % SLOTS].rearrange("p (k n) -> p k n", k=KC)
                for k in range(KC):
                    ins = pe.matmul(ps[:, 0:TOK], w[:, k, P * (c % 2):P * (c % 2) + P], hT[:, k], start=k == 0,
                                    stop=k == KC - 1)
                    if k == 0:
                        settle(ins)
                ins.then_inc(user_mm.s, 1)
                if c % 2:
                    owed.append(n % SLOTS)

            def branch(l, b, c):
                ps = user_bank(l, (f"br{b}", c))
                n = UNIT[f"br{b}", c // 4]
                arrived(l, n)
                if b < 2:
                    j = 7 if b == 0 else 11
                    pe.wait_ge(user_act.s, user_act.at(l, evacuated(USER_AT["pv", j])))
                else:
                    pe.wait_ge(ot2_ok.s, ot2_ok.at(l, 1))
                w = ring[:, n % SLOTS].rearrange("p (k n) -> p k n", k=4)
                o = (OT0, OT1, OT2)[b]
                for k in range(4):
                    ins = pe.matmul(ps[:, 0:TOK], w[:, k, P * (c % 4):P * (c % 4) + P], o[:, k], start=k == 0,
                                    stop=k == 3)
                    if k == 0:
                        settle(ins)
                ins.then_inc(user_mm.s, 1)
                if c % 4 == 3:
                    owed.append(n % SLOTS)

            def fill(l, key):
                kind = key[0]
                if kind == "c1":
                    project(l, key, [UNIT["c1", u] for u in range(4)], ZG_W, 384, 384 * key[2], key[1],
                            key[1:] == (2, 1))
                elif kind == "c2":
                    half, t, q = key[1] // 6, key[1] % 6 // 2, key[1] % 2
                    project(l, key, [UNIT["c2", 4 * half + u] for u in range(4)], 768, 384, 384 * q, t,
                            (t, q) == (2, 1))
                elif kind.startswith("gate"):
                    gate(l, int(kind[4]), key[1])
                else:
                    branch(l, int(kind[2]), key[1])

            def prep(l, j):
                kind, i = JOBS[j]
                if j >= 2:
                    before = OUT_AT[j - 2, 1 if JOBS[j - 2][0] == "gqa" else 0] + 1
                    pe.wait_ge(pt_act.s, pt_act.at(l, before))
                    pe.wait_ge(pt_dve.s, pt_dve.at(l, before))
                if j == 1:
                    pe.wait_ge(prep_act.s, prep_act.at(l, 1))
                    pe.wait_ge(prep_dve.s, prep_dve.at(l, 1))
                if kind == "mla":
                    for c in range(2):
                        settle(pe.matmul(PS[0:NOPE, 4], UKV[:, 0, c, NOPE * i:NOPE * i + NOPE], CKT[:, c],
                                         start=c == 0, stop=c == 1))
                    if i == 0:
                        pe.wait_ge(qrope_ok.s, qrope_ok.at(l, 1))
                    for t in range(NT):
                        ins = turn(PS[0:QD, 5, P * t:P * t + P], QQ[:, t, QD * i:QD * i + QD])
                elif kind == "gqa":
                    if i == 0:
                        pe.wait_ge(gq_ok.s, gq_ok.at(l, 1))
                        for kt, src in enumerate((ZG[:, 0, G_K:G_K + 128], CTX_GK, ZG[:, 1, G_K:G_K + 128],
                                                  ZG[:, 2, G_K:G_K + 128])):
                            settle(turn(PS[:, 4, P * kt:P * kt + P], src))
                    for t in range(NT):
                        ins = turn(PS[:, 5, P * t:P * t + P], ZG[:, t, P * i:P * i + P])
                        if t == 0:
                            settle(ins)
                else:
                    if i == 0:
                        pe.wait_ge(dq_ok.s, dq_ok.at(l, 1))
                    k0 = D_K + P * i
                    for kt, src in enumerate((ZD[:, 0, k0:k0 + P], CTX_DK[:, P * i:P * i + P], ZD[:, 1, k0:k0 + P],
                                              ZD[:, 2, k0:k0 + P])):
                        settle(turn(PS[:, 4, P * kt:P * kt + P], src))
                    for t in range(NT):
                        ins = turn(PS[:, 5, P * t:P * t + P], ZD[:, t, P * i:P * i + P])
                ins.then_inc(prep_mm.s, 1)

            def scores(l, j):
                kind, i = JOBS[j]
                pe.wait_ge(prep_act.s, prep_act.at(l, j + 1))
                pe.wait_ge(prep_dve.s, prep_dve.at(l, j + 1))
                if j >= 1:
                    n = MAP_AT[j - 1, 0 if JOBS[j - 1][0] == "mla" else 1]
                    pe.wait_ge(exp_ok.s, exp_ok.at(l, n + 1))
                if (kind, i) == ("gqa", 0):
                    pe.wait_ge(zero_ok.s, zero_ok.at(l, 1))
                b = j % 2
                for m in range(1 if kind == "mla" else 2):
                    q = QM[0:QD, b] if kind == "mla" else QAB[:, b, m]
                    k = KT[0:QD, b] if kind == "mla" else KT[:, i // 2 if kind == "gqa" else b]
                    settle(pe.matmul(PS[:, 2 * m, 0:384], q[:, P:2 * P], k[:, P:NKEY], start=True, stop=True))
                    pe.matmul(PS[:, 2 * m, 384:512], q[:, 0:P], k[:, 0:P], start=True, stop=True)
                    pe.matmul(PS[:, 2 * m + 1, 0:384], q[:, 2 * P:TOK], k[:, P:NKEY], start=True, stop=True)\
                        .then_inc(score_mm.s, 1)

            def turn_probs(l, j):
                for m in range(2 if JOBS[j][0] == "gqa" else 1):
                    n = OUT_AT[j, m]
                    pe.wait_ge(prob_ok.s, prob_ok.at(l, n + 1))
                    if m == 0 and j + 1 < NJ:
                        pe.wait_ge(prep_act.s, prep_act.at(l, j + 2))
                        pe.wait_ge(prep_dve.s, prep_dve.at(l, j + 2))
                    elif n >= 1:
                        pe.wait_ge(pt_act.s, pt_act.at(l, n))
                        pe.wait_ge(pt_dve.s, pt_dve.at(l, n))
                    p = PB[:, MAP_AT[j, m] % 2]
                    settle(turn(PS[:, 4, 0:P], p[:, 384:512]))
                    for q, at_q in enumerate((0, 512)):
                        turn(PS[:, 4, P * (q + 1):P * (q + 2)], p[:, at_q:at_q + P])
                    for kt in range(1, 3):
                        for q, at_q in enumerate((0, 512)):
                            ins = turn(PS[:, 5, 256 * (kt - 1) + P * q:256 * (kt - 1) + P * q + P],
                                       p[:, at_q + P * kt:at_q + P * kt + P])
                    ins.then_inc(pt_mm.s, 1)

            def values(l, j):
                kind, i = JOBS[j]
                ps = user_bank(l, ("pv", j))
                for m in range(2 if kind == "gqa" else 1):
                    n = OUT_AT[j, m]
                    pe.wait_ge(pt_act.s, pt_act.at(l, n + 1))
                    pe.wait_ge(pt_dve.s, pt_dve.at(l, n + 1))
                    if kind == "mla":
                        c = 64 * i
                        v = [VM[:, kt, c:c + 64] for kt in range(4)]
                        out = ps[64 * (i % 2):64 * (i % 2) + 64]
                    elif kind == "gqa":
                        kv = 64 * (i // 2)
                        c = G_V + kv
                        v = [ZG[:, 0, c:c + 64], CTX_GV[:, kv:kv + 64], ZG[:, 1, c:c + 64],
                             ZG[:, 2, c:c + 64]]
                        out = ps[64 * m:64 * m + 64]
                    else:
                        c = D_V + P * i
                        v = [ZD[:, 0, c:c + P], CTX_DV[:, P * i:P * i + P], ZD[:, 1, c:c + P], ZD[:, 2, c:c + P]]
                        out = ps
                    pt = PT[:, n % 2]
                    settle(pe.matmul(out[:, 0:P], v[0], pt[:, 0:P], start=True, stop=True))
                    for kt in range(3):
                        ins = pe.matmul(out[:, P:TOK], v[kt + 1], pt[:, P + 256 * kt:P + 256 * kt + 256],
                                        start=kt == 0, stop=kt == 2)
                ins.then_inc(user_mm.s, 1)

            def gate_rows(l, which, bank):
                for s in range(2):
                    sel = CST[:, C_SEL + (2 * which + s) * P:C_SEL + (2 * which + s + 1) * P]
                    for h in range(2):
                        ins = pe.matmul(PS[:, bank + 2 * s + h], sel, MODR[:, BF * (1 + h):BF * (2 + h)],
                                        start=True, stop=True)
                        if (s, h) == (0, 0):
                            settle(ins)
                ins.then_inc(gb_mm.s, 1)

            for free in (*used, router_mm, at_mm, comb_mm):
                pe.sem_inc(free.s, 1)
            pe.wait_ge(const_in.s, 16)
            pe.wait_ge(cond_in.s, 32)
            turn(PS[:, 0, 0:16], CR, 16).then_inc(cond_t.s, 1)
            pe.wait_ge(cond_ok.s, 1)
            with pe.Fori(0, DEPTH) as l:
                pe.wait_ge(early_in.s, early_in.at(l, 96))
                apart(pe)
                turn(PS[:, 3, 0:16], NR, 16).then_inc(mod_t.s, 1)

                def mod_turn(i):
                    pe.wait_ge(mod_row.s, mod_row.at(l, i + 1))
                    if i == 0:
                        pe.wait_ge(ncol_ok.s, ncol_ok.at(l, 1))
                    else:
                        pe.wait_ge(mod_col.s, mod_col.at(l, i))
                    for q in range(4):
                        ins = turn(PS[:, 3, P * q:P * q + P], MODR[:, BF * i + P * q:BF * i + P * q + P])
                        if q == 0:
                            settle(ins)
                    ins.then_inc(mod_t.s, 1)

                for i in range(3):
                    for k in range(KC):
                        n = UNIT["ada", i, k]
                        arrived(l, n)
                        for j in range(4):
                            ins = pe.matmul(PS[32 * j:32 * j + 2, i], SC[:, k], ring[:, n % SLOTS, BF * j:BF * j + BF],
                                            start=k == 0, stop=k == KC - 1)
                            if j == 0:
                                settle(ins)
                        if k < KC - 1:
                            ins.then_inc(used[n % SLOTS].s, 1)
                        else:
                            ins.then_inc(ada_mm.s, 1)
                            owed.append(n % SLOTS)
                    if i >= 1:
                        mod_turn(i - 1)
                mod_turn(2)
                norm_turn(l, 0)
                pe.wait_ge(ht_act.s, ht_act.at(l, 4))
                pe.wait_ge(ht_dve.s, ht_dve.at(l, 4))
                units = [UNIT["c0", u] for u in range(4)]
                for t in range(NT):
                    for h in range(2):
                        project(l, ("c0", t, h), units, ZA_W, 336, 336 * h, t, (t, h) == (2, 1))
                pe.wait_ge(za_ok.s, za_ok.at(l, 1))
                for c in range(3):
                    for t in range(NT):
                        ins = turn(PS[:, c, P * t:P * t + P], ZA[:, t, P * c:P * c + P])
                        if (c, t) == (0, 0):
                            settle(ins)
                ins.then_inc(tr_mm.s, 1)
                pe.wait_ge(late_in.s, late_in.at(l, 18 * 16))
                for c in range(2):
                    k0 = Z_KV + P * c
                    for kt, src in enumerate((ZA[:, 0, k0:k0 + P], CTX_CKV[:, P * c:P * c + P], ZA[:, 1, k0:k0 + P],
                                              ZA[:, 2, k0:k0 + P])):
                        ins = turn(PS[:, 3 + c, P * kt:P * kt + P], src)
                ins.then_inc(tr_mm.s, 1)
                pe.wait_ge(kpe_ok.s, kpe_ok.at(l, 1))
                for kt, src in enumerate((ZA[:, 0, Z_PE:Z_PE + ROPE], CTX_KPE, KPR[:, 0], KPR[:, 1])):
                    ins = turn(PS[0:ROPE, 5, P * kt:P * kt + P], src)
                ins.then_inc(tr_mm.s, 1)
                pe.wait_ge(tr_act.s, tr_act.at(l, 1))
                for t in range(NT):
                    for h in range(2):
                        ps = user_bank(l, ("q", t, h))
                        for k in range(3):
                            n = UNIT["uq", k // 2]
                            arrived(l, n)
                            c0 = (k % 2) * 768 + 384 * h
                            ins = pe.matmul(ps[:, 0:384], CQT[:, k, P * t:P * t + P],
                                            ring[:, n % SLOTS, c0:c0 + 384], start=k == 0, stop=k == 2)
                            if (t, h) == (2, 1) and k == 1:
                                ins.then_inc(used[n % SLOTS].s, 1)
                        ins.then_inc(user_mm.s, 1)
                owed.append(n % SLOTS)
                pe.wait_ge(tr_dve.s, tr_dve.at(l, 2))
                for kt in range(4):
                    ps = user_bank(l, ("v", kt))
                    for c in range(2):
                        ins = pe.matmul(ps, CKT[:, c, P * kt:P * kt + P], UKV[:, 1, c], start=c == 0, stop=c == 1)
                        if c == 0:
                            settle(ins)
                    ins.then_inc(user_mm.s, 1)
                prep(l, 0)
                for i in range(NJ + 1):
                    if i < NJ:
                        scores(l, i)
                    if i + 1 < NJ:
                        prep(l, i + 1)
                    if i >= 1:
                        values(l, i - 1)
                    for key in FILL[i]:
                        fill(l, key)
                    if i < NJ:
                        turn_probs(l, i)
                for c in range(KC):
                    gate(l, 2, c)
                    if c == 1:
                        pe.wait_ge(sqd_ok.s, sqd_ok.at(l, 1))
                        for h in range(4):
                            ins = pe.matmul(PS[:, h, 0:TOK], ONES, SQD[:, h], start=True, stop=True)
                            if h == 0:
                                settle(ins)
                        ins.then_inc(sqd_mm.s, 1)
                pe.wait_ge(msd_ok.s, msd_ok.at(l, 1))
                pe.wait_ge(stored_d.s, stored_d.at(l, 32))
                gate_rows(l, 0, 0)
                for c in range(KC):
                    branch(l, 2, c)
                pe.wait_ge(user_dve.s, user_dve.at(l, evacuated(USER_AT["br2", KC - 1])))
                for t in range(NT):
                    for h in range(2):
                        ps = user_bank(l, ("out", t, h))
                        for k in range(KC):
                            n = UNIT["wout", k // 2]
                            arrived(l, n)
                            c0 = (k % 2) * D + BF * h
                            ins = pe.matmul(ps, MG[:, k, P * t:P * t + P], ring[:, n % SLOTS, c0:c0 + BF],
                                            start=k == 0, stop=k == KC - 1)
                            if k == 0:
                                settle(ins)
                            if (t, h) == (2, 1) and k % 2 and k < KC - 1:
                                ins.then_inc(used[n % SLOTS].s, 1)
                        ins.then_inc(user_mm.s, 1)
                owed.append(n % SLOTS)
                norm_turn(l, 1)
                pe.wait_ge(ht_act.s, ht_act.at(l, 8))
                pe.wait_ge(ht_dve.s, ht_dve.at(l, 8))
                for t in range(NT):
                    for k in range(KC):
                        ins = pe.matmul(PS[:, 0, NE * t:NE * t + NE], hT[:, k, P * t:P * t + P], WR[:, k],
                                        start=k == 0, stop=k == KC - 1)
                ins.then_inc(router_mm.s, 1)
                gate_rows(l, 1, 4)
                pe.wait_ge(aff_ok.s, aff_ok.at(l, 1))
                for t in range(NT):
                    ins = turn(PS[0:NE, 1, P * t:P * t + P], AFF[:, t])
                ins.then_inc(aff_t.s, 1)
                pe.wait_ge(pos_ok.s, pos_ok.at(l, 1))
                apart(pe)
                for t in range(NT):
                    ins = turn(PS[:, 2, NE * t:NE * t + NE], SN[:, P * t:P * t + P], NE)
                ins.then_inc(pos_t.s, 1)
                pe.wait_ge(disp_ok.s, disp_ok.at(l, 1))
                for c in range(KC):
                    for s in range(2):
                        n = 2 * c + s
                        if n >= 4:
                            freed = gather_dve if s else gather_act
                            pe.wait_ge(freed.s, freed.at(l, (n - 4) // 2 + 1))
                        if s == 0:
                            for t in range(1, 3):
                                ins = pe.matmul(PS[:, n % 4], XN[:, t, P * c:P * c + P],
                                                DD[:, t].rearrange("p e s -> p (e s)"), start=t == 1, stop=t == 2)
                        else:
                            ins = pe.matmul(PS[:, n % 4, 0:NE * CAP_P], XN[:, 0, P * c:P * c + P],
                                            DD[:, 0, :, 0:CAP_P], start=True, stop=True)
                        ins.then_inc(gather_mm.s, 1)
                pe.wait_ge(gb_ok.s, gb_ok.at(l, 2))
                for g in range(NG):
                    for t in range(NT):
                        n = NT * g + t
                        src = DG[:, t, GE * g:GE * g + GE].rearrange("p e s -> p (e s)")
                        ins = turn(PS[:, 4 + n // 4, P * (n % 4):P * (n % 4) + P], src)
                ins.then_inc(dgt_mm.s, 1)
                pe.wait_ge(dgt_ok.s, dgt_ok.at(l, 1))
                pe.wait_ge(gather_act.s, gather_act.at(l, 8))
                pe.wait_ge(gather_dve.s, gather_dve.at(l, 8))
                apart(pe)
                with pe.Fori(0, NG) as g:
                    def wide(e, first, lhs, bank, done):
                        for u in range(4):
                            n = 12 * e + first + u
                            pe.wait_ge(filled[n % SLOTS].s,
                                       (l * USES + g * (GROUP_UNITS // SLOTS) + (ATT_UNITS + n) // SLOTS + 1) * 16)
                            for k in range(2 * u, 2 * u + 2):
                                for h in range(2):
                                    c0 = (k % 2) * D + BF * h
                                    ins = pe.matmul(PS[64 * h:64 * h + 64, bank], lhs(k),
                                                    ring[:, n % SLOTS, c0:c0 + BF], start=k == 0, stop=k == KC - 1)
                                    if (k, h) == (0, 0):
                                        settle(ins)
                            if u < 3:
                                ins.then_inc(used[n % SLOTS].s, 1)
                        ins.then_inc(done.s, 1)
                        owed.append(n % SLOTS)

                    for e in range(GE):
                        pe.wait_ge(xb_ok.s, xb_ok.in_group(l, g, e + 1))
                        wide(e, 0, lambda k: XB[:, e % 2, k], e % 2, gu_mm)
                        wide(e, 4, lambda k: XB[:, e % 2, k], 2 + e % 2, gu_mm)
                        pe.wait_ge(ac_ok.s, ac_ok.in_group(l, g, e + 1))
                        for q in range(4):
                            ins = turn(PS[:, 4, P * q:P * q + P], AC[:, P * q:P * q + P])
                            if q == 0:
                                settle(ins)
                        ins.then_inc(at_mm.s, 1)
                        pe.wait_ge(at_ok.s, at_ok.in_group(l, g, e + 1))
                        pe.wait_ge(y_ok.s, y_ok.in_group(l, g, e))
                        wide(e, 8, lambda k: AT[:, k % 4, XW * (k // 4):XW * (k // 4) + XW], 5, y_mm)
                    pe.wait_ge(dgb_ok.s, dgb_ok.in_group(l, g, 1))
                    pe.wait_ge(y_ok.s, y_ok.in_group(l, g, GE))
                    for n in range(6):
                        t, h = n // 2, n % 2
                        pe.wait_ge(comb_ok.s, comb_ok.in_group(l, g, max(n - 1, 0)))
                        w = DGB[:, P * t:P * t + P]
                        for half in range(2):
                            y = YS[:, 0 if t else 1, BF * h + 256 * half:BF * h + 256 * half + 256]
                            ins = pe.matmul(PS[:, 6 + h, 256 * half:256 * half + 256], w, y, start=True, stop=True)
                            if half == 0:
                                settle(ins)
                        ins.then_inc(comb_mm.s, 1)
                    assert not owed


_INS = ["x_prompt", "x_sample", "cache_mla_ckv", "cache_mla_kpe", "cache_gqa_k", "cache_gqa_v", "cache_diff_k",
        "cache_diff_v", "c", "c_ctx", "w_ada", "b_ada", "norm1", "norm2", "w_in", "mla_q_norm", "mla_kv_norm",
        "mla_w_uq", "mla_w_uk", "mla_w_uv", "gqa_q_norm", "gqa_k_norm", "diff_lam_q1", "diff_lam_k1",
        "diff_lam_q2", "diff_lam_k2", "diff_subln", "w_br_mla", "w_br_gqa", "w_br_diff", "w_out", "w_router",
        "w_gate", "w_up", "w_down", "final_norm"]
_OUTS = [("y_prompt", (1, 128, 1024)), ("y_sample", (1, 256, 1024)), ("new_ckv", (1, 2, 128, 256)),
         ("new_kpe", (1, 2, 128, 32)), ("new_gk", (1, 2, 128, 2, 64)), ("new_gv", (1, 2, 128, 2, 64)),
         ("new_dk", (1, 2, 128, 4, 128)), ("new_dv", (1, 2, 128, 4, 128))]


def kernel(**inputs):
    import concourse.bacc as bacc
    from concourse.bass_utils import run_bass_kernel_spmd

    nc = bacc.Bacc("TRN2", target_bir_lowering=False, num_devices=1)
    arrays, args = {}, {}
    for name in _INS:
        x = np.ascontiguousarray(inputs[name])
        arrays[f"in_{name}"] = x
        args[name] = nc.dram_tensor(f"in_{name}", x.shape, mybir.dt.from_np(x.dtype), kind="ExternalInput").ap()
    arrays["in_constants"] = constants()
    args["constants"] = nc.dram_tensor("in_constants", (P, C_W), F32, kind="ExternalInput").ap()
    for name, shape in _OUTS:
        args[name] = nc.dram_tensor(f"out_{name}", shape, F32, kind="ExternalOutput").ap()
    backbone(nc, args)
    r = run_bass_kernel_spmd(nc, [arrays], core_ids=[0])
    return tuple(r.results[0][f"out_{name}"] for name, _ in _OUTS)
```

```python
from contextlib import ExitStack
import math

import numpy as np
import concourse.bass as bass
from concourse import mybir

F32 = mybir.dt.float32
ALU = mybir.AluOpType
ACT = mybir.ActivationFunctionType
AX = mybir.AxisListType.X

P = 128
D = 1024
KC = D // P
DEPTH = 2
NT = 3
TOK = NT * P
NKEY = 4 * P
EPS = 1e-6
QR, KVR, ROPE, NOPE = 384, 256, 32, 64
QD = NOPE + ROPE
NE, FF = 16, 1024
CAP_S, CAP_P = 32, 16
CAP = CAP_S + CAP_P
XW = 64
ATT = 2976
SLOTS = 8
SLOT = 2048
UNITS = 256
ATT_UNITS = 64
GE = 4
NG = NE // GE
GROUP_UNITS = 12 * GE
USES = UNITS // SLOTS
BF = 512

ZA_W, ZG_W, ZD_W = 672, 768, 1536
Z_KV, Z_PE = QR, QR + KVR
G_K, G_V = 512, 640
D_K, D_V = 512, 1024

C_ID = 0
C_ONE = C_ID + P
C_COS = C_ONE + P
C_IOTA = C_COS + 2 * 192
C_LAM = C_IOTA + CAP_S
C_W = C_LAM + 2 * DEPTH


def lam_init(layer):
    return 0.8 - 0.6 * math.exp(-0.3 * layer)


def constants():
    c = np.zeros((P, C_W), np.float32)
    c[:, C_ID:C_ID + P] = np.eye(P)
    c[:, C_ONE:C_ONE + P] = 1.0
    token = np.arange(2 * P)
    axes = ((token // 64).astype(np.float32), (token % 64).astype(np.float32))
    at = C_COS
    tables = []
    for width in (64, 32):
        half = width // 4
        freqs = (np.float32(10000.0) ** (-np.arange(half, dtype=np.float32) / np.float32(half))).astype(np.float32)
        cos, sin = [], []
        for pos in axes:
            ang = (pos[:, None] * freqs[None, :]).astype(np.float32)
            co, si = np.cos(ang), np.sin(ang)
            cos += [co, co]
            sin += [-si, si]
        tables += [np.concatenate(cos, 1), np.concatenate(sin, 1)]
    table = np.concatenate(tables, 1).astype(np.float32)
    for t in range(2):
        c[:, at + 192 * t:at + 192 * (t + 1)] = table[t * P:(t + 1) * P]
    c[:, C_IOTA:C_IOTA + CAP_S] = np.arange(1, CAP_S + 1)
    for layer in range(DEPTH):
        c[:, C_LAM + 2 * layer] = lam_init(layer)
        c[:, C_LAM + 2 * layer + 1] = 1.0 - lam_init(layer)
    return c


class Signal:

    def __init__(self, handle, per, base):
        self.s, self.per, self.base = handle, per, base

    def at(self, layer, n):
        return layer * self.per + (n + self.base)

    def in_group(self, layer, g, n):
        return layer * self.per + g * (self.per // NG) + (n + self.base)


JOBS = [("mla", h) for h in range(8)] + [("gqa", i) for i in range(4)] + [("diff", h) for h in range(4)]
NJ = len(JOBS)
MAPS = []
OUTS = []
for _j, (_kind, _) in enumerate(JOBS):
    MAPS += [(_j, m) for m in range(1 if _kind == "mla" else 2)]
    OUTS += [(_j, m) for m in range(2 if _kind == "gqa" else 1)]
MAP_AT = {jm: n for n, jm in enumerate(MAPS)}
OUT_AT = {jm: n for n, jm in enumerate(OUTS)}
SCALE = {"mla": QD ** -0.5, "gqa": 64 ** -0.5, "diff": 64 ** -0.5}

FILL = [[] for _ in range(NJ + 1)]
for _t in range(1, NT):
    FILL[_t - 1] += [("c1", _t, h) for h in range(2)]
FILL[4].append(("ada", 1))
FILL[5].append(("adat", 1))
FILL[6].append(("ada", 2))
FILL[7].append(("adat", 2))
for _c in range(KC):
    FILL[(2, 3, 5, 7)[_c // 2]].append(("gate0", _c))
for _n in range(12):
    FILL[8 + _n // 6].append(("c2", _n))
for _c in range(KC):
    FILL[10 + _c // 4].append(("br0", _c))
for _c in range(KC):
    FILL[12 + _c // 2] += [("gate1", _c), ("br1", _c)]

USERS = [("c0", t, h) for t in range(NT) for h in range(2)]
USERS += [("c1", 0, h) for h in range(2)]
USERS += [("q", t, h) for t in range(NT) for h in range(2)] + [("v", t) for t in range(4)]
for _i in range(NJ + 1):
    if _i >= 1:
        USERS.append(("pv", _i - 1))
    USERS += FILL[_i]
USERS += [("gate2", c) for c in range(KC)] + [("br2", c) for c in range(KC)]
USERS += [("out", t, h) for t in range(NT) for h in range(2)]
USER_AT = {u: n for n, u in enumerate(USERS)}
BY_DVE = {"ada", "adat", "v", "br0", "br1", "br2", "out"}


def evacuated(n):
    dve = USERS[n][0] in BY_DVE
    return sum((u[0] in BY_DVE) == dve for u in USERS[:n + 1])


N_DVE_USERS = sum(u[0] in BY_DVE for u in USERS)
N_ACT_USERS = len(USERS) - N_DVE_USERS

PLAN = [("ada", 0, k) for k in range(KC)]
PLAN += [("c0", u) for u in range(4)] + [("c1", u) for u in range(4)] + [("uq", 0), ("uq", 1)]
PLAN += [("gate0", 0), ("gate0", 1)] + [("ada", 1, k) for k in range(KC)]
PLAN += [("gate0", 2)] + [("ada", 2, k) for k in range(KC)] + [("gate0", 3)]
PLAN += [("c2", u) for u in range(8)] + [("br0", 0), ("br0", 1)]
PLAN += [("gate1", 0), ("br1", 0), ("gate1", 1), ("gate1", 2), ("br1", 1), ("gate1", 3)]
PLAN += [("gate2", u) for u in range(4)] + [("br2", 0), ("br2", 1)] + [("wout", u) for u in range(4)]
assert len(PLAN) == ATT_UNITS
UNIT = {u: n for n, u in enumerate(PLAN)}

DVE_LINKS = 101
POOL_LINKS = 24


def backbone(nc, a):
    ctx = ExitStack()
    with ctx:
        arena = ctx.enter_context(nc.sbuf_tensor("arena", [P, 36800], F32))
        ring = ctx.enter_context(nc.sbuf_tensor("ring", [P, SLOTS, SLOT], F32))
        PS = ctx.enter_context(nc.psum_tensor("banks", [P, 8, BF], F32))

        def at(start, *shape):
            n = int(np.prod(shape))
            v = arena[:, start:start + n]
            names = "abcd"[:len(shape)]
            if len(shape) == 1:
                return v
            return v.rearrange(f"p ({' '.join(names)}) -> p {' '.join(names)}",
                               **{x: s for x, s in zip(names, shape)})

        hT = at(0, KC, TOK)
        XN = at(3072, NT, D)
        MG = at(3072, KC, TOK)
        ZA = at(6144, NT, ZA_W)
        ZG = at(8160, NT, ZG_W)
        QQ = at(10464, NT, 768)
        QAB = at(10464, 2, 2, TOK)
        VM = at(12768, 4, 512)
        CKT = at(14816, 2, NKEY)
        UKV = at(15840, 2, 2, 512)
        ZD = at(12768, NT, ZD_W)
        QM = at(17888, 2, TOK)
        SG1 = at(17888, 2, TOK)
        KT = at(18656, 2, NKEY)
        PB = at(19680, 2, 896)
        CQT = at(19680, 3, TOK)
        PT = at(21472, 2, 896)
        OT0 = at(23264, 4, TOK)
        OT1 = at(6144, 4, TOK)
        OT2 = at(8160, 4, TOK)
        XN2 = at(9696, NT, D)
        SQD = at(19680, 4, TOK)
        RSD = at(21472, 4, TOK)
        RT1 = at(24800, 640)
        RT2 = at(25440, 640)
        TMP = at(24800, 2, BF)
        SQG = at(3072, NT, 640)
        G1 = at(12768, 2, D)
        SG2 = at(14816, KC, TOK)
        CTX_CKV = at(26080, KVR)
        CTX_KPE = at(26336, ROPE)
        CTX_GK = at(26368, 128)
        CTX_GV = at(26496, 128)
        CTX_DK = at(26624, 512)
        CTX_DV = at(27136, 512)
        YS = at(0, 2, D)
        CTMP = at(2048, 2, BF)
        SGE = at(3072, BF)
        AC = at(3584, BF)
        AT = at(4096, 4, P)
        DD = at(6144, NT, NE, CAP_S)
        DG = at(7680, NT, NE, CAP_S)
        DGT = at(4608, NG, NT * P)
        DGB = at(9216, NT * P)
        G2 = at(12768, 2, D)
        XB = at(14816, 2, KC, XW)
        AFT = at(24192, TOK)[0:NE]
        WK = at(24576, TOK)[0:NE]
        MK = at(24960, TOK)[0:NE]
        SN = at(25344, TOK)[0:NE]
        XE = at(17888, KC, NE, CAP)
        AFF = at(24032, NT, NE)
        POS = at(24080, NT, NE)
        LG = at(24128, NT, NE)
        M8 = at(24176, 8)[0:NE]
        X = at(27648, NT, D)
        MODR = at(30720, 1536)
        BR = at(32256, 1536)
        MODC = at(33792, 2, 48)
        AA = at(33888, 2, 2, KC)
        CST = at(33920, C_W)
        o = 33920 + C_W
        GNQ = at(o, QR)
        GNK = at(o + 384, KVR)
        GGQ = at(o + 640, 64)
        GGK = at(o + 704, 64)
        LAMV = at(o + 768, 4, 64)
        NR = at(o + 1024, P)[0:16]
        NCOL = at(o + 1152, 2, KC)
        SUB = at(o + 1168, 1)
        WR = at(o + 1172, KC, NE)
        SC = at(o + 1300, KC, 2)
        CR = NR
        SIGC = at(o + 1316, 16)
        ST = at(o + 1332, 3)
        RS = at(o + 1336, 3)
        ST2 = at(o + 1340, 6)
        R2 = at(o + 1346, 6)
        STG = at(o + 1352, 30)
        RG = at(o + 1382, 30)
        MX = at(o + 1412, 2, 3)
        NB = at(o + 1418, 2, 3)
        SM = at(o + 1424, 2, 3)
        RC = at(o + 1430, 2, 3)
        LP = at(o + 1436, 2, 64)
        LE = at(o + 1564, 2)
        LAM = at(o + 1566, 1)
        LIC = at(o + 1567, 2)
        WARM = at(o + 1633, 1)
        KPR = at(o + 1569, 2, ROPE)
        assert o + 1634 <= 36800
        IDT = CST[:, C_ID:C_ID + P]
        ONES = CST[:, C_ONE:C_ONE + P]
        IOTA = CST[:, C_IOTA:C_IOTA + CAP_S]
        GSTAT = ST2

        def sem(name, per=0, base=0):
            return Signal(ctx.enter_context(nc.semaphore(name)), per, base)

        filled = [sem(f"filled{i}", 16 * USES) for i in range(SLOTS)]
        used = [sem(f"used{i}", USES, 1) for i in range(SLOTS)]
        const_in, cond_in, x_in = sem("const_in"), sem("cond_in"), sem("x_in")
        cond_t, cond_sig, cond_ok = sem("cond_t"), sem("cond_sig"), sem("cond_ok")
        early_in = sem("early_in", 6 * 16)
        late_in = sem("late_in", 18 * 16)
        ada_mm = sem("ada_mm", 1)
        mod_row, mod_col = sem("mod_row", 1), sem("mod_col", 1)
        mod_t = sem("mod_t", 2)
        ncol_ok, aa_ok = sem("ncol_ok", 1), sem("aa_ok", 2)
        ss_ok, root_ok, ms_ok, xn_ok = sem("ss_ok", 1), sem("root_ok", 1), sem("ms_ok", 1), sem("xn_ok", NT)
        ss_t, root_t, ms_t, xn_t = sem("ss_t", NT), sem("root_t", NT), sem("ms_t", NT), sem("xn_t", NT)
        h2_mm, h2_act, h2_dve = sem("h2_mm", 2), sem("h2_act", 2), sem("h2_dve", 2)
        ht_mm, ht_act, ht_dve = sem("ht_mm", 8), sem("ht_act", 4), sem("ht_dve", 4)
        user_mm = sem("user_mm", len(USERS))
        user_act, user_dve = sem("user_act", N_ACT_USERS), sem("user_dve", N_DVE_USERS)
        sq2_ok, ms2_ok, root2_ok, za_ok = sem("sq2_ok", 1), sem("ms2_ok", 1), sem("root2_ok", 1), sem("za_ok", 1)
        kpe_ok, qrope_ok = sem("kpe_ok", 1), sem("qrope_ok", 1)
        tr_mm, tr_act, tr_dve = sem("tr_mm", 3), sem("tr_act", 1), sem("tr_dve", 2)
        prep_mm, prep_act, prep_dve = sem("prep_mm", NJ), sem("prep_act", NJ), sem("prep_dve", NJ)
        score_mm, max_ok, exp_ok = sem("score_mm", len(MAPS)), sem("max_ok", len(MAPS)), sem("exp_ok", len(MAPS))
        prob_ok = sem("prob_ok", len(OUTS))
        pt_mm, pt_act, pt_dve = sem("pt_mm", len(OUTS)), sem("pt_act", len(OUTS)), sem("pt_dve", len(OUTS))
        sqg_ok, msg_ok, rootg_ok, rg_ok, gq_ok = (sem("sqg_ok", 1), sem("msg_ok", 1), sem("rootg_ok", 1),
                                                  sem("rg_ok", 1), sem("gq_ok", 1))
        zero_ok, dq_ok = sem("zero_ok", 1), sem("dq_ok", 1)
        lamp_ok, lame_ok = sem("lamp_ok", 1), sem("lame_ok", 1)
        stored_a, stored_g, stored_d = sem("stored_a", 32), sem("stored_g", 32), sem("stored_d", 32)
        sqd_ok, sqd_mm, msd_ok, rootd_ok, ot2_ok = (sem("sqd_ok", 1), sem("sqd_mm", 1), sem("msd_ok", 1),
                                                    sem("rootd_ok", 1), sem("ot2_ok", 1))
        gb_mm, gb_ok = sem("gb_mm", 2), sem("gb_ok", 2)
        x1_ok, xg_ok, silu_ok = sem("x1_ok", NT), sem("xg_ok", NG, 1), sem("silu_ok", NE)
        router_mm, logit_ok, aexp_ok, aff_ok = (sem("router_mm", 1, 1), sem("logit_ok", 1), sem("aexp_ok", 1),
                                                sem("aff_ok", 1))
        aff_t, pos_ok, pos_t, disp_ok = sem("aff_t", 1), sem("pos_ok", 1), sem("pos_t", 1), sem("disp_ok", 1)
        gated_ok = sem("gated_ok", 1)
        gather_mm, gather_act, gather_dve = sem("gather_mm", 16), sem("gather_act", 8), sem("gather_dve", 8)
        dgt_mm, dgt_ok = sem("dgt_mm", 1), sem("dgt_ok", 1)
        xb_ok = sem("xb_ok", NE)
        gu_mm = sem("gu_mm", 2 * NE)
        sig_ok, ac_ok, at_mm, at_ok = sem("sig_ok", NE), sem("ac_ok", NE, 1), sem("at_mm", NE, 1), sem("at_ok", NE)
        y_mm, y_ok = sem("y_mm", NE), sem("y_ok", NE, 1)
        comb_mm, comb_ok, dgb_ok = sem("comb_mm", 6 * NG, 1), sem("comb_ok", 6 * NG, 1), sem("dgb_ok", NG)
        dve_chain, pool_chain = sem("dve_chain", DVE_LINKS), sem("pool_chain", POOL_LINKS)
        fn_in, y_out = sem("fn_in"), sem("y_out")
        fin_ss, fin_ms, fin_root, fin_ok = sem("fin_ss"), sem("fin_ms"), sem("fin_root"), sem("fin_ok")

        def h2_pieces(n):
            for c in range(KC):
                for t in (0, 1) if n == 0 else (2,):
                    if n == 0:
                        bank, col = c // 2, 256 * (c % 2) + P * t
                    else:
                        bank, col = 4 + c // 2 % 2, 256 * (c // 4) + P * (c % 2)
                    yield c, min(t, 1), P * t, P * t + P, PS[:, bank, col:col + P]

        def h2_dve_chunk(c):
            return c // 2 % 2 == 1

        passed = sem("passed")

        def apart(eng):
            eng.sem_inc(passed.s, 1)

        block = ctx.enter_context(nc.Block())

        @block.sync
        def _(sp):
            sp.dma_start(CST, a["constants"]).then_inc(const_in.s, 16)
            sp.dma_start(CR[0:8], a["c_ctx"].rearrange("(k p) -> k p", p=P)).then_inc(cond_in.s, 16)
            sp.dma_start(CR[8:16], a["c"].rearrange("b (k p) -> (b k) p", p=P)).then_inc(cond_in.s, 16)
            sp.dma_start(X[:, 0], a["x_prompt"].rearrange("b p d -> (b p) d")).then_inc(x_in.s, 16)
            sp.dma_start(X[:, 1:3], a["x_sample"].rearrange("b (t p) d -> p (b t) d", p=P)).then_inc(x_in.s, 16)
            w_ada = a["w_ada"].rearrange("l (k p) (i j n) -> l k i p j n", p=P, j=4, i=3)
            w_in = a["w_in"].rearrange("l (k p) n -> l p k n", p=P)
            w_uq = a["mla_w_uq"].rearrange("l (k p) n -> l p k n", p=P)
            w_br = [a[f"w_br_{n}"].rearrange("l (k p) n -> l p k n", p=P) for n in ("mla", "gqa", "diff")]
            w_out = a["w_out"].rearrange("l (k p) n -> l p k n", p=P)
            w_exp = [a[n].rearrange("l e (k p) n -> l e p k n", p=P) for n in ("w_gate", "w_up", "w_down")]

            def source(l, unit):
                kind, u = unit[0], unit[1]
                if kind == "ada":
                    return w_ada[l, unit[2], u]
                if kind == "c0":
                    return w_in[l, :, 2 * u:2 * u + 2, 0:ZA_W]
                if kind == "c1":
                    return w_in[l, :, 2 * u:2 * u + 2, ZA_W:ZA_W + ZG_W]
                if kind == "c2":
                    c = ZA_W + ZG_W + 768 * (u // 4)
                    return w_in[l, :, 2 * (u % 4):2 * (u % 4) + 2, c:c + 768]
                if kind == "uq":
                    return w_uq[l, :, 2 * u:min(2 * u + 2, 3), :]
                if kind.startswith("gate"):
                    c = ATT + D * int(kind[4]) + 256 * u
                    return w_in[l, :, :, c:c + 256]
                if kind.startswith("br"):
                    return w_br[int(kind[2])][l, :, :, 512 * u:512 * u + 512]
                return w_out[l, :, 2 * u:2 * u + 2, :]

            with sp.Fori(0, DEPTH) as l:
                for n, unit in enumerate(PLAN):
                    src = source(l, unit)
                    _, parts, cols = src.shape
                    dst = ring[:, n % SLOTS, 0:parts * cols].rearrange("p (k n) -> p k n", k=parts)
                    sp.wait_ge(used[n % SLOTS].s, used[n % SLOTS].at(l, n // SLOTS))
                    sp.dma_start(dst, src).then_inc(filled[n % SLOTS].s, 16)
                with sp.Fori(0, NG) as g:
                    for e in range(GE):
                        for m in range(3):
                            for u in range(4):
                                n = 12 * e + 4 * m + u
                                src = w_exp[m][l, bass.ds(g * GE + e, 1), :, 2 * u:2 * u + 2, :]
                                sp.wait_ge(used[n % SLOTS].s,
                                           l * USES + g * (GROUP_UNITS // SLOTS) + ((ATT_UNITS + n) // SLOTS + 1))
                                sp.dma_start(ring[:, n % SLOTS, :].rearrange("p (k n) -> p k n", k=2),
                                             src.rearrange("e p k n -> (e p) k n")).then_inc(filled[n % SLOTS].s, 16)
            sp.wait_ge(xg_ok.s, DEPTH * NG + 1)
            sp.dma_start(at(0, D), a["final_norm"].rearrange("(o n) -> o n", o=1).to_broadcast([P, D]))\
              .then_inc(fn_in.s, 16)
            sp.wait_ge(fin_ok.s, NT)
            sp.dma_start(a["y_prompt"].rearrange("b p d -> (b p) d"), XN[:, 0]).then_inc(y_out.s, 16)
            sp.dma_start(a["y_sample"].rearrange("b (t p) d -> p (b t) d", p=P), XN[:, 1:3]).then_inc(y_out.s, 16)
            sp.wait_ge(y_out.s, 32)
            sp.wait_ge(stored_a.s, 32 * DEPTH)
            sp.wait_ge(stored_g.s, 32 * DEPTH)
            sp.wait_ge(stored_d.s, 32 * DEPTH)

        @block.gpsimd
        def _(pool):
            links = [0]

            def link(ins, l):
                links[0] += 1
                ins.then_inc(pool_chain.s, 1)
                pool.wait_ge(pool_chain.s, pool_chain.at(l, links[0]))

            def rotate(l, z, heads, width, t):
                c0 = C_COS + 192 * t + (0 if width == 64 else 128)
                half = width // 4
                cos = CST[:, c0:c0 + width].rearrange("p (o n) -> p o n", o=1).to_broadcast([P, heads, width])
                sin = CST[:, c0 + width:c0 + 2 * width].rearrange("p (x h n) -> p x h n", x=2, h=2)
                t1 = RT1[:, 0:heads * width].rearrange("p (a n) -> p a n", a=heads)
                t2 = RT2[:, 0:heads * width].rearrange("p (a n) -> p a n", a=heads)
                t2v = RT2[:, 0:heads * width].rearrange("p (a x h n) -> p a x h n", a=heads, x=2, h=2)
                pool.tensor_tensor(t1, z, cos, ALU.mult)
                for h in range(2):
                    for x in range(2):
                        src = z[:, :, (2 * x + 1 - h) * half:(2 * x + 2 - h) * half]
                        sx = sin[:, x, h, :].rearrange("p (o n) -> p o n", o=1).to_broadcast([P, heads, half])
                        ins = pool.tensor_tensor(t2v[:, :, x, h, :], src, sx, ALU.mult)
                link(ins, l)
                return pool.tensor_tensor(z, t1, t2, ALU.add)

            def row(ap, n):
                return ap.rearrange("(o n) -> o n", o=1).to_broadcast([P, n])

            pool.wait_ge(const_in.s, 16)
            pool.wait_ge(cond_t.s, 1)
            with pool.Fori(0, DEPTH) as l:
                links[0] = 0
                pool.wait_ge(router_mm.s, router_mm.at(l, 0))
                b_ada = a["b_ada"].rearrange("l (i j n) -> l j i n", i=3, j=4)
                for j in range(4):
                    pool.dma_start(BR[32 * j:32 * j + 2].rearrange("p (i n) -> p i n", i=3),
                                   b_ada[l, j].rearrange("(o i) n -> o i n", o=1).to_broadcast([2, 3, BF]))\
                        .then_inc(early_in.s, 16)
                pool.dma_start(NR[0:8], a["norm1"].rearrange("l (k p) -> l k p", p=P)[l]).then_inc(early_in.s, 16)
                pool.dma_start(NR[8:16], a["norm2"].rearrange("l (k p) -> l k p", p=P)[l]).then_inc(early_in.s, 16)
                for dst, name, n in ((GNQ, "mla_q_norm", QR), (GNK, "mla_kv_norm", KVR), (GGQ, "gqa_q_norm", 64),
                                     (GGK, "gqa_k_norm", 64), (LAMV[:, 0], "diff_lam_q1", 64),
                                     (LAMV[:, 1], "diff_lam_q2", 64), (LAMV[:, 2], "diff_lam_k1", 64),
                                     (LAMV[:, 3], "diff_lam_k2", 64)):
                    pool.dma_start(dst, row(a[name][l], n)).then_inc(late_in.s, 16)
                pool.dma_start(SUB, a["diff_subln"][l].rearrange("(p o) -> p o", o=1)).then_inc(late_in.s, 16)
                pool.dma_start(WR, a["w_router"].rearrange("l (k p) e -> l p k e", p=P)[l]).then_inc(late_in.s, 16)
                for m, name in enumerate(("mla_w_uk", "mla_w_uv")):
                    pool.dma_start(UKV[:, m], a[name].rearrange("l (k p) h d -> l p k (h d)", p=P)[l])\
                        .then_inc(late_in.s, 16)
                for dst, name, form in ((CTX_CKV, "cache_mla_ckv", "b l p r -> l (b p) r"),
                                        (CTX_KPE, "cache_mla_kpe", "b l p r -> l (b p) r"),
                                        (CTX_GK, "cache_gqa_k", "b l p h d -> l (b p) (h d)"),
                                        (CTX_GV, "cache_gqa_v", "b l p h d -> l (b p) (h d)"),
                                        (CTX_DK, "cache_diff_k", "b l p h d -> l (b p) (h d)"),
                                        (CTX_DV, "cache_diff_v", "b l p h d -> l (b p) (h d)")):
                    pool.dma_start(dst, a[name].rearrange(form)[l]).then_inc(late_in.s, 16)
                pool.wait_ge(user_act.s, user_act.at(l, evacuated(USER_AT["c0", 2, 1])))
                for t in range(2):
                    apart(pool)
                    link(pool.tensor_copy(KPR[:, t:t + 1], ZA[:, 1 + t:2 + t, Z_PE:Z_PE + ROPE]), l)
                    ins = rotate(l, KPR[:, t:t + 1], 1, ROPE, t)
                    if t == 0:
                        link(ins, l)
                    else:
                        ins.then_inc(kpe_ok.s, 1)
                pool.wait_ge(za_ok.s, za_ok.at(l, 1))
                apart(pool)
                pool.dma_start(a["new_ckv"].rearrange("b l p r -> l (b p) r")[l],
                               ZA[:, 0, Z_KV:Z_KV + KVR]).then_inc(stored_a.s, 16)
                pool.dma_start(a["new_kpe"].rearrange("b l p r -> l (b p) r")[l],
                               ZA[:, 0, Z_PE:Z_PE + ROPE]).then_inc(stored_a.s, 16)
                pool.wait_ge(user_act.s, user_act.at(l, evacuated(USER_AT["q", 2, 1])))
                pool.wait_ge(kpe_ok.s, kpe_ok.at(l, 1))
                for t in range(2):
                    z = QQ[:, 1 + t].rearrange("p (h d) -> p h d", h=8)[:, :, NOPE:QD]
                    ins = rotate(l, z, 8, ROPE, t)
                    if t == 0:
                        link(ins, l)
                    else:
                        ins.then_inc(qrope_ok.s, 1)
                pool.wait_ge(rg_ok.s, rg_ok.at(l, 1))
                pool.wait_ge(qrope_ok.s, qrope_ok.at(l, 1))
                for t in range(NT):
                    z = ZG[:, t, 0:640].rearrange("p (h d) -> p h d", h=10)
                    rg = RG[:, 10 * t:10 * t + 10].rearrange("p (h o) -> p h o", o=1).to_broadcast([P, 10, 64])
                    link(pool.tensor_tensor(z, z, rg, ALU.mult), l)
                    pool.tensor_tensor(z[:, 0:8], z[:, 0:8],
                                       GGQ.rearrange("p (o n) -> p o n", o=1).to_broadcast([P, 8, 64]), ALU.mult)
                    link(pool.tensor_tensor(z[:, 8:10], z[:, 8:10],
                                            GGK.rearrange("p (o n) -> p o n", o=1).to_broadcast([P, 2, 64]),
                                            ALU.mult), l)
                    if t >= 1:
                        ins = rotate(l, z, 10, 64, t - 1)
                        if t == 1:
                            link(ins, l)
                        else:
                            ins.then_inc(gq_ok.s, 1)
                pool.wait_ge(gq_ok.s, gq_ok.at(l, 1))
                apart(pool)
                pool.dma_start(a["new_gk"].rearrange("b l p h d -> l (b p) (h d)")[l],
                               ZG[:, 0, G_K:G_K + 128]).then_inc(stored_g.s, 16)
                pool.dma_start(a["new_gv"].rearrange("b l p h d -> l (b p) (h d)")[l],
                               ZG[:, 0, G_V:G_V + 128]).then_inc(stored_g.s, 16)
                pool.wait_ge(prep_mm.s, prep_mm.at(l, 8))
                apart(pool)
                pool.memset(QAB[64:128, :, 0], 0.0)
                pool.memset(QAB[0:64, :, 1], 0.0).then_inc(zero_ok.s, 1)
                pool.wait_ge(user_act.s, user_act.at(l, evacuated(USER_AT["c2", 11])))
                for t in range(2):
                    for part in range(2):
                        z = ZD[:, 1 + t, 512 * part:512 * part + 512].rearrange("p (h d) -> p h d", h=8)
                        ins = rotate(l, z, 8, 64, t)
                        if (t, part) != (1, 1):
                            link(ins, l)
                        else:
                            ins.then_inc(dq_ok.s, 1)
                pool.dma_start(a["new_dk"].rearrange("b l p h d -> l (b p) (h d)")[l],
                               ZD[:, 0, D_K:D_K + 512]).then_inc(stored_d.s, 16)
                pool.dma_start(a["new_dv"].rearrange("b l p h d -> l (b p) (h d)")[l],
                               ZD[:, 0, D_V:D_V + 512]).then_inc(stored_d.s, 16)
                assert links[0] == POOL_LINKS, ("POOL_LINKS", links[0])

        @block.scalar
        def _(act):
            def norm_root(l):
                for t in range(NT):
                    ins = nc.scalar.activation(XN[:, t], X[:, t], ACT.Square, accum_out=ST[:, t:t + 1])
                ins.then_inc(ss_ok.s, 1)
                act.wait_ge(ms_ok.s, ms_ok.at(l, 1))
                nc.scalar.activation(RS, RS, ACT.Sqrt).then_inc(root_ok.s, 1)

            def ht_even(l):
                for c in range(0, KC, 2):
                    act.wait_ge(ht_mm.s, ht_mm.at(l, c + 1))
                    ps = PS[:, 4 + c % 4]
                    for s, lo, hi in ((0, 0, P), (1, P, TOK)):
                        ins = nc.scalar.activation(hT[:, c, lo:hi], ps[:, lo:hi], ACT.Identity,
                                                   scale=AA[:, 0, s, c:c + 1], bias=MODC[:, s, c:c + 1])
                    ins.then_inc(ht_act.s, 1)

            def h2_out(l, n):
                act.wait_ge(h2_mm.s, h2_mm.at(l, n + 1))
                for c, s, lo, hi, ps in h2_pieces(n):
                    if not h2_dve_chunk(c):
                        ins = nc.scalar.activation(hT[:, c, lo:hi], ps, ACT.Identity, scale=AA[:, 1, s, c:c + 1],
                                                   bias=MODC[:, s, 24 + c:25 + c])
                ins.then_inc(h2_act.s, 1)

            def user(l, key, write):
                n = USER_AT[key]
                act.wait_ge(user_mm.s, user_mm.at(l, n + 1))
                write(PS[:, 6 + n % 2]).then_inc(user_act.s, 1)

            def exps(l, j):
                kind, _ = JOBS[j]
                for m in range(1 if kind == "mla" else 2):
                    n = MAP_AT[j, m]
                    act.wait_ge(max_ok.s, max_ok.at(l, n + 1))
                    if n >= 2:
                        before = MAPS[n - 2]
                        act.wait_ge(pt_mm.s, pt_mm.at(l, OUT_AT.get(before, OUT_AT[before[0], 0]) + 1))
                    b = n % 2
                    for r, (lo, hi, bank, c) in enumerate(((0, 384, 0, 0), (384, 512, 0, 384), (512, 896, 1, 0))):
                        ins = nc.scalar.activation(PB[:, b, lo:hi], PS[:, 2 * m + bank, c:c + hi - lo], ACT.Exp,
                                                   scale=SCALE[kind], bias=NB[:, b, r:r + 1],
                                                   accum_out=SM[:, b, r:r + 1])
                    ins.then_inc(exp_ok.s, 1)

            def prep(l, j):
                kind, i = JOBS[j]
                act.wait_ge(prep_mm.s, prep_mm.at(l, j + 1))
                if kind == "mla":
                    ins = nc.scalar.copy(QM[0:QD, j % 2], PS[0:QD, 5, 0:TOK])
                else:
                    ins = nc.scalar.copy(QAB[0:64, j % 2, 0], PS[0:64, 5, 0:TOK])
                ins.then_inc(prep_act.s, 1)

            def values(l, j):
                kind, i = JOBS[j]
                n = USER_AT["pv", j]
                ps = PS[:, 6 + n % 2]
                act.wait_ge(user_mm.s, user_mm.at(l, n + 1))
                if kind == "mla":
                    r = 64 * (i % 2)
                    ins = nc.scalar.copy(OT0[r:r + 64, i // 2], ps[r:r + 64, 0:TOK])
                elif kind == "gqa":
                    if i == 0:
                        act.wait_ge(stored_a.s, stored_a.at(l, 32))
                    ins = nc.scalar.copy(OT1[:, i], ps[:, 0:TOK])
                else:
                    if i == 0:
                        act.wait_ge(stored_g.s, stored_g.at(l, 32))
                    ins = nc.scalar.copy(OT2[:, i], ps[:, 0:TOK])
                ins.then_inc(user_act.s, 1)

            def fill(l, key):
                kind = key[0]
                if kind == "c1":
                    user(l, key, lambda ps: nc.scalar.copy(ZG[:, key[1], 384 * key[2]:384 * key[2] + 384],
                                                           ps[:, 0:384]))
                elif kind == "c2":
                    half, t, q = key[1] // 6, key[1] % 6 // 2, key[1] % 2
                    c = 768 * half + 384 * q
                    user(l, key, lambda ps: nc.scalar.copy(ZD[:, t, c:c + 384], ps[:, 0:384]))
                elif kind == "gate0":
                    user(l, key, lambda ps: nc.scalar.activation(MG[:, key[1]], ps[:, 0:TOK], ACT.Tanh, scale=0.5))
                elif kind == "gate1":
                    if key[1] >= 2:
                        act.wait_ge(user_dve.s, user_dve.at(l, evacuated(USER_AT["br1", key[1] - 2])))
                    user(l, key, lambda ps: nc.scalar.activation(SG1[:, key[1] % 2], ps[:, 0:TOK], ACT.Tanh,
                                                                 scale=0.5))
                elif kind == "gate2":
                    user(l, key, lambda ps: nc.scalar.activation(SG2[:, key[1]], ps[:, 0:TOK], ACT.Tanh, scale=0.5))

            act.sem_inc(y_ok.s, 1)
            act.wait_ge(cond_t.s, 1)
            nc.scalar.activation(SIGC, PS[:, 0, 0:16], ACT.Sigmoid).then_inc(cond_sig.s, 1)
            act.wait_ge(x_in.s, 32)
            with act.Fori(0, DEPTH) as l:
                act.wait_ge(xg_ok.s, xg_ok.at(l, 0))
                norm_root(l)
                act.wait_ge(aa_ok.s, aa_ok.at(l, 1))
                ht_even(l)
                for t in range(NT):
                    for h in range(2):
                        user(l, ("c0", t, h), lambda ps: nc.scalar.copy(ZA[:, t, 336 * h:336 * h + 336],
                                                                        ps[:, 0:336]))
                    act.wait_ge(user_act.s, user_act.at(l, evacuated(USER_AT["c0", t, 1])))
                    nc.scalar.activation(SQG[:, t, 0:QR], ZA[:, t, 0:QR], ACT.Square, accum_out=ST2[:, t:t + 1])
                    ins = nc.scalar.activation(SQG[:, t, QR:640], ZA[:, t, Z_KV:Z_KV + KVR], ACT.Square,
                                               accum_out=ST2[:, 3 + t:4 + t])
                ins.then_inc(sq2_ok.s, 1)
                act.wait_ge(ms2_ok.s, ms2_ok.at(l, 1))
                nc.scalar.activation(R2, R2, ACT.Sqrt).then_inc(root2_ok.s, 1)
                for h in range(2):
                    fill(l, ("c1", 0, h))
                act.wait_ge(tr_mm.s, tr_mm.at(l, 1))
                nc.scalar.copy(CQT, PS[:, 0:3, 0:TOK]).then_inc(tr_act.s, 1)
                for t in range(NT):
                    for h in range(2):
                        user(l, ("q", t, h), lambda ps: nc.scalar.copy(QQ[:, t, 384 * h:384 * h + 384],
                                                                       ps[:, 0:384]))
                act.wait_ge(lamp_ok.s, lamp_ok.at(l, 1))
                nc.scalar.activation(LE, LE, ACT.Exp).then_inc(lame_ok.s, 1)
                prep(l, 0)
                for i in range(NJ + 1):
                    if i < NJ:
                        exps(l, i)
                    if i + 1 < NJ:
                        prep(l, i + 1)
                    if i >= 1:
                        values(l, i - 1)
                    if i == 2:
                        act.wait_ge(msg_ok.s, msg_ok.at(l, 1))
                        nc.scalar.activation(RG, RG, ACT.Sqrt).then_inc(rootg_ok.s, 1)
                    for key in FILL[i]:
                        fill(l, key)
                    if i == 1:
                        act.wait_ge(user_act.s, user_act.at(l, evacuated(USER_AT["c1", 2, 1])))
                        nc.scalar.activation(SQG, ZG[:, :, 0:640], ACT.Square).then_inc(sqg_ok.s, 1)
                    if i < NJ:
                        for m in range(2 if JOBS[i][0] == "gqa" else 1):
                            n = OUT_AT[i, m]
                            act.wait_ge(pt_mm.s, pt_mm.at(l, n + 1))
                            if n >= 2:
                                act.wait_ge(user_mm.s, user_mm.at(l, USER_AT["pv", OUTS[n - 2][0]] + 1))
                            nc.scalar.copy(PT[:, n % 2, 0:384], PS[:, 4, 0:384]).then_inc(pt_act.s, 1)
                act.wait_ge(user_act.s, user_act.at(l, evacuated(USER_AT["pv", NJ - 1])))
                nc.scalar.activation(SQD, OT2, ACT.Square).then_inc(sqd_ok.s, 1)
                act.wait_ge(stored_d.s, stored_d.at(l, 32))
                for c in range(KC):
                    fill(l, ("gate2", c))
                    if c == 2:
                        act.wait_ge(msd_ok.s, msd_ok.at(l, 1))
                        nc.scalar.activation(RSD, RSD, ACT.Sqrt).then_inc(rootd_ok.s, 1)
                act.wait_ge(gb_mm.s, gb_mm.at(l, 1))
                nc.scalar.mul(G1, PS[:, 0:4, :].rearrange("p (s h) n -> p s (h n)", s=2), 0.5).then_inc(gb_ok.s, 1)
                act.wait_ge(aa_ok.s, aa_ok.at(l, 2))
                for t in range(NT):
                    act.wait_ge(x1_ok.s, x1_ok.at(l, t + 1))
                    nc.scalar.activation(XN2[:, t], X[:, t], ACT.Square, accum_out=ST[:, t:t + 1])\
                        .then_inc(ss_t.s, 1)
                    act.wait_ge(ms_t.s, ms_t.at(l, t + 1))
                    nc.scalar.activation(RS[:, t:t + 1], RS[:, t:t + 1], ACT.Sqrt).then_inc(root_t.s, 1)
                    if t == 1:
                        h2_out(l, 0)
                nc.scalar.activation(WARM, AA[:, 1, 0, 0:1], ACT.Exp, scale=0.0)
                h2_out(l, 1)
                act.wait_ge(logit_ok.s, logit_ok.at(l, 1))
                nc.scalar.activation(LG, LG, ACT.Exp).then_inc(aexp_ok.s, 1)
                act.wait_ge(gb_mm.s, gb_mm.at(l, 2))
                nc.scalar.copy(G2, PS[:, 4:8, :].rearrange("p (s h) n -> p s (h n)", s=2)).then_inc(gb_ok.s, 1)
                for c in range(KC):
                    n = 2 * c
                    act.wait_ge(gather_mm.s, gather_mm.at(l, n + 1))
                    nc.scalar.activation(XE[:, c, :, 0:CAP_S],
                                         PS[:, n % 4, :].rearrange("p (e s) -> p e s", e=NE), ACT.Identity,
                                         scale=AA[:, 1, 1, c:c + 1], bias=MODC[:, 1, 24 + c:25 + c])\
                        .then_inc(gather_act.s, 1)
                with act.Fori(0, NG) as g:
                    for e in range(GE):
                        act.wait_ge(gu_mm.s, gu_mm.in_group(l, g, 2 * e + 1))
                        act.wait_ge(ac_ok.s, ac_ok.in_group(l, g, e))
                        nc.scalar.activation(SGE, PS[:, e % 2], ACT.Sigmoid).then_inc(sig_ok.s, 1)
                        act.wait_ge(at_mm.s, at_mm.in_group(l, g, e + 1))
                        nc.scalar.copy(AT, PS[:, 4].rearrange("p (q n) -> p q n", q=4)).then_inc(at_ok.s, 1)
                        act.wait_ge(y_mm.s, y_mm.in_group(l, g, e + 1))
                        if e == 0:
                            act.wait_ge(comb_mm.s, comb_mm.in_group(l, g, 0))
                        for h in range(2):
                            nc.scalar.copy(YS[32 * e:32 * e + 32, 0, BF * h:BF * h + BF],
                                           PS[64 * h:64 * h + 32, 5])
                            ins = nc.scalar.copy(YS[32 * e:32 * e + 16, 1, BF * h:BF * h + BF],
                                                 PS[64 * h + 32:64 * h + 48, 5])
                        ins.then_inc(y_ok.s, 1)
            act.wait_ge(xg_ok.s, DEPTH * NG + 1)
            for t in range(NT):
                ins = nc.scalar.activation(XN[:, t], X[:, t], ACT.Square, accum_out=ST[:, t:t + 1])
            ins.then_inc(fin_ss.s, 1)
            act.wait_ge(fin_ms.s, 1)
            nc.scalar.activation(RS, RS, ACT.Sqrt).then_inc(fin_root.s, 1)

        @block.vector
        def _(dve):
            links = [0]

            def link(ins, l):
                links[0] += 1
                ins.then_inc(dve_chain.s, 1)
                dve.wait_ge(dve_chain.s, dve_chain.at(l, links[0]))

            def norm_rows(l):
                dve.wait_ge(ss_ok.s, ss_ok.at(l, 1))
                nc.vector.tensor_scalar(RS, ST, 1.0 / D, EPS, ALU.mult, ALU.add).then_inc(ms_ok.s, 1)
                dve.wait_ge(root_ok.s, root_ok.at(l, 1))
                link(nc.vector.reciprocal(RS, RS), l)
                for t in range(NT):
                    nc.vector.tensor_scalar(XN[:, t], X[:, t], RS[:, t:t + 1], None, ALU.mult).then_inc(xn_ok.s, 1)

            def ht_odd(l):
                for c in range(1, KC, 2):
                    dve.wait_ge(ht_mm.s, ht_mm.at(l, c + 1))
                    ps = PS[:, 4 + c % 4]
                    for s, lo, hi in ((0, 0, P), (1, P, TOK)):
                        ins = nc.vector.tensor_scalar(hT[:, c, lo:hi], ps[:, lo:hi], AA[:, 0, s, c:c + 1],
                                                      MODC[:, s, c:c + 1], ALU.mult, ALU.add)
                    ins.then_inc(ht_dve.s, 1)

            def h2_out(l, n):
                dve.wait_ge(h2_mm.s, h2_mm.at(l, n + 1))
                for c, s, lo, hi, ps in h2_pieces(n):
                    if h2_dve_chunk(c):
                        ins = nc.vector.tensor_scalar(hT[:, c, lo:hi], ps, AA[:, 1, s, c:c + 1],
                                                      MODC[:, s, 24 + c:25 + c], ALU.mult, ALU.add)
                ins.then_inc(h2_dve.s, 1)

            def modulation(l, key):
                kind, i = key
                n = USER_AT[key]
                dve.wait_ge(user_mm.s, user_mm.at(l, n + 1))
                ins = (mod_rows if kind == "ada" else mod_cols)(PS[:, 6 + n % 2], i)
                ins.then_inc(user_dve.s, 1)
                if key == ("adat", 2):
                    dve.wait_ge(user_dve.s, user_dve.at(l, evacuated(n)))
                    gain_scale(1).then_inc(aa_ok.s, 1)

            def mod_rows(ps, i):
                for j in range(4):
                    r = slice(32 * j, 32 * j + 2)
                    ins = nc.vector.tensor_tensor(MODR[r, BF * i:BF * i + BF], ps[r], BR[r, BF * i:BF * i + BF],
                                                  ALU.add)
                return ins

            def mod_cols(ps, i):
                for s in range(2):
                    src = ps.rearrange("p (q j r) -> p j q r", q=4, j=4)[:, :, :, s]
                    dst = MODC[:, s, 16 * i:16 * i + 16].rearrange("p (j q) -> p j q", j=4)
                    ins = nc.vector.tensor_copy(dst, src)
                return ins

            def gain_scale(n):
                for s in range(2):
                    ins = nc.vector.scalar_tensor_tensor(out=AA[:, n, s], in0=MODC[:, s, 24 * n + 8:24 * n + 16],
                                                         scalar=1.0, in1=NCOL[:, n], op0=ALU.add, op1=ALU.mult)
                return ins

            def maxima(l, j):
                kind, _ = JOBS[j]
                for m in range(1 if kind == "mla" else 2):
                    n = MAP_AT[j, m]
                    b = n % 2
                    dve.wait_ge(score_mm.s, score_mm.at(l, n + 1))
                    if n >= 2:
                        dve.wait_ge(exp_ok.s, exp_ok.at(l, n - 1))
                    for r, (w, bank, c) in enumerate(((384, 0, 0), (128, 0, 384), (384, 1, 0))):
                        ins = nc.vector.reduce_max(MX[:, b, r:r + 1], PS[:, 2 * m + bank, c:c + w], AX)
                    link(ins, l)
                    nc.vector.tensor_scalar(NB[:, b], MX[:, b], -SCALE[kind], None, ALU.mult).then_inc(max_ok.s, 1)

            def prep(l, j):
                kind, i = JOBS[j]
                dve.wait_ge(prep_mm.s, prep_mm.at(l, j + 1))
                if kind == "mla":
                    ins = nc.vector.tensor_copy(KT[0:NOPE, j % 2], PS[0:NOPE, 4])
                else:
                    if kind == "diff":
                        nc.vector.tensor_copy(KT[:, j % 2], PS[:, 4])
                    elif i == 0:
                        for g in range(2):
                            for r in range(2):
                                nc.vector.tensor_copy(KT[64 * r:64 * r + 64, g], PS[64 * g:64 * g + 64, 4])
                    ins = nc.vector.tensor_copy(QAB[64:128, j % 2, 1], PS[64:128, 5, 0:TOK])
                ins.then_inc(prep_dve.s, 1)

            def normalise(l, j):
                kind, _ = JOBS[j]
                rows = ((0, 384), (384, 512), (512, 896))
                for m in range(1 if kind == "mla" else 2):
                    n = MAP_AT[j, m]
                    b = n % 2
                    dve.wait_ge(exp_ok.s, exp_ok.at(l, n + 1))
                    link(nc.vector.reciprocal(RC[:, b], SM[:, b]), l)
                    if kind == "diff" and m == 1:
                        link(nc.vector.tensor_scalar(RC[:, b], RC[:, b], LAM, None, ALU.mult), l)
                        for r, (lo, hi) in enumerate(rows):
                            ins = nc.vector.scalar_tensor_tensor(
                                out=PB[:, 0, lo:hi], in0=PB[:, 1, lo:hi], scalar=RC[:, b, r:r + 1],
                                in1=PB[:, 0, lo:hi], op0=ALU.mult, op1=ALU.add)
                    else:
                        for r, (lo, hi) in enumerate(rows):
                            ins = nc.vector.tensor_scalar(PB[:, b, lo:hi], PB[:, b, lo:hi], RC[:, b, r:r + 1],
                                                          None, ALU.mult)
                    if kind == "diff" and m == 0:
                        link(ins, l)
                    else:
                        ins.then_inc(prob_ok.s, 1)

            def branch(l, key):
                kind, c = key
                n = USER_AT[key]
                dve.wait_ge(user_mm.s, user_mm.at(l, n + 1))
                dve.wait_ge(user_act.s, user_act.at(l, evacuated(USER_AT["gate" + kind[2], c])))
                ps = PS[:, 6 + n % 2, 0:TOK]
                gate = {"br0": MG[:, c], "br1": SG1[:, c % 2], "br2": SG2[:, c]}[kind]
                if kind == "br0":
                    nc.vector.scalar_tensor_tensor(out=gate, in0=gate, scalar=1.0, in1=ps, op0=ALU.add,
                                                   op1=ALU.mult).then_inc(user_dve.s, 1)
                else:
                    link(nc.vector.scalar_tensor_tensor(out=gate, in0=gate, scalar=1.0, in1=ps, op0=ALU.add,
                                                        op1=ALU.mult), l)
                    nc.vector.tensor_tensor(MG[:, c], MG[:, c], gate, ALU.add).then_inc(user_dve.s, 1)

            for free in (xg_ok, ac_ok, comb_ok):
                dve.sem_inc(free.s, 1)
            dve.wait_ge(const_in.s, 16)
            nc.vector.memset(MODR, 0.0)
            dve.wait_ge(cond_sig.s, 1)
            nc.vector.tensor_tensor(SC.rearrange("p k s -> p s k"),
                                    PS[:, 0, 0:16].rearrange("p (s k) -> p s k", s=2),
                                    SIGC.rearrange("p (s k) -> p s k", s=2), ALU.mult).then_inc(cond_ok.s, 1)
            with dve.Fori(0, DEPTH) as l:
                links[0] = 0
                norm_rows(l)
                dve.wait_ge(mod_t.s, mod_t.at(l, 1))
                nc.vector.tensor_copy(NCOL, PS[:, 3, 0:16].rearrange("p (n k) -> p n k", n=2)).then_inc(ncol_ok.s, 1)

                dve.wait_ge(early_in.s, early_in.at(l, 96))
                dve.wait_ge(ada_mm.s, ada_mm.at(l, 1))
                mod_rows(PS[:, 0], 0).then_inc(mod_row.s, 1)
                dve.wait_ge(mod_t.s, mod_t.at(l, 2))
                mod_cols(PS[:, 3], 0).then_inc(mod_col.s, 1)
                dve.wait_ge(mod_col.s, mod_col.at(l, 1))
                gain_scale(0).then_inc(aa_ok.s, 1)
                dve.wait_ge(aa_ok.s, aa_ok.at(l, 1))
                ht_odd(l)
                dve.wait_ge(late_in.s, late_in.at(l, 18 * 16))
                dve.wait_ge(sq2_ok.s, sq2_ok.at(l, 1))
                nc.vector.tensor_scalar(R2[:, 0:3], ST2[:, 0:3], 1.0 / QR, EPS, ALU.mult, ALU.add)
                nc.vector.tensor_scalar(R2[:, 3:6], ST2[:, 3:6], 1.0 / KVR, EPS, ALU.mult, ALU.add)\
                    .then_inc(ms2_ok.s, 1)
                dve.wait_ge(root2_ok.s, root2_ok.at(l, 1))
                link(nc.vector.reciprocal(R2, R2), l)
                for t in range(NT):
                    for col, w, gain, r in ((0, QR, GNQ, t), (Z_KV, KVR, GNK, 3 + t)):
                        z = ZA[:, t, col:col + w]
                        ins = nc.vector.scalar_tensor_tensor(out=z, in0=z, scalar=R2[:, r:r + 1], in1=gain,
                                                             op0=ALU.mult, op1=ALU.mult)
                ins.then_inc(za_ok.s, 1)
                link(nc.vector.tensor_tensor(LP, LAMV[:, 0:2], LAMV[:, 2:4], ALU.mult), l)
                nc.vector.reduce_sum(LE, LP, AX).then_inc(lamp_ok.s, 1)
                nc.vector.tensor_copy(LIC, CST[:, bass.ds(l * 2 + C_LAM, 2)])
                dve.wait_ge(tr_mm.s, tr_mm.at(l, 2))
                nc.vector.tensor_copy(CKT, PS[:, 3:5, :]).then_inc(tr_dve.s, 1)
                dve.wait_ge(tr_mm.s, tr_mm.at(l, 3))
                nc.vector.tensor_copy(KT[NOPE:QD, 0], PS[0:ROPE, 5])
                nc.vector.tensor_copy(KT[NOPE:QD, 1], PS[0:ROPE, 5]).then_inc(tr_dve.s, 1)
                for t in range(4):
                    n = USER_AT["v", t]
                    dve.wait_ge(user_mm.s, user_mm.at(l, n + 1))
                    nc.vector.tensor_copy(VM[:, t], PS[:, 6 + n % 2]).then_inc(user_dve.s, 1)
                dve.wait_ge(lame_ok.s, lame_ok.at(l, 1))
                link(nc.vector.tensor_tensor(LAM, LE[:, 1:2], LE[:, 0:1], ALU.subtract), l)
                link(nc.vector.tensor_tensor(LAM, LAM, LIC[:, 0:1], ALU.subtract), l)
                nc.vector.tensor_tensor(SUB, SUB, LIC[:, 1:2], ALU.mult)
                prep(l, 0)
                for i in range(NJ + 1):
                    if i < NJ:
                        maxima(l, i)
                    if i + 1 < NJ:
                        prep(l, i + 1)
                    if i < NJ:
                        normalise(l, i)
                    if i == 2:
                        dve.wait_ge(sqg_ok.s, sqg_ok.at(l, 1))
                        link(nc.vector.reduce_sum(STG, SQG.rearrange("p t (h d) -> p (t h) d", d=64), AX), l)
                        nc.vector.tensor_scalar(RG, STG, 1.0 / 64, EPS, ALU.mult, ALU.add).then_inc(msg_ok.s, 1)
                        dve.wait_ge(rootg_ok.s, rootg_ok.at(l, 1))
                        nc.vector.reciprocal(RG, RG).then_inc(rg_ok.s, 1)
                    for key in FILL[i]:
                        if key[0] in ("br0", "br1"):
                            branch(l, key)
                        elif key[0] in ("ada", "adat"):
                            modulation(l, key)
                    if i < NJ:
                        for m in range(2 if JOBS[i][0] == "gqa" else 1):
                            n = OUT_AT[i, m]
                            dve.wait_ge(pt_mm.s, pt_mm.at(l, n + 1))
                            if n >= 2:
                                dve.wait_ge(user_mm.s, user_mm.at(l, USER_AT["pv", OUTS[n - 2][0]] + 1))
                            nc.vector.tensor_copy(PT[:, n % 2, 384:896], PS[:, 5]).then_inc(pt_dve.s, 1)
                dve.wait_ge(sqd_mm.s, sqd_mm.at(l, 1))
                nc.vector.tensor_scalar(RSD, PS[:, 0:4, 0:TOK], 1.0 / 128, EPS, ALU.mult, ALU.add)\
                    .then_inc(msd_ok.s, 1)
                dve.wait_ge(rootd_ok.s, rootd_ok.at(l, 1))
                link(nc.vector.reciprocal(RSD, RSD), l)
                nc.vector.scalar_tensor_tensor(out=OT2, in0=OT2, scalar=SUB, in1=RSD, op0=ALU.mult,
                                               op1=ALU.mult).then_inc(ot2_ok.s, 1)
                for c in range(KC):
                    branch(l, ("br2", c))
                dve.wait_ge(gb_ok.s, gb_ok.at(l, 1))
                for t in range(NT):
                    for h in range(2):
                        n = USER_AT["out", t, h]
                        dve.wait_ge(user_mm.s, user_mm.at(l, n + 1))
                        x = X[:, t, BF * h:BF * h + BF]
                        nc.vector.tensor_tensor(TMP[:, h], PS[:, 6 + n % 2], G1[:, min(t, 1), BF * h:BF * h + BF],
                                                ALU.mult).then_inc(user_dve.s, 1)
                        dve.wait_ge(user_dve.s, user_dve.at(l, evacuated(n)))
                        ins = nc.vector.tensor_tensor(x, x, TMP[:, h], ALU.add)
                        if (t, h) == (2, 0):
                            h2_out(l, 0)
                    ins.then_inc(x1_ok.s, 1)
                    dve.wait_ge(ss_t.s, ss_t.at(l, t + 1))
                    r = RS[:, t:t + 1]
                    nc.vector.tensor_scalar(r, ST[:, t:t + 1], 1.0 / D, EPS, ALU.mult, ALU.add)\
                        .then_inc(ms_t.s, 1)
                    dve.wait_ge(root_t.s, root_t.at(l, t + 1))
                    link(nc.vector.reciprocal(r, r), l)
                    nc.vector.tensor_scalar(XN2[:, t], X[:, t], r, None, ALU.mult).then_inc(xn_t.s, 1)
                h2_out(l, 1)
                nc.vector.memset(AFT, 1.0)
                nc.vector.memset(XB[:, :, :, CAP:XW], 0.0)
                dve.wait_ge(router_mm.s, router_mm.at(l, 1))
                ps = PS[:, 0, 0:NT * NE].rearrange("p (t e) -> p t e", t=NT)
                link(nc.vector.reduce_max(ST, ps, AX), l)
                st = ST.rearrange("p (t o) -> p t o", o=1).to_broadcast([P, NT, NE])
                nc.vector.tensor_tensor(LG, ps, st, ALU.subtract).then_inc(logit_ok.s, 1)
                dve.wait_ge(aexp_ok.s, aexp_ok.at(l, 1))
                link(nc.vector.reduce_sum(ST, LG, AX), l)
                link(nc.vector.reciprocal(RS, ST), l)
                nc.vector.tensor_tensor(AFF, LG, RS.rearrange("p (t o) -> p t o", o=1).to_broadcast([P, NT, NE]),
                                        ALU.mult).then_inc(aff_ok.s, 1)
                dve.wait_ge(aff_t.s, aff_t.at(l, 1))
                link(nc.vector.tensor_copy(WK, PS[0:NE, 1, 0:TOK]), l)
                for lo, hi, rounds in ((0, P, CAP_P // 8), (P, TOK, CAP_S // 8)):
                    for _ in range(rounds):
                        apart(dve)
                        link(nc.vector.max(M8, WK[:, lo:hi]), l)
                        apart(dve)
                        link(nc.vector.match_replace(WK[:, lo:hi], M8, WK[:, lo:hi], -1.0), l)
                link(nc.vector.tensor_scalar(MK, WK, 0.0, None, ALU.is_lt), l)
                for lo, hi in ((0, P), (P, TOK)):
                    ins = nc.vector.tensor_tensor_scan(SN[:, lo:hi], AFT[:, lo:hi], MK[:, lo:hi], 0.0,
                                                       ALU.mult, ALU.add)
                link(ins, l)
                nc.vector.tensor_tensor(SN, SN, MK, ALU.mult).then_inc(pos_ok.s, 1)
                dve.wait_ge(pos_t.s, pos_t.at(l, 1))
                link(nc.vector.tensor_copy(POS, PS[:, 2, 0:NT * NE].rearrange("p (t e) -> p t e", t=NT)), l)
                for t in range(NT):
                    pos = POS[:, t].rearrange("p (e o) -> p e o", o=1).to_broadcast([P, NE, CAP_S])
                    iota = IOTA.rearrange("p (o s) -> p o s", o=1).to_broadcast([P, NE, CAP_S])
                    ins = nc.vector.tensor_tensor(DD[:, t], pos, iota, ALU.is_equal)
                ins.then_inc(disp_ok.s, 1)
                dve.wait_ge(disp_ok.s, disp_ok.at(l, 1))
                for t in range(NT):
                    aff = AFF[:, t].rearrange("p (e o) -> p e o", o=1).to_broadcast([P, NE, CAP_S])
                    ins = nc.vector.tensor_tensor(DG[:, t], DD[:, t], aff, ALU.mult)
                ins.then_inc(gated_ok.s, 1)
                nc.vector.memset(YS[:, 1], 0.0)
                for c in range(KC):
                    n = 2 * c + 1
                    dve.wait_ge(gather_mm.s, gather_mm.at(l, n + 1))
                    nc.vector.tensor_scalar(XE[:, c, :, CAP_S:CAP],
                                            PS[:, n % 4, 0:NE * CAP_P].rearrange("p (e s) -> p e s", e=NE),
                                            AA[:, 1, 0, c:c + 1], MODC[:, 0, 24 + c:25 + c],
                                            ALU.mult, ALU.add).then_inc(gather_dve.s, 1)
                    if c == 5:
                        dve.wait_ge(dgt_mm.s, dgt_mm.at(l, 1))
                        nc.vector.tensor_copy(DGT, PS[:, 4:7, :].rearrange("p a b -> p (a b)")
                                              .rearrange("p (g n) -> p g n", g=NG)).then_inc(dgt_ok.s, 1)
                dve.wait_ge(gather_act.s, gather_act.at(l, 8))
                dve.wait_ge(gather_dve.s, gather_dve.at(l, 8))
                dve.wait_ge(dgt_ok.s, dgt_ok.at(l, 1))
                dve.wait_ge(gb_ok.s, gb_ok.at(l, 2))
                apart(dve)
                with dve.Fori(0, NG) as g:
                    dve.wait_ge(comb_mm.s, comb_mm.in_group(l, g, 0))
                    nc.vector.tensor_copy(DGB, DGT.rearrange("p g n -> p (g n)")[:, bass.ds(g * (NT * P), NT * P)])\
                        .then_inc(dgb_ok.s, 1)

                    def tokens(e):
                        xe = XE[:, :, bass.ds(g * GE + e, 1), :].rearrange("p k e s -> p k (e s)")
                        nc.vector.tensor_copy(XB[:, e % 2, :, 0:CAP], xe).then_inc(xb_ok.s, 1)

                    tokens(0)
                    for e in range(GE):
                        if e + 1 < GE:
                            if e >= 1:
                                dve.wait_ge(gu_mm.s, gu_mm.in_group(l, g, 2 * e))
                            tokens(e + 1)
                        dve.wait_ge(sig_ok.s, sig_ok.in_group(l, g, e + 1))
                        dve.wait_ge(at_mm.s, at_mm.in_group(l, g, e))
                        nc.vector.tensor_tensor(AC, PS[:, e % 2], SGE, ALU.mult).then_inc(silu_ok.s, 1)
                        dve.wait_ge(silu_ok.s, silu_ok.in_group(l, g, e + 1))
                        dve.wait_ge(gu_mm.s, gu_mm.in_group(l, g, 2 * e + 2))
                        nc.vector.tensor_tensor(AC, AC, PS[:, 2 + e % 2], ALU.mult).then_inc(ac_ok.s, 1)
                    for n in range(6):
                        t, h = n // 2, n % 2
                        x = X[:, t, BF * h:BF * h + BF]
                        dve.wait_ge(comb_mm.s, comb_mm.in_group(l, g, n + 1))
                        nc.vector.tensor_tensor(CTMP[:, h], PS[:, 6 + h], G2[:, min(t, 1), BF * h:BF * h + BF],
                                                ALU.mult).then_inc(comb_ok.s, 1)
                        dve.wait_ge(comb_ok.s, comb_ok.in_group(l, g, n + 1))
                        ins = nc.vector.tensor_tensor(x, x, CTMP[:, h], ALU.add)
                    ins.then_inc(xg_ok.s, 1)
                    dve.wait_ge(xg_ok.s, xg_ok.in_group(l, g, 1))
                assert links[0] == DVE_LINKS, ("DVE_LINKS", links[0])
            dve.wait_ge(fin_ss.s, 1)
            nc.vector.tensor_scalar(RS, ST, 1.0 / D, EPS, ALU.mult, ALU.add).then_inc(fin_ms.s, 1)
            dve.wait_ge(fin_root.s, 1)
            nc.vector.reciprocal(RS, RS).then_inc(fin_ms.s, 1)
            dve.wait_ge(fin_ms.s, 2)
            dve.wait_ge(fn_in.s, 16)
            for t in range(NT):
                nc.vector.scalar_tensor_tensor(out=XN[:, t], in0=X[:, t], scalar=RS[:, t:t + 1], in1=at(0, D),
                                               op0=ALU.mult, op1=ALU.mult).then_inc(fin_ok.s, 1)

        @block.tensor
        def _(pe):
            def arrived(l, n):
                pe.wait_ge(filled[n % SLOTS].s, (l * USES + n // SLOTS + 1) * 16)

            owed = []

            def settle(ins):
                if owed:
                    ins.then_inc(used[owed.pop()].s, 1)
                return ins

            def user_bank(l, key):
                n = USER_AT[key]
                if n >= 2:
                    freed = user_dve if USERS[n - 2][0] in BY_DVE else user_act
                    pe.wait_ge(freed.s, freed.at(l, evacuated(n - 2)))
                return PS[:, 6 + n % 2]

            def turn(out, src, rows=P):
                return pe.transpose(out, src, IDT[0:rows, 0:rows])

            def norm_turn(l):
                pe.wait_ge(xn_ok.s, xn_ok.at(l, NT))
                for c in range(KC):
                    if c >= 4:
                        freed = ht_dve if c % 2 else ht_act
                        pe.wait_ge(freed.s, freed.at(l, (c - 4) // 2 + 1))
                    for t in range(NT):
                        ins = turn(PS[:, 4 + c % 4, P * t:P * t + P], XN[:, t, P * c:P * c + P])
                        if (c, t) == (0, 0):
                            settle(ins)
                    ins.then_inc(ht_mm.s, 1)

            def h2_turn(l, n):
                pe.wait_ge(xn_t.s, xn_t.at(l, 2 if n == 0 else 3))
                for c, _, lo, hi, ps in h2_pieces(n):
                    ins = settle(turn(ps, XN2[:, lo // P, P * c:P * c + P]))
                ins.then_inc(h2_mm.s, 1)

            def router(l, tiles):
                for t in tiles:
                    for k in range(KC):
                        ins = pe.matmul(PS[:, 0, NE * t:NE * t + NE], hT[:, k, P * t:P * t + P], WR[:, k],
                                        start=k == 0, stop=k == KC - 1)
                return ins

            def ada(l, i, ps):
                for k in range(KC):
                    n = UNIT["ada", i, k]
                    arrived(l, n)
                    for j in range(4):
                        ins = pe.matmul(ps[32 * j:32 * j + 2], SC[:, k], ring[:, n % SLOTS, BF * j:BF * j + BF],
                                        start=k == 0, stop=k == KC - 1)
                        if j == 0:
                            settle(ins)
                    if k < KC - 1:
                        ins.then_inc(used[n % SLOTS].s, 1)
                owed.append(n % SLOTS)
                return ins

            def mod_turn(i, ps):
                for q in range(4):
                    ins = settle(turn(ps[:, P * q:P * q + P], MODR[:, BF * i + P * q:BF * i + P * q + P]))
                return ins

            def project(l, key, units, stride, width, col, t, last):
                ps = user_bank(l, key)
                for k in range(KC):
                    n = units[k // 2]
                    if k % 2 == 0:
                        arrived(l, n)
                    c0 = (k % 2) * stride + col
                    ins = pe.matmul(ps[:, 0:width], hT[:, k, P * t:P * t + P], ring[:, n % SLOTS, c0:c0 + width],
                                    start=k == 0, stop=k == KC - 1)
                    if k == 0:
                        settle(ins)
                    if last and k % 2 and k < KC - 1:
                        ins.then_inc(used[n % SLOTS].s, 1)
                ins.then_inc(user_mm.s, 1)
                if last:
                    owed.append(n % SLOTS)

            def gate(l, b, c):
                ps = user_bank(l, (f"gate{b}", c))
                n = UNIT[f"gate{b}", c // 2]
                arrived(l, n)
                w = ring[:, n % SLOTS].rearrange("p (k n) -> p k n", k=KC)
                for k in range(KC):
                    ins = pe.matmul(ps[:, 0:TOK], w[:, k, P * (c % 2):P * (c % 2) + P], hT[:, k], start=k == 0,
                                    stop=k == KC - 1)
                    if k == 0:
                        settle(ins)
                ins.then_inc(user_mm.s, 1)
                if c % 2:
                    owed.append(n % SLOTS)

            def branch(l, b, c):
                ps = user_bank(l, (f"br{b}", c))
                n = UNIT[f"br{b}", c // 4]
                arrived(l, n)
                if b < 2:
                    j = 7 if b == 0 else 11
                    pe.wait_ge(user_act.s, user_act.at(l, evacuated(USER_AT["pv", j])))
                else:
                    pe.wait_ge(ot2_ok.s, ot2_ok.at(l, 1))
                w = ring[:, n % SLOTS].rearrange("p (k n) -> p k n", k=4)
                o = (OT0, OT1, OT2)[b]
                for k in range(4):
                    ins = pe.matmul(ps[:, 0:TOK], w[:, k, P * (c % 4):P * (c % 4) + P], o[:, k], start=k == 0,
                                    stop=k == 3)
                    if k == 0:
                        settle(ins)
                ins.then_inc(user_mm.s, 1)
                if c % 4 == 3:
                    owed.append(n % SLOTS)

            def fill(l, key):
                kind = key[0]
                if kind == "c1":
                    project(l, key, [UNIT["c1", u] for u in range(4)], ZG_W, 384, 384 * key[2], key[1],
                            key[1:] == (2, 1))
                elif kind == "c2":
                    half, t, q = key[1] // 6, key[1] % 6 // 2, key[1] % 2
                    project(l, key, [UNIT["c2", 4 * half + u] for u in range(4)], 768, 384, 384 * q, t,
                            (t, q) == (2, 1))
                elif kind.startswith("gate"):
                    gate(l, int(kind[4]), key[1])
                elif kind == "ada":
                    ada(l, key[1], user_bank(l, key)).then_inc(user_mm.s, 1)
                elif kind == "adat":
                    ps = user_bank(l, key)
                    pe.wait_ge(user_dve.s, user_dve.at(l, evacuated(USER_AT["ada", key[1]])))
                    mod_turn(key[1], ps).then_inc(user_mm.s, 1)
                else:
                    branch(l, int(kind[2]), key[1])

            def prep(l, j):
                kind, i = JOBS[j]
                if j >= 2:
                    before = OUT_AT[j - 2, 1 if JOBS[j - 2][0] == "gqa" else 0] + 1
                    pe.wait_ge(pt_act.s, pt_act.at(l, before))
                    pe.wait_ge(pt_dve.s, pt_dve.at(l, before))
                if j == 1:
                    pe.wait_ge(prep_act.s, prep_act.at(l, 1))
                    pe.wait_ge(prep_dve.s, prep_dve.at(l, 1))
                if kind == "mla":
                    for c in range(2):
                        settle(pe.matmul(PS[0:NOPE, 4], UKV[:, 0, c, NOPE * i:NOPE * i + NOPE], CKT[:, c],
                                         start=c == 0, stop=c == 1))
                    if i == 0:
                        pe.wait_ge(qrope_ok.s, qrope_ok.at(l, 1))
                    for t in range(NT):
                        ins = turn(PS[0:QD, 5, P * t:P * t + P], QQ[:, t, QD * i:QD * i + QD])
                elif kind == "gqa":
                    if i == 0:
                        pe.wait_ge(gq_ok.s, gq_ok.at(l, 1))
                        for kt, src in enumerate((ZG[:, 0, G_K:G_K + 128], CTX_GK, ZG[:, 1, G_K:G_K + 128],
                                                  ZG[:, 2, G_K:G_K + 128])):
                            settle(turn(PS[:, 4, P * kt:P * kt + P], src))
                    for t in range(NT):
                        ins = turn(PS[:, 5, P * t:P * t + P], ZG[:, t, P * i:P * i + P])
                        if t == 0:
                            settle(ins)
                else:
                    if i == 0:
                        pe.wait_ge(dq_ok.s, dq_ok.at(l, 1))
                    k0 = D_K + P * i
                    for kt, src in enumerate((ZD[:, 0, k0:k0 + P], CTX_DK[:, P * i:P * i + P], ZD[:, 1, k0:k0 + P],
                                              ZD[:, 2, k0:k0 + P])):
                        settle(turn(PS[:, 4, P * kt:P * kt + P], src))
                    for t in range(NT):
                        ins = turn(PS[:, 5, P * t:P * t + P], ZD[:, t, P * i:P * i + P])
                ins.then_inc(prep_mm.s, 1)

            def scores(l, j):
                kind, i = JOBS[j]
                pe.wait_ge(prep_act.s, prep_act.at(l, j + 1))
                pe.wait_ge(prep_dve.s, prep_dve.at(l, j + 1))
                if j >= 1:
                    n = MAP_AT[j - 1, 0 if JOBS[j - 1][0] == "mla" else 1]
                    pe.wait_ge(exp_ok.s, exp_ok.at(l, n + 1))
                if (kind, i) == ("gqa", 0):
                    pe.wait_ge(zero_ok.s, zero_ok.at(l, 1))
                b = j % 2
                for m in range(1 if kind == "mla" else 2):
                    q = QM[0:QD, b] if kind == "mla" else QAB[:, b, m]
                    k = KT[0:QD, b] if kind == "mla" else KT[:, i // 2 if kind == "gqa" else b]
                    settle(pe.matmul(PS[:, 2 * m, 0:384], q[:, P:2 * P], k[:, P:NKEY], start=True, stop=True))
                    pe.matmul(PS[:, 2 * m, 384:512], q[:, 0:P], k[:, 0:P], start=True, stop=True)
                    pe.matmul(PS[:, 2 * m + 1, 0:384], q[:, 2 * P:TOK], k[:, P:NKEY], start=True, stop=True)\
                        .then_inc(score_mm.s, 1)

            def turn_probs(l, j):
                for m in range(2 if JOBS[j][0] == "gqa" else 1):
                    n = OUT_AT[j, m]
                    pe.wait_ge(prob_ok.s, prob_ok.at(l, n + 1))
                    if m == 0 and j + 1 < NJ:
                        pe.wait_ge(prep_act.s, prep_act.at(l, j + 2))
                        pe.wait_ge(prep_dve.s, prep_dve.at(l, j + 2))
                    elif n >= 1:
                        pe.wait_ge(pt_act.s, pt_act.at(l, n))
                        pe.wait_ge(pt_dve.s, pt_dve.at(l, n))
                    p = PB[:, MAP_AT[j, m] % 2]
                    settle(turn(PS[:, 4, 0:P], p[:, 384:512]))
                    for q, at_q in enumerate((0, 512)):
                        turn(PS[:, 4, P * (q + 1):P * (q + 2)], p[:, at_q:at_q + P])
                    for kt in range(1, 3):
                        for q, at_q in enumerate((0, 512)):
                            ins = turn(PS[:, 5, 256 * (kt - 1) + P * q:256 * (kt - 1) + P * q + P],
                                       p[:, at_q + P * kt:at_q + P * kt + P])
                    ins.then_inc(pt_mm.s, 1)

            def values(l, j):
                kind, i = JOBS[j]
                ps = user_bank(l, ("pv", j))
                for m in range(2 if kind == "gqa" else 1):
                    n = OUT_AT[j, m]
                    pe.wait_ge(pt_act.s, pt_act.at(l, n + 1))
                    pe.wait_ge(pt_dve.s, pt_dve.at(l, n + 1))
                    if kind == "mla":
                        c = 64 * i
                        v = [VM[:, kt, c:c + 64] for kt in range(4)]
                        out = ps[64 * (i % 2):64 * (i % 2) + 64]
                    elif kind == "gqa":
                        kv = 64 * (i // 2)
                        c = G_V + kv
                        v = [ZG[:, 0, c:c + 64], CTX_GV[:, kv:kv + 64], ZG[:, 1, c:c + 64],
                             ZG[:, 2, c:c + 64]]
                        out = ps[64 * m:64 * m + 64]
                    else:
                        c = D_V + P * i
                        v = [ZD[:, 0, c:c + P], CTX_DV[:, P * i:P * i + P], ZD[:, 1, c:c + P], ZD[:, 2, c:c + P]]
                        out = ps
                    pt = PT[:, n % 2]
                    settle(pe.matmul(out[:, 0:P], v[0], pt[:, 0:P], start=True, stop=True))
                    for kt in range(3):
                        ins = pe.matmul(out[:, P:TOK], v[kt + 1], pt[:, P + 256 * kt:P + 256 * kt + 256],
                                        start=kt == 0, stop=kt == 2)
                ins.then_inc(user_mm.s, 1)

            def gate_rows(l, which, bank):
                for s in range(2):
                    for h in range(2):
                        row = 32 * (2 * which + h) + s
                        ins = pe.matmul(PS[:, bank + 2 * s + h], IDT[:, row:row + 1].to_broadcast([P, P]),
                                        MODR[:, BF * (1 + which):BF * (2 + which)], start=True, stop=True)
                        if (s, h) == (0, 0):
                            settle(ins)
                ins.then_inc(gb_mm.s, 1)

            for free in (*used, router_mm, at_mm, comb_mm):
                pe.sem_inc(free.s, 1)
            pe.wait_ge(const_in.s, 16)
            pe.wait_ge(cond_in.s, 32)
            turn(PS[:, 0, 0:16], CR, 16).then_inc(cond_t.s, 1)
            pe.wait_ge(cond_ok.s, 1)
            with pe.Fori(0, DEPTH) as l:
                pe.wait_ge(early_in.s, early_in.at(l, 96))
                apart(pe)
                turn(PS[:, 3, 0:16], NR, 16).then_inc(mod_t.s, 1)

                ada(l, 0, PS[:, 0]).then_inc(ada_mm.s, 1)
                pe.wait_ge(mod_row.s, mod_row.at(l, 1))
                pe.wait_ge(ncol_ok.s, ncol_ok.at(l, 1))
                mod_turn(0, PS[:, 3]).then_inc(mod_t.s, 1)
                norm_turn(l)
                pe.wait_ge(ht_act.s, ht_act.at(l, 4))
                pe.wait_ge(ht_dve.s, ht_dve.at(l, 4))
                units = [UNIT["c0", u] for u in range(4)]
                for t in range(NT):
                    for h in range(2):
                        project(l, ("c0", t, h), units, ZA_W, 336, 336 * h, t, (t, h) == (2, 1))
                for h in range(2):
                    fill(l, ("c1", 0, h))
                pe.wait_ge(za_ok.s, za_ok.at(l, 1))
                for c in range(3):
                    for t in range(NT):
                        ins = turn(PS[:, c, P * t:P * t + P], ZA[:, t, P * c:P * c + P])
                        if (c, t) == (0, 0):
                            settle(ins)
                ins.then_inc(tr_mm.s, 1)
                pe.wait_ge(late_in.s, late_in.at(l, 18 * 16))
                for c in range(2):
                    k0 = Z_KV + P * c
                    for kt, src in enumerate((ZA[:, 0, k0:k0 + P], CTX_CKV[:, P * c:P * c + P], ZA[:, 1, k0:k0 + P],
                                              ZA[:, 2, k0:k0 + P])):
                        ins = turn(PS[:, 3 + c, P * kt:P * kt + P], src)
                ins.then_inc(tr_mm.s, 1)
                pe.wait_ge(kpe_ok.s, kpe_ok.at(l, 1))
                for kt, src in enumerate((ZA[:, 0, Z_PE:Z_PE + ROPE], CTX_KPE, KPR[:, 0], KPR[:, 1])):
                    ins = turn(PS[0:ROPE, 5, P * kt:P * kt + P], src)
                ins.then_inc(tr_mm.s, 1)
                pe.wait_ge(tr_act.s, tr_act.at(l, 1))
                for t in range(NT):
                    for h in range(2):
                        ps = user_bank(l, ("q", t, h))
                        for k in range(3):
                            n = UNIT["uq", k // 2]
                            arrived(l, n)
                            c0 = (k % 2) * 768 + 384 * h
                            ins = pe.matmul(ps[:, 0:384], CQT[:, k, P * t:P * t + P],
                                            ring[:, n % SLOTS, c0:c0 + 384], start=k == 0, stop=k == 2)
                            if (t, h) == (2, 1) and k == 1:
                                ins.then_inc(used[n % SLOTS].s, 1)
                        ins.then_inc(user_mm.s, 1)
                owed.append(n % SLOTS)
                pe.wait_ge(tr_dve.s, tr_dve.at(l, 2))
                for kt in range(4):
                    ps = user_bank(l, ("v", kt))
                    for c in range(2):
                        ins = pe.matmul(ps, CKT[:, c, P * kt:P * kt + P], UKV[:, 1, c], start=c == 0, stop=c == 1)
                        if c == 0:
                            settle(ins)
                    ins.then_inc(user_mm.s, 1)
                prep(l, 0)
                for i in range(NJ + 1):
                    if i < NJ:
                        scores(l, i)
                    if i + 1 < NJ:
                        prep(l, i + 1)
                    if i >= 1:
                        values(l, i - 1)
                    for key in FILL[i]:
                        fill(l, key)
                    if i < NJ:
                        turn_probs(l, i)
                for c in range(KC):
                    gate(l, 2, c)
                    if c == 1:
                        pe.wait_ge(sqd_ok.s, sqd_ok.at(l, 1))
                        for h in range(4):
                            ins = pe.matmul(PS[:, h, 0:TOK], ONES, SQD[:, h], start=True, stop=True)
                            if h == 0:
                                settle(ins)
                        ins.then_inc(sqd_mm.s, 1)
                pe.wait_ge(msd_ok.s, msd_ok.at(l, 1))
                pe.wait_ge(stored_d.s, stored_d.at(l, 32))
                gate_rows(l, 0, 0)
                for c in range(KC):
                    branch(l, 2, c)
                pe.wait_ge(user_dve.s, user_dve.at(l, evacuated(USER_AT["br2", KC - 1])))
                for t in range(NT):
                    for h in range(2):
                        if (t, h) == (2, 1):
                            pe.wait_ge(gb_ok.s, gb_ok.at(l, 1))
                            h2_turn(l, 0)
                        ps = user_bank(l, ("out", t, h))
                        for k in range(KC):
                            n = UNIT["wout", k // 2]
                            arrived(l, n)
                            c0 = (k % 2) * D + BF * h
                            ins = pe.matmul(ps, MG[:, k, P * t:P * t + P], ring[:, n % SLOTS, c0:c0 + BF],
                                            start=k == 0, stop=k == KC - 1)
                            if k == 0:
                                settle(ins)
                            if (t, h) == (2, 1) and k % 2 and k < KC - 1:
                                ins.then_inc(used[n % SLOTS].s, 1)
                        ins.then_inc(user_mm.s, 1)
                owed.append(n % SLOTS)
                pe.wait_ge(h2_act.s, h2_act.at(l, 1))
                pe.wait_ge(h2_dve.s, h2_dve.at(l, 1))
                settle(router(l, (0, 1)))
                h2_turn(l, 1)
                pe.wait_ge(h2_act.s, h2_act.at(l, 2))
                pe.wait_ge(h2_dve.s, h2_dve.at(l, 2))
                router(l, (2,)).then_inc(router_mm.s, 1)
                gate_rows(l, 1, 4)
                pe.wait_ge(aff_ok.s, aff_ok.at(l, 1))
                for t in range(NT):
                    ins = turn(PS[0:NE, 1, P * t:P * t + P], AFF[:, t])
                ins.then_inc(aff_t.s, 1)
                pe.wait_ge(pos_ok.s, pos_ok.at(l, 1))
                apart(pe)
                for t in range(NT):
                    ins = turn(PS[:, 2, NE * t:NE * t + NE], SN[:, P * t:P * t + P], NE)
                ins.then_inc(pos_t.s, 1)
                pe.wait_ge(disp_ok.s, disp_ok.at(l, 1))
                for c in range(KC):
                    if c == 4:
                        pe.wait_ge(gb_ok.s, gb_ok.at(l, 2))
                        pe.wait_ge(gated_ok.s, gated_ok.at(l, 1))
                        for n in range(NG * NT):
                            src = DG[:, n % NT, GE * (n // NT):GE * (n // NT) + GE].rearrange("p e s -> p (e s)")
                            ins = turn(PS[:, 4 + n // 4, P * (n % 4):P * (n % 4) + P], src)
                        ins.then_inc(dgt_mm.s, 1)
                    for s in range(2):
                        n = 2 * c + s
                        if n >= 4:
                            freed = gather_dve if s else gather_act
                            pe.wait_ge(freed.s, freed.at(l, (n - 4) // 2 + 1))
                        if s == 0:
                            for t in range(1, 3):
                                ins = pe.matmul(PS[:, n % 4], XN2[:, t, P * c:P * c + P],
                                                DD[:, t].rearrange("p e s -> p (e s)"), start=t == 1, stop=t == 2)
                        else:
                            ins = pe.matmul(PS[:, n % 4, 0:NE * CAP_P], XN2[:, 0, P * c:P * c + P],
                                            DD[:, 0, :, 0:CAP_P], start=True, stop=True)
                        ins.then_inc(gather_mm.s, 1)
                apart(pe)
                with pe.Fori(0, NG) as g:
                    def wide(e, first, lhs, bank, done):
                        for u in range(4):
                            n = 12 * e + first + u
                            pe.wait_ge(filled[n % SLOTS].s,
                                       (l * USES + g * (GROUP_UNITS // SLOTS) + (ATT_UNITS + n) // SLOTS + 1) * 16)
                            for k in range(2 * u, 2 * u + 2):
                                for h in range(2):
                                    c0 = (k % 2) * D + BF * h
                                    ins = pe.matmul(PS[64 * h:64 * h + 64, bank], lhs(k),
                                                    ring[:, n % SLOTS, c0:c0 + BF], start=k == 0, stop=k == KC - 1)
                                    if (k, h) == (0, 0):
                                        settle(ins)
                            if u < 3:
                                ins.then_inc(used[n % SLOTS].s, 1)
                        ins.then_inc(done.s, 1)
                        owed.append(n % SLOTS)

                    for e in range(GE):
                        pe.wait_ge(xb_ok.s, xb_ok.in_group(l, g, e + 1))
                        wide(e, 0, lambda k: XB[:, e % 2, k], e % 2, gu_mm)
                        wide(e, 4, lambda k: XB[:, e % 2, k], 2 + e % 2, gu_mm)
                        pe.wait_ge(ac_ok.s, ac_ok.in_group(l, g, e + 1))
                        for q in range(4):
                            ins = turn(PS[:, 4, P * q:P * q + P], AC[:, P * q:P * q + P])
                            if q == 0:
                                settle(ins)
                        ins.then_inc(at_mm.s, 1)
                        pe.wait_ge(at_ok.s, at_ok.in_group(l, g, e + 1))
                        pe.wait_ge(y_ok.s, y_ok.in_group(l, g, e))
                        wide(e, 8, lambda k: AT[:, k % 4, XW * (k // 4):XW * (k // 4) + XW], 5, y_mm)
                    pe.wait_ge(dgb_ok.s, dgb_ok.in_group(l, g, 1))
                    pe.wait_ge(y_ok.s, y_ok.in_group(l, g, GE))
                    for n in range(6):
                        t, h = n // 2, n % 2
                        pe.wait_ge(comb_ok.s, comb_ok.in_group(l, g, max(n - 1, 0)))
                        w = DGB[:, P * t:P * t + P]
                        for half in range(2):
                            y = YS[:, 0 if t else 1, BF * h + 256 * half:BF * h + 256 * half + 256]
                            ins = pe.matmul(PS[:, 6 + h, 256 * half:256 * half + 256], w, y, start=True, stop=True)
                            if half == 0:
                                settle(ins)
                        ins.then_inc(comb_mm.s, 1)
                    assert not owed


_INS = ["x_prompt", "x_sample", "cache_mla_ckv", "cache_mla_kpe", "cache_gqa_k", "cache_gqa_v", "cache_diff_k",
        "cache_diff_v", "c", "c_ctx", "w_ada", "b_ada", "norm1", "norm2", "w_in", "mla_q_norm", "mla_kv_norm",
        "mla_w_uq", "mla_w_uk", "mla_w_uv", "gqa_q_norm", "gqa_k_norm", "diff_lam_q1", "diff_lam_k1",
        "diff_lam_q2", "diff_lam_k2", "diff_subln", "w_br_mla", "w_br_gqa", "w_br_diff", "w_out", "w_router",
        "w_gate", "w_up", "w_down", "final_norm"]
_OUTS = [("y_prompt", (1, 128, 1024)), ("y_sample", (1, 256, 1024)), ("new_ckv", (1, 2, 128, 256)),
         ("new_kpe", (1, 2, 128, 32)), ("new_gk", (1, 2, 128, 2, 64)), ("new_gv", (1, 2, 128, 2, 64)),
         ("new_dk", (1, 2, 128, 4, 128)), ("new_dv", (1, 2, 128, 4, 128))]


def kernel(**inputs):
    import concourse.bacc as bacc
    from concourse.bass_utils import run_bass_kernel_spmd

    nc = bacc.Bacc("TRN2", target_bir_lowering=False, num_devices=1)
    arrays, args = {}, {}
    for name in _INS:
        x = np.ascontiguousarray(inputs[name])
        arrays[f"in_{name}"] = x
        args[name] = nc.dram_tensor(f"in_{name}", x.shape, mybir.dt.from_np(x.dtype), kind="ExternalInput").ap()
    arrays["in_constants"] = constants()
    args["constants"] = nc.dram_tensor("in_constants", (P, C_W), F32, kind="ExternalInput").ap()
    for name, shape in _OUTS:
        args[name] = nc.dram_tensor(f"out_{name}", shape, F32, kind="ExternalOutput").ap()
    backbone(nc, args)
    r = run_bass_kernel_spmd(nc, [arrays], core_ids=[0])
    return tuple(r.results[0][f"out_{name}"] for name, _ in _OUTS)
```

```python
from contextlib import ExitStack
import math

import numpy as np
import concourse.bass as bass
from concourse import mybir

F32 = mybir.dt.float32
ALU = mybir.AluOpType
ACT = mybir.ActivationFunctionType
AX = mybir.AxisListType.X

P = 128
D = 1024
KC = D // P
DEPTH = 2
NT = 3
TOK = NT * P
NKEY = 4 * P
EPS = 1e-6
QR, KVR, ROPE, NOPE = 384, 256, 32, 64
QD = NOPE + ROPE
NE, FF = 16, 1024
CAP_S, CAP_P = 32, 16
CAP = CAP_S + CAP_P
XW = 64
ATT = 2976
SLOTS = 8
SLOT = 2048
ATT_UNITS = 64
EXP_UNITS = 12
GE = 4
NG = NE // GE
ATT_USES = ATT_UNITS // SLOTS
BF = 512

ZA_W, ZG_W, ZD_W = 672, 768, 1536
Z_KV, Z_PE = QR, QR + KVR
G_K, G_V = 512, 640
D_K, D_V = 512, 1024

C_ID = 0
C_ONE = C_ID + P
C_COS = C_ONE + P
C_IOTA = C_COS + 2 * 192
C_LAM = C_IOTA + CAP_S
C_W = C_LAM + 2 * DEPTH


def lam_init(layer):
    return 0.8 - 0.6 * math.exp(-0.3 * layer)


def constants():
    c = np.zeros((P, C_W), np.float32)
    c[:, C_ID:C_ID + P] = np.eye(P)
    c[:, C_ONE:C_ONE + P] = 1.0
    token = np.arange(2 * P)
    axes = ((token // 64).astype(np.float32), (token % 64).astype(np.float32))
    at = C_COS
    tables = []
    for width in (64, 32):
        half = width // 4
        freqs = (np.float32(10000.0) ** (-np.arange(half, dtype=np.float32) / np.float32(half))).astype(np.float32)
        cos, sin = [], []
        for pos in axes:
            ang = (pos[:, None] * freqs[None, :]).astype(np.float32)
            co, si = np.cos(ang), np.sin(ang)
            cos += [co, co]
            sin += [-si, si]
        tables += [np.concatenate(cos, 1), np.concatenate(sin, 1)]
    table = np.concatenate(tables, 1).astype(np.float32)
    for t in range(2):
        c[:, at + 192 * t:at + 192 * (t + 1)] = table[t * P:(t + 1) * P]
    c[:, C_IOTA:C_IOTA + CAP_S] = np.arange(1, CAP_S + 1)
    for layer in range(DEPTH):
        c[:, C_LAM + 2 * layer] = lam_init(layer)
        c[:, C_LAM + 2 * layer + 1] = 1.0 - lam_init(layer)
    return c


class Signal:

    def __init__(self, handle, per, base):
        self.s, self.per, self.base = handle, per, base

    def at(self, layer, n):
        return layer * self.per + (n + self.base)

    def in_group(self, layer, g, n):
        return layer * self.per + g * (self.per // NG) + (n + self.base)


JOBS = [("mla", h) for h in range(8)] + [("gqa", i) for i in range(4)] + [("diff", h) for h in range(4)]
NJ = len(JOBS)
MAPS = []
OUTS = []
for _j, (_kind, _) in enumerate(JOBS):
    MAPS += [(_j, m) for m in range(1 if _kind == "mla" else 2)]
    OUTS += [(_j, m) for m in range(2 if _kind == "gqa" else 1)]
MAP_AT = {jm: n for n, jm in enumerate(MAPS)}
OUT_AT = {jm: n for n, jm in enumerate(OUTS)}
SCALE = {"mla": QD ** -0.5, "gqa": 64 ** -0.5, "diff": 64 ** -0.5}

FILL = [[] for _ in range(NJ + 1)]
for _t in range(1, NT):
    FILL[_t - 1] += [("c1", _t, h) for h in range(2)]
FILL[4].append(("ada", 1))
FILL[5].append(("adat", 1))
FILL[6].append(("ada", 2))
FILL[7].append(("adat", 2))
for _c in range(KC):
    FILL[(2, 3, 5, 7)[_c // 2]].append(("gate0", _c))
for _n in range(12):
    FILL[8 + _n // 6].append(("c2", _n))
for _c in range(KC):
    FILL[10 + _c // 4].append(("br0", _c))
for _c in range(KC):
    FILL[12 + _c // 2] += [("gate1", _c), ("br1", _c)]


def values_of(j):
    if JOBS[j][0] == "mla":
        return [(j - 1, 0), (j, 0)] if j % 2 else []
    return [(j, m) for m in range(2 if JOBS[j][0] == "gqa" else 1)]


def values_user(j):
    return USER_AT["pv", j | 1 if JOBS[j][0] == "mla" else j]


def key_preps(j):
    return j // 2 + 1 if j < 8 else j - 3


USERS = [("c0", t, h) for t in range(NT) for h in range(2)]
USERS += [("c1", 0, h) for h in range(2)]
USERS += [("q", t, h) for t in range(NT) for h in range(2)] + [("v", t) for t in range(4)]
for _i in range(NJ + 1):
    if _i >= 1 and values_of(_i - 1):
        USERS.append(("pv", _i - 1))
    USERS += FILL[_i]
USERS += [("gate2", c) for c in range(KC)] + [("br2", c) for c in range(KC)]
USERS += [("out", t, h) for t in range(NT) for h in range(2)]
USER_AT = {u: n for n, u in enumerate(USERS)}
BY_DVE = {"ada", "adat", "v", "br0", "br1", "br2", "out"}


def evacuated(n):
    dve = USERS[n][0] in BY_DVE
    return sum((u[0] in BY_DVE) == dve for u in USERS[:n + 1])


N_DVE_USERS = sum(u[0] in BY_DVE for u in USERS)
N_ACT_USERS = len(USERS) - N_DVE_USERS

PLAN = [("ada", 0, k) for k in range(KC)]
PLAN += [("c0", u) for u in range(4)] + [("c1", u) for u in range(4)] + [("uq", 0), ("uq", 1)]
PLAN += [("gate0", 0), ("gate0", 1)] + [("ada", 1, k) for k in range(KC)]
PLAN += [("gate0", 2)] + [("ada", 2, k) for k in range(KC)] + [("gate0", 3)]
PLAN += [("c2", u) for u in range(8)] + [("br0", 0), ("br0", 1)]
PLAN += [("gate1", 0), ("br1", 0), ("gate1", 1), ("gate1", 2), ("br1", 1), ("gate1", 3)]
PLAN += [("gate2", u) for u in range(4)] + [("br2", 0), ("br2", 1)] + [("wout", u) for u in range(4)]
assert len(PLAN) == ATT_UNITS
UNIT = {u: n for n, u in enumerate(PLAN)}

DVE_LINKS = 101
POOL_LINKS = 24


def backbone(nc, a):
    ctx = ExitStack()
    with ctx:
        arena = ctx.enter_context(nc.sbuf_tensor("arena", [P, 36800], F32))
        ring = ctx.enter_context(nc.sbuf_tensor("ring", [P, SLOTS, SLOT], F32))
        PS = ctx.enter_context(nc.psum_tensor("banks", [P, 8, BF], F32))

        def at(start, *shape):
            n = int(np.prod(shape))
            v = arena[:, start:start + n]
            names = "abcd"[:len(shape)]
            if len(shape) == 1:
                return v
            return v.rearrange(f"p ({' '.join(names)}) -> p {' '.join(names)}",
                               **{x: s for x, s in zip(names, shape)})

        hT = at(0, KC, TOK)
        XN = at(3072, NT, D)
        MG = at(3072, KC, TOK)
        ZA = at(6144, NT, ZA_W)
        ZG = at(8160, NT, ZG_W)
        QQ = at(10464, NT, 768)
        QAB = at(10464, 2, 2, TOK)
        VM = at(12768, 4, 512)
        CKT = at(14816, 2, NKEY)
        UKV = at(15840, 2, 2, 512)
        ZD = at(12768, NT, ZD_W)
        QM = at(17888, 2, TOK)
        SG1 = at(17888, 2, TOK)
        KT = at(18656, 2, NKEY)
        PB = at(19680, 2, 896)
        CQT = at(19680, 3, TOK)
        PT = at(21472, 2, 896)
        OT0 = at(23264, 4, TOK)
        OT1 = at(6144, 4, TOK)
        OT2 = at(8160, 4, TOK)
        XN2 = at(9696, NT, D)
        SQD = at(19680, 4, TOK)
        RSD = at(21472, 4, TOK)
        RT1 = at(24800, 640)
        RT2 = at(25440, 640)
        TMP = at(24800, 2, BF)
        SQG = at(3072, NT, 640)
        G1 = at(12768, 2, D)
        SG2 = at(14816, KC, TOK)
        CTX_CKV = at(26080, KVR)
        CTX_KPE = at(26336, ROPE)
        CTX_GK = at(26368, 128)
        CTX_GV = at(26496, 128)
        CTX_DK = at(26624, 512)
        CTX_DV = at(27136, 512)
        YS = at(9696, 2, D)
        CTMP = at(2048, 2, BF)
        SGE = at(3072, BF)
        AC = at(3584, BF)
        AT = at(4096, 4, P)
        DD = at(6144, NT, NE, CAP_S)
        DG = at(7680, NT, NE, CAP_S)
        DGT = at(4608, NG, NT * P)
        DGB = at(9216, NT * P)
        G2 = at(12768, 2, D)
        XB = at(14816, 2, KC, XW)
        AFT = at(24184, TOK)[0:NE]
        WK = at(24568, TOK)[0:NE]
        SN = at(24952, TOK)[0:NE]
        XE = at(17888, KC, NE, CAP)
        AFF = at(24032, NT, NE)
        POS = at(24080, NT, NE)
        LG = at(24128, NT, NE)
        M8 = at(24176, 8)[0:NE]
        EXTRA = [at(15840, SLOT),
                 at(25600, SLOT),
                 at(30720, SLOT),
                 at(0, SLOT)]
        FNG = at(11744, D)
        X = at(27648, NT, D)
        GNQ = at(30720, QR)
        GNK = at(31104, KVR)
        GGQ = at(31360, 64)
        GGK = at(31424, 64)
        MODR = at(31488, 1536)
        BR = at(33024, 1536)
        MODC = at(34560, 2, 48)
        AA = at(34656, 2, 2, KC)
        CST = at(34688, C_W)
        o = 34688 + C_W
        LAMV = at(o, 4, 64)
        NR = at(o + 256, P)[0:16]
        NCOL = at(o + 384, 2, KC)
        SUB = at(o + 400, 1)
        WR = at(o + 404, KC, NE)
        SC = at(o + 532, KC, 2)
        CR = NR
        SIGC = at(o + 548, 16)
        ST = at(o + 564, 3)
        RS = at(o + 568, 3)
        ST2 = at(o + 572, 6)
        R2 = at(o + 578, 6)
        STG = at(o + 584, 30)
        RG = at(o + 614, 30)
        MX = at(o + 644, 2, 3)
        NB = at(o + 650, 2, 3)
        SM = at(o + 656, 2, 3)
        RC = at(o + 662, 2, 3)
        LP = at(o + 668, 2, 64)
        LE = at(o + 796, 2)
        LAM = at(o + 798, 1)
        LIC = at(o + 799, 2)
        WARM = at(o + 865, 1)
        KPR = at(o + 801, 2, ROPE)
        assert o + 866 <= 36800
        IDT = CST[:, C_ID:C_ID + P]
        ONES = CST[:, C_ONE:C_ONE + P]
        IOTA = CST[:, C_IOTA:C_IOTA + CAP_S]

        def sem(name, per=0, base=0):
            return Signal(ctx.enter_context(nc.semaphore(name)), per, base)

        slots = [ring[:, i] for i in range(SLOTS)] + EXTRA
        before = [ATT_USES] * SLOTS + [0] * len(EXTRA)
        filled = [sem(f"filled{i}", 16 * (n + NE)) for i, n in enumerate(before)]
        used = [sem(f"used{i}", n + NE, 1) for i, n in enumerate(before)]

        def expert_use(l, i, g, e):
            return l * (before[i] + NE) + g * GE + (before[i] + e)

        const_in, cond_in, x_in = sem("const_in"), sem("cond_in"), sem("x_in")
        cond_t, cond_sig, cond_ok = sem("cond_t"), sem("cond_sig"), sem("cond_ok")
        early_in = sem("early_in", 6 * 16)
        late_in = sem("late_in", 18 * 16)
        ada_mm = sem("ada_mm", 1)
        mod_row, mod_col = sem("mod_row", 1), sem("mod_col", 1)
        mod_t = sem("mod_t", 2)
        ncol_ok, aa_ok = sem("ncol_ok", 1), sem("aa_ok", 2)
        ss_ok, root_ok, ms_ok, xn_ok = sem("ss_ok", 1), sem("root_ok", 1), sem("ms_ok", 1), sem("xn_ok", NT)
        ss_t, root_t, ms_t, xn_t = sem("ss_t", NT), sem("root_t", NT), sem("ms_t", NT), sem("xn_t", NT)
        h2_mm, h2_act, h2_dve = sem("h2_mm", 2), sem("h2_act", 2), sem("h2_dve", 2)
        ht_mm, ht_act, ht_dve = sem("ht_mm", 8), sem("ht_act", 4), sem("ht_dve", 4)
        user_mm = sem("user_mm", len(USERS))
        user_act, user_dve = sem("user_act", N_ACT_USERS), sem("user_dve", N_DVE_USERS)
        sq2_ok, ms2_ok, root2_ok, za_ok = sem("sq2_ok", 1), sem("ms2_ok", 1), sem("root2_ok", 1), sem("za_ok", 1)
        kpe_ok, qrope_ok = sem("kpe_ok", 1), sem("qrope_ok", 1)
        tr_mm, tr_act, tr_dve = sem("tr_mm", 3), sem("tr_act", 1), sem("tr_dve", 2)
        prep_mm, prep_act, prep_dve = sem("prep_mm", NJ), sem("prep_act", NJ), sem("prep_dve", key_preps(NJ - 1))
        score_mm, max_ok, exp_ok = sem("score_mm", len(MAPS)), sem("max_ok", len(MAPS)), sem("exp_ok", len(MAPS))
        prob_ok = sem("prob_ok", len(OUTS))
        pt_mm, pt_act, pt_dve = sem("pt_mm", len(OUTS)), sem("pt_act", len(OUTS)), sem("pt_dve", len(OUTS))
        sqg_ok, msg_ok, rootg_ok, rg_ok, gq_ok = (sem("sqg_ok", 1), sem("msg_ok", 1), sem("rootg_ok", 1),
                                                  sem("rg_ok", 1), sem("gq_ok", 1))
        zero_ok, dq_ok = sem("zero_ok", 1), sem("dq_ok", 1)
        lamp_ok, lame_ok = sem("lamp_ok", 1), sem("lame_ok", 1)
        stored_a, stored_g, stored_d = sem("stored_a", 32), sem("stored_g", 32), sem("stored_d", 32)
        sqd_ok, sqd_mm, msd_ok, rootd_ok, ot2_ok = (sem("sqd_ok", 1), sem("sqd_mm", 1), sem("msd_ok", 1),
                                                    sem("rootd_ok", 1), sem("ot2_ok", 1))
        gb_mm, gb_ok = sem("gb_mm", 2), sem("gb_ok", 2)
        x1_ok, xg_ok, silu_ok = sem("x1_ok", NT), sem("xg_ok", NT * NG, NT), sem("silu_ok", NE)
        router_mm, logit_ok, aexp_ok, aff_ok = (sem("router_mm", 1, 1), sem("logit_ok", 1), sem("aexp_ok", 1),
                                                sem("aff_ok", 1))
        aff_t, pos_ok, pos_t, disp_ok = sem("aff_t", 1), sem("pos_ok", 1), sem("pos_t", 1), sem("disp_ok", NT)
        gated_ok = sem("gated_ok", 1)
        gather_mm, gather_act, gather_dve = sem("gather_mm", 16), sem("gather_act", 8), sem("gather_dve", 8)
        dgt_mm, dgt_ok = sem("dgt_mm", 1), sem("dgt_ok", 1)
        xb_ok = sem("xb_ok", NE)
        gu_mm = sem("gu_mm", 2 * NE)
        sig_ok, ac_ok, at_mm, at_ok = sem("sig_ok", NE), sem("ac_ok", NE, 1), sem("at_mm", NE, 1), sem("at_ok", NE)
        y_mm, y_ok = sem("y_mm", NE), sem("y_ok", NE, 1)
        comb_mm, comb_ok, dgb_ok = sem("comb_mm", 6 * NG, 1), sem("comb_ok", 6 * NG, 1), sem("dgb_ok", NG)
        dve_chain, pool_chain = sem("dve_chain", DVE_LINKS), sem("pool_chain", POOL_LINKS)
        fn_in, y_out = sem("fn_in"), sem("y_out")
        fin_ss, fin_ms, fin_root, fin_rec, fin_ok = (sem("fin_ss"), sem("fin_ms"), sem("fin_root"), sem("fin_rec"),
                                                     sem("fin_ok"))

        def h2_pieces(n):
            for c in range(KC):
                for t in (0, 1) if n == 0 else (2,):
                    if n == 0:
                        bank, col = c // 2, 256 * (c % 2) + P * t
                    else:
                        bank, col = 4 + c // 2 % 2, 256 * (c // 4) + P * (c % 2)
                    yield c, min(t, 1), P * t, P * t + P, PS[:, bank, col:col + P]

        def h2_dve_chunk(c):
            return c // 2 % 2 == 1

        def gather_bank(c, stream):
            return PS[:, ((7, 2), (1, 3))[stream][c % 2]]

        passed = sem("passed")

        def apart(eng):
            eng.sem_inc(passed.s, 1)

        block = ctx.enter_context(nc.Block())

        @block.sync
        def _(sp):
            sp.dma_start(CST, a["constants"]).then_inc(const_in.s, 16)
            sp.dma_start(CR[0:8], a["c_ctx"].rearrange("(k p) -> k p", p=P)).then_inc(cond_in.s, 16)
            sp.dma_start(CR[8:16], a["c"].rearrange("b (k p) -> (b k) p", p=P)).then_inc(cond_in.s, 16)
            sp.dma_start(X[:, 0], a["x_prompt"].rearrange("b p d -> (b p) d")).then_inc(x_in.s, 16)
            sp.dma_start(X[:, 1:3], a["x_sample"].rearrange("b (t p) d -> p (b t) d", p=P)).then_inc(x_in.s, 16)
            w_ada = a["w_ada"].rearrange("l (k p) (i j n) -> l k i p j n", p=P, j=4, i=3)
            w_in = a["w_in"].rearrange("l (k p) n -> l p k n", p=P)
            w_uq = a["mla_w_uq"].rearrange("l (k p) n -> l p k n", p=P)
            w_br = [a[f"w_br_{n}"].rearrange("l (k p) n -> l p k n", p=P) for n in ("mla", "gqa", "diff")]
            w_out = a["w_out"].rearrange("l (k p) n -> l p k n", p=P)
            w_exp = [a[n].rearrange("l e (k p) n -> l e p k n", p=P) for n in ("w_gate", "w_up", "w_down")]

            def source(l, unit):
                kind, u = unit[0], unit[1]
                if kind == "ada":
                    return w_ada[l, unit[2], u]
                if kind == "c0":
                    return w_in[l, :, 2 * u:2 * u + 2, 0:ZA_W]
                if kind == "c1":
                    return w_in[l, :, 2 * u:2 * u + 2, ZA_W:ZA_W + ZG_W]
                if kind == "c2":
                    c = ZA_W + ZG_W + 768 * (u // 4)
                    return w_in[l, :, 2 * (u % 4):2 * (u % 4) + 2, c:c + 768]
                if kind == "uq":
                    return w_uq[l, :, 2 * u:min(2 * u + 2, 3), :]
                if kind.startswith("gate"):
                    c = ATT + D * int(kind[4]) + 256 * u
                    return w_in[l, :, :, c:c + 256]
                if kind.startswith("br"):
                    return w_br[int(kind[2])][l, :, :, 512 * u:512 * u + 512]
                return w_out[l, :, 2 * u:2 * u + 2, :]

            sp.wait_ge(cond_t.s, 1)
            with sp.Fori(0, DEPTH) as l:
                sp.wait_ge(router_mm.s, router_mm.at(l, 0))
                b_ada = a["b_ada"].rearrange("l (i j n) -> l j i n", i=3, j=4)
                for j in range(4):
                    sp.dma_start(BR[32 * j:32 * j + 2].rearrange("p (i n) -> p i n", i=3),
                                   b_ada[l, j].rearrange("(o i) n -> o i n", o=1).to_broadcast([2, 3, BF]))\
                        .then_inc(early_in.s, 16)
                sp.dma_start(NR[0:8], a["norm1"].rearrange("l (k p) -> l k p", p=P)[l]).then_inc(early_in.s, 16)
                sp.dma_start(NR[8:16], a["norm2"].rearrange("l (k p) -> l k p", p=P)[l]).then_inc(early_in.s, 16)
                for n, unit in enumerate(PLAN):
                    src = source(l, unit)
                    _, parts, cols = src.shape
                    dst = ring[:, n % SLOTS, 0:parts * cols].rearrange("p (k n) -> p k n", k=parts)
                    sp.wait_ge(used[n % SLOTS].s, used[n % SLOTS].at(l, n // SLOTS))
                    sp.dma_start(dst, src).then_inc(filled[n % SLOTS].s, 16)
                ready = {8: (user_dve, evacuated(USER_AT["br2", KC - 1])), 9: (x1_ok, NT), 10: (gb_mm, 2),
                         11: (router_mm, 1)}

                def experts(g, opening):
                    for e in range(GE):
                        for i in range(EXP_UNITS):
                            m, u = i // 4, i % 4
                            if type(g) is int:
                                src = w_exp[m][l, g * GE + e, :, 2 * u:2 * u + 2, :]
                            else:
                                src = w_exp[m][l, bass.ds(g * GE + e, 1), :, 2 * u:2 * u + 2, :]\
                                    .rearrange("e p k n -> (e p) k n")
                            sp.wait_ge(used[i].s, expert_use(l, i, g, e) + 1)
                            if opening and e == 0 and i in ready:
                                apart(sp)
                                signal, n = ready[i]
                                sp.wait_ge(signal.s, signal.at(l, n))
                            sp.dma_start(slots[i].rearrange("p (k n) -> p k n", k=2), src)\
                                .then_inc(filled[i].s, 16)

                experts(0, True)
                with sp.Fori(1, NG) as g:
                    experts(g, False)
            sp.dma_start(FNG, a["final_norm"].rearrange("(o n) -> o n", o=1).to_broadcast([P, D]))\
              .then_inc(fn_in.s, 16)
            sp.wait_ge(fin_ok.s, 1)
            sp.dma_start(a["y_prompt"].rearrange("b p d -> (b p) d"), XN[:, 0]).then_inc(y_out.s, 16)
            for t in range(1, NT):
                sp.wait_ge(fin_ok.s, t + 1)
                sp.dma_start(a["y_sample"].rearrange("b (t p) d -> t p (b d)", p=P)[t - 1], XN[:, t])\
                  .then_inc(y_out.s, 16)
            sp.wait_ge(y_out.s, 16 * NT)
            sp.wait_ge(stored_a.s, 32 * DEPTH)
            sp.wait_ge(stored_g.s, 32 * DEPTH)
            sp.wait_ge(stored_d.s, 32 * DEPTH)

        @block.gpsimd
        def _(pool):
            links = [0]

            def link(ins, l):
                links[0] += 1
                ins.then_inc(pool_chain.s, 1)
                pool.wait_ge(pool_chain.s, pool_chain.at(l, links[0]))

            def rotate(l, z, heads, width, t):
                c0 = C_COS + 192 * t + (0 if width == 64 else 128)
                half = width // 4
                cos = CST[:, c0:c0 + width].rearrange("p (o n) -> p o n", o=1).to_broadcast([P, heads, width])
                sin = CST[:, c0 + width:c0 + 2 * width].rearrange("p (x h n) -> p x h n", x=2, h=2)
                t1 = RT1[:, 0:heads * width].rearrange("p (a n) -> p a n", a=heads)
                t2 = RT2[:, 0:heads * width].rearrange("p (a n) -> p a n", a=heads)
                t2v = RT2[:, 0:heads * width].rearrange("p (a x h n) -> p a x h n", a=heads, x=2, h=2)
                pool.tensor_tensor(t1, z, cos, ALU.mult)
                for h in range(2):
                    for x in range(2):
                        src = z[:, :, (2 * x + 1 - h) * half:(2 * x + 2 - h) * half]
                        sx = sin[:, x, h, :].rearrange("p (o n) -> p o n", o=1).to_broadcast([P, heads, half])
                        ins = pool.tensor_tensor(t2v[:, :, x, h, :], src, sx, ALU.mult)
                link(ins, l)
                return pool.tensor_tensor(z, t1, t2, ALU.add)

            def row(ap, n):
                return ap.rearrange("(o n) -> o n", o=1).to_broadcast([P, n])

            pool.wait_ge(const_in.s, 16)
            with pool.Fori(0, DEPTH) as l:
                links[0] = 0
                pool.wait_ge(ada_mm.s, ada_mm.at(l, 1))
                apart(pool)
                for dst, name, n in ((GNQ, "mla_q_norm", QR), (GNK, "mla_kv_norm", KVR), (GGQ, "gqa_q_norm", 64),
                                     (GGK, "gqa_k_norm", 64), (LAMV[:, 0], "diff_lam_q1", 64),
                                     (LAMV[:, 1], "diff_lam_q2", 64), (LAMV[:, 2], "diff_lam_k1", 64),
                                     (LAMV[:, 3], "diff_lam_k2", 64)):
                    pool.dma_start(dst, row(a[name][l], n)).then_inc(late_in.s, 16)
                pool.dma_start(SUB, a["diff_subln"][l].rearrange("(p o) -> p o", o=1)).then_inc(late_in.s, 16)
                pool.dma_start(WR, a["w_router"].rearrange("l (k p) e -> l p k e", p=P)[l]).then_inc(late_in.s, 16)
                for m, name in enumerate(("mla_w_uk", "mla_w_uv")):
                    pool.dma_start(UKV[:, m], a[name].rearrange("l (k p) h d -> l p k (h d)", p=P)[l])\
                        .then_inc(late_in.s, 16)
                for dst, name, form in ((CTX_CKV, "cache_mla_ckv", "b l p r -> l (b p) r"),
                                        (CTX_KPE, "cache_mla_kpe", "b l p r -> l (b p) r"),
                                        (CTX_GK, "cache_gqa_k", "b l p h d -> l (b p) (h d)"),
                                        (CTX_GV, "cache_gqa_v", "b l p h d -> l (b p) (h d)"),
                                        (CTX_DK, "cache_diff_k", "b l p h d -> l (b p) (h d)"),
                                        (CTX_DV, "cache_diff_v", "b l p h d -> l (b p) (h d)")):
                    pool.dma_start(dst, a[name].rearrange(form)[l]).then_inc(late_in.s, 16)
                pool.wait_ge(user_act.s, user_act.at(l, evacuated(USER_AT["c0", 2, 1])))
                for t in range(2):
                    apart(pool)
                    link(pool.tensor_copy(KPR[:, t:t + 1], ZA[:, 1 + t:2 + t, Z_PE:Z_PE + ROPE]), l)
                    ins = rotate(l, KPR[:, t:t + 1], 1, ROPE, t)
                    if t == 0:
                        link(ins, l)
                    else:
                        ins.then_inc(kpe_ok.s, 1)
                pool.wait_ge(za_ok.s, za_ok.at(l, 1))
                apart(pool)
                pool.dma_start(a["new_ckv"].rearrange("b l p r -> l (b p) r")[l],
                               ZA[:, 0, Z_KV:Z_KV + KVR]).then_inc(stored_a.s, 16)
                pool.dma_start(a["new_kpe"].rearrange("b l p r -> l (b p) r")[l],
                               ZA[:, 0, Z_PE:Z_PE + ROPE]).then_inc(stored_a.s, 16)
                pool.wait_ge(user_act.s, user_act.at(l, evacuated(USER_AT["q", 2, 1])))
                pool.wait_ge(kpe_ok.s, kpe_ok.at(l, 1))
                for t in range(2):
                    z = QQ[:, 1 + t].rearrange("p (h d) -> p h d", h=8)[:, :, NOPE:QD]
                    ins = rotate(l, z, 8, ROPE, t)
                    if t == 0:
                        link(ins, l)
                    else:
                        ins.then_inc(qrope_ok.s, 1)
                pool.wait_ge(rg_ok.s, rg_ok.at(l, 1))
                pool.wait_ge(qrope_ok.s, qrope_ok.at(l, 1))
                for t in range(NT):
                    z = ZG[:, t, 0:640].rearrange("p (h d) -> p h d", h=10)
                    rg = RG[:, 10 * t:10 * t + 10].rearrange("p (h o) -> p h o", o=1).to_broadcast([P, 10, 64])
                    link(pool.tensor_tensor(z, z, rg, ALU.mult), l)
                    pool.tensor_tensor(z[:, 0:8], z[:, 0:8],
                                       GGQ.rearrange("p (o n) -> p o n", o=1).to_broadcast([P, 8, 64]), ALU.mult)
                    link(pool.tensor_tensor(z[:, 8:10], z[:, 8:10],
                                            GGK.rearrange("p (o n) -> p o n", o=1).to_broadcast([P, 2, 64]),
                                            ALU.mult), l)
                    if t >= 1:
                        ins = rotate(l, z, 10, 64, t - 1)
                        if t == 1:
                            link(ins, l)
                        else:
                            ins.then_inc(gq_ok.s, 1)
                pool.wait_ge(gq_ok.s, gq_ok.at(l, 1))
                apart(pool)
                pool.dma_start(a["new_gk"].rearrange("b l p h d -> l (b p) (h d)")[l],
                               ZG[:, 0, G_K:G_K + 128]).then_inc(stored_g.s, 16)
                pool.dma_start(a["new_gv"].rearrange("b l p h d -> l (b p) (h d)")[l],
                               ZG[:, 0, G_V:G_V + 128]).then_inc(stored_g.s, 16)
                pool.wait_ge(prep_mm.s, prep_mm.at(l, 8))
                apart(pool)
                pool.memset(QAB[64:128, :, 0], 0.0)
                pool.memset(QAB[0:64, :, 1], 0.0).then_inc(zero_ok.s, 1)
                pool.wait_ge(user_act.s, user_act.at(l, evacuated(USER_AT["c2", 11])))
                for t in range(2):
                    for part in range(2):
                        z = ZD[:, 1 + t, 512 * part:512 * part + 512].rearrange("p (h d) -> p h d", h=8)
                        ins = rotate(l, z, 8, 64, t)
                        if (t, part) != (1, 1):
                            link(ins, l)
                        else:
                            ins.then_inc(dq_ok.s, 1)
                pool.dma_start(a["new_dk"].rearrange("b l p h d -> l (b p) (h d)")[l],
                               ZD[:, 0, D_K:D_K + 512]).then_inc(stored_d.s, 16)
                pool.dma_start(a["new_dv"].rearrange("b l p h d -> l (b p) (h d)")[l],
                               ZD[:, 0, D_V:D_V + 512]).then_inc(stored_d.s, 16)
                assert links[0] == POOL_LINKS, ("POOL_LINKS", links[0])

        @block.scalar
        def _(act):
            def norm_root(l):
                for t in range(NT):
                    act.wait_ge(xg_ok.s, xg_ok.at(l, t + 1 - NT))
                    ins = nc.scalar.activation(XN[:, t], X[:, t], ACT.Square, accum_out=ST[:, t:t + 1])
                ins.then_inc(ss_ok.s, 1)
                act.wait_ge(ms_ok.s, ms_ok.at(l, 1))
                nc.scalar.activation(RS, RS, ACT.Sqrt).then_inc(root_ok.s, 1)

            def ht_even(l):
                for c in range(0, KC, 2):
                    act.wait_ge(ht_mm.s, ht_mm.at(l, c + 1))
                    ps = PS[:, 4 + c % 4]
                    for s, lo, hi in ((0, 0, P), (1, P, TOK)):
                        ins = nc.scalar.activation(hT[:, c, lo:hi], ps[:, lo:hi], ACT.Identity,
                                                   scale=AA[:, 0, s, c:c + 1], bias=MODC[:, s, c:c + 1])
                    ins.then_inc(ht_act.s, 1)

            def h2_out(l, n):
                act.wait_ge(h2_mm.s, h2_mm.at(l, n + 1))
                for c, s, lo, hi, ps in h2_pieces(n):
                    if not h2_dve_chunk(c):
                        ins = nc.scalar.activation(hT[:, c, lo:hi], ps, ACT.Identity, scale=AA[:, 1, s, c:c + 1],
                                                   bias=MODC[:, s, 24 + c:25 + c])
                ins.then_inc(h2_act.s, 1)

            def user(l, key, write):
                n = USER_AT[key]
                act.wait_ge(user_mm.s, user_mm.at(l, n + 1))
                write(PS[:, 6 + n % 2]).then_inc(user_act.s, 1)

            def exps(l, j):
                kind, _ = JOBS[j]
                for m in range(1 if kind == "mla" else 2):
                    n = MAP_AT[j, m]
                    act.wait_ge(max_ok.s, max_ok.at(l, n + 1))
                    if n >= 2:
                        before = MAPS[n - 2]
                        act.wait_ge(pt_mm.s, pt_mm.at(l, OUT_AT.get(before, OUT_AT[before[0], 0]) + 1))
                    b = n % 2
                    for r, (lo, hi, bank, c) in enumerate(((0, 384, 0, 0), (384, 512, 0, 384), (512, 896, 1, 0))):
                        ins = nc.scalar.activation(PB[:, b, lo:hi], PS[:, 2 * m + bank, c:c + hi - lo], ACT.Exp,
                                                   scale=SCALE[kind], bias=NB[:, b, r:r + 1],
                                                   accum_out=SM[:, b, r:r + 1])
                    ins.then_inc(exp_ok.s, 1)

            def prep(l, j):
                kind, i = JOBS[j]
                act.wait_ge(prep_mm.s, prep_mm.at(l, j + 1))
                if kind == "mla":
                    ins = nc.scalar.copy(QM[0:QD, j % 2], PS[0:QD, 5, 0:TOK])
                else:
                    ins = nc.scalar.copy(QAB[0:64, j % 2, 0], PS[0:64, 5, 0:TOK])
                ins.then_inc(prep_act.s, 1)

            def values(l, j):
                kind, i = JOBS[j]
                if not values_of(j):
                    return
                n = USER_AT["pv", j]
                ps = PS[:, 6 + n % 2]
                act.wait_ge(user_mm.s, user_mm.at(l, n + 1))
                if kind == "mla":
                    ins = nc.scalar.copy(OT0[:, i // 2], ps[:, 0:TOK])
                elif kind == "gqa":
                    if i == 0:
                        act.wait_ge(stored_a.s, stored_a.at(l, 32))
                    ins = nc.scalar.copy(OT1[:, i], ps[:, 0:TOK])
                else:
                    if i == 0:
                        act.wait_ge(stored_g.s, stored_g.at(l, 32))
                    ins = nc.scalar.copy(OT2[:, i], ps[:, 0:TOK])
                ins.then_inc(user_act.s, 1)

            def fill(l, key):
                kind = key[0]
                if kind == "c1":
                    user(l, key, lambda ps: nc.scalar.copy(ZG[:, key[1], 384 * key[2]:384 * key[2] + 384],
                                                           ps[:, 0:384]))
                elif kind == "c2":
                    half, t, q = key[1] // 6, key[1] % 6 // 2, key[1] % 2
                    c = 768 * half + 384 * q
                    user(l, key, lambda ps: nc.scalar.copy(ZD[:, t, c:c + 384], ps[:, 0:384]))
                elif kind == "gate0":
                    user(l, key, lambda ps: nc.scalar.activation(MG[:, key[1]], ps[:, 0:TOK], ACT.Tanh, scale=0.5))
                elif kind == "gate1":
                    if key[1] >= 2:
                        act.wait_ge(user_dve.s, user_dve.at(l, evacuated(USER_AT["br1", key[1] - 2])))
                    user(l, key, lambda ps: nc.scalar.activation(SG1[:, key[1] % 2], ps[:, 0:TOK], ACT.Tanh,
                                                                 scale=0.5))
                elif kind == "gate2":
                    user(l, key, lambda ps: nc.scalar.activation(SG2[:, key[1]], ps[:, 0:TOK], ACT.Tanh, scale=0.5))

            act.sem_inc(y_ok.s, 1)
            act.wait_ge(cond_t.s, 1)
            nc.scalar.activation(SIGC, PS[:, 0, 0:16], ACT.Sigmoid).then_inc(cond_sig.s, 1)
            act.wait_ge(x_in.s, 32)
            with act.Fori(0, DEPTH) as l:
                norm_root(l)
                act.wait_ge(aa_ok.s, aa_ok.at(l, 1))
                ht_even(l)
                for t in range(NT):
                    for h in range(2):
                        user(l, ("c0", t, h), lambda ps: nc.scalar.copy(ZA[:, t, 336 * h:336 * h + 336],
                                                                        ps[:, 0:336]))
                    act.wait_ge(user_act.s, user_act.at(l, evacuated(USER_AT["c0", t, 1])))
                    nc.scalar.activation(SQG[:, t, 0:QR], ZA[:, t, 0:QR], ACT.Square, accum_out=ST2[:, t:t + 1])
                    ins = nc.scalar.activation(SQG[:, t, QR:640], ZA[:, t, Z_KV:Z_KV + KVR], ACT.Square,
                                               accum_out=ST2[:, 3 + t:4 + t])
                ins.then_inc(sq2_ok.s, 1)
                act.wait_ge(ms2_ok.s, ms2_ok.at(l, 1))
                nc.scalar.activation(R2, R2, ACT.Sqrt).then_inc(root2_ok.s, 1)
                for h in range(2):
                    fill(l, ("c1", 0, h))
                act.wait_ge(tr_mm.s, tr_mm.at(l, 1))
                nc.scalar.copy(CQT, PS[:, 0:3, 0:TOK]).then_inc(tr_act.s, 1)
                for t in range(NT):
                    for h in range(2):
                        user(l, ("q", t, h), lambda ps: nc.scalar.copy(QQ[:, t, 384 * h:384 * h + 384],
                                                                       ps[:, 0:384]))
                act.wait_ge(lamp_ok.s, lamp_ok.at(l, 1))
                nc.scalar.activation(LE, LE, ACT.Exp).then_inc(lame_ok.s, 1)
                prep(l, 0)
                for i in range(NJ + 1):
                    if i < NJ:
                        exps(l, i)
                    if i + 1 < NJ:
                        prep(l, i + 1)
                    if i >= 1:
                        values(l, i - 1)
                    if i == 2:
                        act.wait_ge(msg_ok.s, msg_ok.at(l, 1))
                        nc.scalar.activation(RG, RG, ACT.Sqrt).then_inc(rootg_ok.s, 1)
                    for key in FILL[i]:
                        fill(l, key)
                    if i == 1:
                        act.wait_ge(user_act.s, user_act.at(l, evacuated(USER_AT["c1", 2, 1])))
                        nc.scalar.activation(SQG, ZG[:, :, 0:640], ACT.Square).then_inc(sqg_ok.s, 1)
                    if i < NJ:
                        for m in range(2 if JOBS[i][0] == "gqa" else 1):
                            n = OUT_AT[i, m]
                            act.wait_ge(pt_mm.s, pt_mm.at(l, n + 1))
                            if n >= 2:
                                act.wait_ge(user_mm.s, user_mm.at(l, values_user(OUTS[n - 2][0]) + 1))
                            nc.scalar.copy(PT[:, n % 2, 0:384], PS[:, 4, 0:384]).then_inc(pt_act.s, 1)
                act.wait_ge(user_act.s, user_act.at(l, evacuated(USER_AT["pv", NJ - 1])))
                nc.scalar.activation(SQD, OT2, ACT.Square).then_inc(sqd_ok.s, 1)
                act.wait_ge(stored_d.s, stored_d.at(l, 32))
                for c in range(KC):
                    fill(l, ("gate2", c))
                    if c == 2:
                        act.wait_ge(msd_ok.s, msd_ok.at(l, 1))
                        nc.scalar.activation(RSD, RSD, ACT.Sqrt).then_inc(rootd_ok.s, 1)
                act.wait_ge(gb_mm.s, gb_mm.at(l, 1))
                nc.scalar.mul(G1, PS[:, 0:4, :].rearrange("p (s h) n -> p s (h n)", s=2), 0.5).then_inc(gb_ok.s, 1)
                act.wait_ge(aa_ok.s, aa_ok.at(l, 2))
                for t in range(NT):
                    act.wait_ge(x1_ok.s, x1_ok.at(l, t + 1))
                    nc.scalar.activation(XN2[:, t], X[:, t], ACT.Square, accum_out=ST[:, t:t + 1])\
                        .then_inc(ss_t.s, 1)
                    act.wait_ge(ms_t.s, ms_t.at(l, t + 1))
                    nc.scalar.activation(RS[:, t:t + 1], RS[:, t:t + 1], ACT.Sqrt).then_inc(root_t.s, 1)
                    if t == 1:
                        h2_out(l, 0)
                nc.scalar.activation(WARM, AA[:, 1, 0, 0:1], ACT.Exp, scale=0.0)
                h2_out(l, 1)
                act.wait_ge(logit_ok.s, logit_ok.at(l, 1))
                nc.scalar.activation(LG, LG, ACT.Exp).then_inc(aexp_ok.s, 1)
                act.wait_ge(gb_mm.s, gb_mm.at(l, 2))
                nc.scalar.copy(G2, PS[:, 4:8, :].rearrange("p (s h) n -> p s (h n)", s=2)).then_inc(gb_ok.s, 1)
                nc.scalar.activation(WARM, AA[:, 1, 0, 0:1], ACT.Sigmoid, scale=0.0)
                for c in range(KC):
                    n = 2 * c
                    act.wait_ge(gather_mm.s, gather_mm.at(l, n + 1))
                    nc.scalar.activation(XE[:, c, :, 0:CAP_S],
                                         gather_bank(c, 1).rearrange("p (e s) -> p e s", e=NE), ACT.Identity,
                                         scale=AA[:, 1, 1, c:c + 1], bias=MODC[:, 1, 24 + c:25 + c])\
                        .then_inc(gather_act.s, 1)
                with act.Fori(0, NG) as g:
                    for e in range(GE):
                        act.wait_ge(gu_mm.s, gu_mm.in_group(l, g, 2 * e + 1))
                        act.wait_ge(ac_ok.s, ac_ok.in_group(l, g, e))
                        nc.scalar.activation(SGE, PS[:, e % 2], ACT.Sigmoid).then_inc(sig_ok.s, 1)
                        act.wait_ge(at_mm.s, at_mm.in_group(l, g, e + 1))
                        nc.scalar.copy(AT, PS[:, 4].rearrange("p (q n) -> p q n", q=4)).then_inc(at_ok.s, 1)
                        act.wait_ge(y_mm.s, y_mm.in_group(l, g, e + 1))
                        if e == 0:
                            act.wait_ge(comb_mm.s, comb_mm.in_group(l, g, 0))
                        for h in range(2):
                            nc.scalar.copy(YS[32 * e:32 * e + 32, 0, BF * h:BF * h + BF],
                                           PS[64 * h:64 * h + 32, 5])
                            ins = nc.scalar.copy(YS[32 * e:32 * e + 16, 1, BF * h:BF * h + BF],
                                                 PS[64 * h + 32:64 * h + 48, 5])
                        ins.then_inc(y_ok.s, 1)
                nc.scalar.activation(WARM, AA[:, 1, 0, 0:1], ACT.Sqrt, scale=0.0)
            for t in range(NT):
                act.wait_ge(xg_ok.s, DEPTH * NT * NG + t + 1)
                nc.scalar.activation(XN[:, t], X[:, t], ACT.Square, accum_out=ST[:, t:t + 1]).then_inc(fin_ss.s, 1)
            for t in range(NT):
                act.wait_ge(fin_ms.s, t + 1)
                nc.scalar.activation(RS[:, t:t + 1], RS[:, t:t + 1], ACT.Sqrt).then_inc(fin_root.s, 1)

        @block.vector
        def _(dve):
            links = [0]

            def link(ins, l):
                links[0] += 1
                ins.then_inc(dve_chain.s, 1)
                dve.wait_ge(dve_chain.s, dve_chain.at(l, links[0]))

            def norm_rows(l):
                dve.wait_ge(ss_ok.s, ss_ok.at(l, 1))
                nc.vector.tensor_scalar(RS, ST, 1.0 / D, EPS, ALU.mult, ALU.add).then_inc(ms_ok.s, 1)
                dve.wait_ge(root_ok.s, root_ok.at(l, 1))
                link(nc.vector.reciprocal(RS, RS), l)
                for t in range(NT):
                    nc.vector.tensor_scalar(XN[:, t], X[:, t], RS[:, t:t + 1], None, ALU.mult).then_inc(xn_ok.s, 1)

            def ht_odd(l):
                for c in range(1, KC, 2):
                    dve.wait_ge(ht_mm.s, ht_mm.at(l, c + 1))
                    ps = PS[:, 4 + c % 4]
                    for s, lo, hi in ((0, 0, P), (1, P, TOK)):
                        ins = nc.vector.tensor_scalar(hT[:, c, lo:hi], ps[:, lo:hi], AA[:, 0, s, c:c + 1],
                                                      MODC[:, s, c:c + 1], ALU.mult, ALU.add)
                    ins.then_inc(ht_dve.s, 1)

            def h2_out(l, n):
                dve.wait_ge(h2_mm.s, h2_mm.at(l, n + 1))
                for c, s, lo, hi, ps in h2_pieces(n):
                    if h2_dve_chunk(c):
                        ins = nc.vector.tensor_scalar(hT[:, c, lo:hi], ps, AA[:, 1, s, c:c + 1],
                                                      MODC[:, s, 24 + c:25 + c], ALU.mult, ALU.add)
                ins.then_inc(h2_dve.s, 1)

            def modulation(l, key):
                kind, i = key
                n = USER_AT[key]
                dve.wait_ge(user_mm.s, user_mm.at(l, n + 1))
                ins = (mod_rows if kind == "ada" else mod_cols)(PS[:, 6 + n % 2], i)
                ins.then_inc(user_dve.s, 1)
                if key == ("adat", 2):
                    dve.wait_ge(user_dve.s, user_dve.at(l, evacuated(n)))
                    gain_scale(1).then_inc(aa_ok.s, 1)

            def mod_rows(ps, i):
                for j in range(4):
                    r = slice(32 * j, 32 * j + 2)
                    ins = nc.vector.tensor_tensor(MODR[r, BF * i:BF * i + BF], ps[r], BR[r, BF * i:BF * i + BF],
                                                  ALU.add)
                return ins

            def mod_cols(ps, i):
                for s in range(2):
                    src = ps.rearrange("p (q j r) -> p j q r", q=4, j=4)[:, :, :, s]
                    dst = MODC[:, s, 16 * i:16 * i + 16].rearrange("p (j q) -> p j q", j=4)
                    ins = nc.vector.tensor_copy(dst, src)
                return ins

            def gain_scale(n):
                for s in range(2):
                    ins = nc.vector.scalar_tensor_tensor(out=AA[:, n, s], in0=MODC[:, s, 24 * n + 8:24 * n + 16],
                                                         scalar=1.0, in1=NCOL[:, n], op0=ALU.add, op1=ALU.mult)
                return ins

            def maxima(l, j):
                kind, _ = JOBS[j]
                for m in range(1 if kind == "mla" else 2):
                    n = MAP_AT[j, m]
                    b = n % 2
                    dve.wait_ge(score_mm.s, score_mm.at(l, n + 1))
                    if n >= 2:
                        dve.wait_ge(exp_ok.s, exp_ok.at(l, n - 1))
                    for r, (w, bank, c) in enumerate(((384, 0, 0), (128, 0, 384), (384, 1, 0))):
                        ins = nc.vector.reduce_max(MX[:, b, r:r + 1], PS[:, 2 * m + bank, c:c + w], AX)
                    link(ins, l)
                    nc.vector.tensor_scalar(NB[:, b], MX[:, b], -SCALE[kind], None, ALU.mult).then_inc(max_ok.s, 1)

            def prep(l, j):
                kind, i = JOBS[j]
                if kind == "mla" and i % 2:
                    return
                dve.wait_ge(prep_mm.s, prep_mm.at(l, j + 1))
                if kind == "mla":
                    nc.vector.tensor_copy(KT[0:NOPE, 0], PS[0:NOPE, 4])
                    ins = nc.vector.tensor_copy(KT[0:NOPE, 1], PS[64:64 + NOPE, 4])
                else:
                    if kind == "diff":
                        nc.vector.tensor_copy(KT[:, j % 2], PS[:, 4])
                    elif i == 0:
                        for g in range(2):
                            for r in range(2):
                                nc.vector.tensor_copy(KT[64 * r:64 * r + 64, g], PS[64 * g:64 * g + 64, 4])
                    ins = nc.vector.tensor_copy(QAB[64:128, j % 2, 1], PS[64:128, 5, 0:TOK])
                ins.then_inc(prep_dve.s, 1)

            def normalise(l, j):
                kind, _ = JOBS[j]
                rows = ((0, 384), (384, 512), (512, 896))
                for m in range(1 if kind == "mla" else 2):
                    n = MAP_AT[j, m]
                    b = n % 2
                    dve.wait_ge(exp_ok.s, exp_ok.at(l, n + 1))
                    link(nc.vector.reciprocal(RC[:, b], SM[:, b]), l)
                    if kind == "diff" and m == 1:
                        link(nc.vector.tensor_scalar(RC[:, b], RC[:, b], LAM, None, ALU.mult), l)
                        for r, (lo, hi) in enumerate(rows):
                            ins = nc.vector.scalar_tensor_tensor(
                                out=PB[:, 0, lo:hi], in0=PB[:, 1, lo:hi], scalar=RC[:, b, r:r + 1],
                                in1=PB[:, 0, lo:hi], op0=ALU.mult, op1=ALU.add)
                    else:
                        for r, (lo, hi) in enumerate(rows):
                            ins = nc.vector.tensor_scalar(PB[:, b, lo:hi], PB[:, b, lo:hi], RC[:, b, r:r + 1],
                                                          None, ALU.mult)
                    if kind == "diff" and m == 0:
                        link(ins, l)
                    else:
                        ins.then_inc(prob_ok.s, 1)

            def branch(l, key):
                kind, c = key
                n = USER_AT[key]
                dve.wait_ge(user_mm.s, user_mm.at(l, n + 1))
                dve.wait_ge(user_act.s, user_act.at(l, evacuated(USER_AT["gate" + kind[2], c])))
                ps = PS[:, 6 + n % 2, 0:TOK]
                gate = {"br0": MG[:, c], "br1": SG1[:, c % 2], "br2": SG2[:, c]}[kind]
                if kind == "br0":
                    nc.vector.scalar_tensor_tensor(out=gate, in0=gate, scalar=1.0, in1=ps, op0=ALU.add,
                                                   op1=ALU.mult).then_inc(user_dve.s, 1)
                else:
                    link(nc.vector.scalar_tensor_tensor(out=gate, in0=gate, scalar=1.0, in1=ps, op0=ALU.add,
                                                        op1=ALU.mult), l)
                    nc.vector.tensor_tensor(MG[:, c], MG[:, c], gate, ALU.add).then_inc(user_dve.s, 1)

            for free in (xg_ok, ac_ok, comb_ok):
                dve.sem_inc(free.s, free.base)
            dve.wait_ge(const_in.s, 16)
            dve.wait_ge(cond_sig.s, 1)
            nc.vector.tensor_tensor(SC.rearrange("p k s -> p s k"),
                                    PS[:, 0, 0:16].rearrange("p (s k) -> p s k", s=2),
                                    SIGC.rearrange("p (s k) -> p s k", s=2), ALU.mult).then_inc(cond_ok.s, 1)
            with dve.Fori(0, DEPTH) as l:
                links[0] = 0
                nc.vector.memset(MODR, 0.0)
                norm_rows(l)
                dve.wait_ge(mod_t.s, mod_t.at(l, 1))
                nc.vector.tensor_copy(NCOL, PS[:, 3, 0:16].rearrange("p (n k) -> p n k", n=2)).then_inc(ncol_ok.s, 1)

                dve.wait_ge(early_in.s, early_in.at(l, 96))
                dve.wait_ge(ada_mm.s, ada_mm.at(l, 1))
                mod_rows(PS[:, 0], 0).then_inc(mod_row.s, 1)
                dve.wait_ge(mod_t.s, mod_t.at(l, 2))
                mod_cols(PS[:, 3], 0).then_inc(mod_col.s, 1)
                dve.wait_ge(mod_col.s, mod_col.at(l, 1))
                gain_scale(0).then_inc(aa_ok.s, 1)
                dve.wait_ge(aa_ok.s, aa_ok.at(l, 1))
                ht_odd(l)
                dve.wait_ge(late_in.s, late_in.at(l, 18 * 16))
                dve.wait_ge(sq2_ok.s, sq2_ok.at(l, 1))
                nc.vector.tensor_scalar(R2[:, 0:3], ST2[:, 0:3], 1.0 / QR, EPS, ALU.mult, ALU.add)
                nc.vector.tensor_scalar(R2[:, 3:6], ST2[:, 3:6], 1.0 / KVR, EPS, ALU.mult, ALU.add)\
                    .then_inc(ms2_ok.s, 1)
                dve.wait_ge(root2_ok.s, root2_ok.at(l, 1))
                link(nc.vector.reciprocal(R2, R2), l)
                for t in range(NT):
                    for col, w, gain, r in ((0, QR, GNQ, t), (Z_KV, KVR, GNK, 3 + t)):
                        z = ZA[:, t, col:col + w]
                        ins = nc.vector.scalar_tensor_tensor(out=z, in0=z, scalar=R2[:, r:r + 1], in1=gain,
                                                             op0=ALU.mult, op1=ALU.mult)
                ins.then_inc(za_ok.s, 1)
                link(nc.vector.tensor_tensor(LP, LAMV[:, 0:2], LAMV[:, 2:4], ALU.mult), l)
                nc.vector.reduce_sum(LE, LP, AX).then_inc(lamp_ok.s, 1)
                nc.vector.tensor_copy(LIC, CST[:, bass.ds(l * 2 + C_LAM, 2)])
                dve.wait_ge(tr_mm.s, tr_mm.at(l, 2))
                nc.vector.tensor_copy(CKT, PS[:, 3:5, :]).then_inc(tr_dve.s, 1)
                dve.wait_ge(tr_mm.s, tr_mm.at(l, 3))
                nc.vector.tensor_copy(KT[NOPE:QD, 0], PS[0:ROPE, 5])
                nc.vector.tensor_copy(KT[NOPE:QD, 1], PS[0:ROPE, 5]).then_inc(tr_dve.s, 1)
                for t in range(4):
                    n = USER_AT["v", t]
                    dve.wait_ge(user_mm.s, user_mm.at(l, n + 1))
                    nc.vector.tensor_copy(VM[:, t], PS[:, 6 + n % 2]).then_inc(user_dve.s, 1)
                dve.wait_ge(lame_ok.s, lame_ok.at(l, 1))
                link(nc.vector.tensor_tensor(LAM, LE[:, 1:2], LE[:, 0:1], ALU.subtract), l)
                link(nc.vector.tensor_tensor(LAM, LAM, LIC[:, 0:1], ALU.subtract), l)
                nc.vector.tensor_tensor(SUB, SUB, LIC[:, 1:2], ALU.mult)
                prep(l, 0)
                for i in range(NJ + 1):
                    if i < NJ:
                        maxima(l, i)
                    if i + 1 < NJ:
                        prep(l, i + 1)
                    if i < NJ:
                        normalise(l, i)
                    if i == 2:
                        dve.wait_ge(sqg_ok.s, sqg_ok.at(l, 1))
                        link(nc.vector.reduce_sum(STG, SQG.rearrange("p t (h d) -> p (t h) d", d=64), AX), l)
                        nc.vector.tensor_scalar(RG, STG, 1.0 / 64, EPS, ALU.mult, ALU.add).then_inc(msg_ok.s, 1)
                        dve.wait_ge(rootg_ok.s, rootg_ok.at(l, 1))
                        nc.vector.reciprocal(RG, RG).then_inc(rg_ok.s, 1)
                    for key in FILL[i]:
                        if key[0] in ("br0", "br1"):
                            branch(l, key)
                        elif key[0] in ("ada", "adat"):
                            modulation(l, key)
                    if i < NJ:
                        for m in range(2 if JOBS[i][0] == "gqa" else 1):
                            n = OUT_AT[i, m]
                            dve.wait_ge(pt_mm.s, pt_mm.at(l, n + 1))
                            if n >= 2:
                                dve.wait_ge(user_mm.s, user_mm.at(l, values_user(OUTS[n - 2][0]) + 1))
                            nc.vector.tensor_copy(PT[:, n % 2, 384:896], PS[:, 5]).then_inc(pt_dve.s, 1)
                dve.wait_ge(sqd_mm.s, sqd_mm.at(l, 1))
                nc.vector.tensor_scalar(RSD, PS[:, 0:4, 0:TOK], 1.0 / 128, EPS, ALU.mult, ALU.add)\
                    .then_inc(msd_ok.s, 1)
                dve.wait_ge(rootd_ok.s, rootd_ok.at(l, 1))
                link(nc.vector.reciprocal(RSD, RSD), l)
                nc.vector.scalar_tensor_tensor(out=OT2, in0=OT2, scalar=SUB, in1=RSD, op0=ALU.mult,
                                               op1=ALU.mult).then_inc(ot2_ok.s, 1)
                for c in range(KC):
                    branch(l, ("br2", c))
                dve.wait_ge(gb_ok.s, gb_ok.at(l, 1))
                for t in range(NT):
                    for h in range(2):
                        n = USER_AT["out", t, h]
                        dve.wait_ge(user_mm.s, user_mm.at(l, n + 1))
                        x = X[:, t, BF * h:BF * h + BF]
                        nc.vector.tensor_tensor(TMP[:, h], PS[:, 6 + n % 2], G1[:, min(t, 1), BF * h:BF * h + BF],
                                                ALU.mult).then_inc(user_dve.s, 1)
                        dve.wait_ge(user_dve.s, user_dve.at(l, evacuated(n)))
                        ins = nc.vector.tensor_tensor(x, x, TMP[:, h], ALU.add)
                        if (t, h) == (2, 0):
                            h2_out(l, 0)
                    ins.then_inc(x1_ok.s, 1)
                    dve.wait_ge(ss_t.s, ss_t.at(l, t + 1))
                    r = RS[:, t:t + 1]
                    nc.vector.tensor_scalar(r, ST[:, t:t + 1], 1.0 / D, EPS, ALU.mult, ALU.add)\
                        .then_inc(ms_t.s, 1)
                    dve.wait_ge(root_t.s, root_t.at(l, t + 1))
                    link(nc.vector.reciprocal(r, r), l)
                    nc.vector.tensor_scalar(XN2[:, t], X[:, t], r, None, ALU.mult).then_inc(xn_t.s, 1)
                h2_out(l, 1)
                nc.vector.memset(AFT, 1.0)
                nc.vector.memset(XB[:, :, :, CAP:XW], 0.0)
                dve.wait_ge(router_mm.s, router_mm.at(l, 1))
                ps = PS[:, 0, 0:NT * NE].rearrange("p (t e) -> p t e", t=NT)
                link(nc.vector.reduce_max(ST, ps, AX), l)
                st = ST.rearrange("p (t o) -> p t o", o=1).to_broadcast([P, NT, NE])
                nc.vector.tensor_tensor(LG, ps, st, ALU.subtract).then_inc(logit_ok.s, 1)
                dve.wait_ge(aexp_ok.s, aexp_ok.at(l, 1))
                link(nc.vector.reduce_sum(ST, LG, AX), l)
                link(nc.vector.reciprocal(RS, ST), l)
                nc.vector.tensor_tensor(AFF, LG, RS.rearrange("p (t o) -> p t o", o=1).to_broadcast([P, NT, NE]),
                                        ALU.mult).then_inc(aff_ok.s, 1)
                dve.wait_ge(aff_t.s, aff_t.at(l, 1))
                link(nc.vector.tensor_copy(WK, PS[0:NE, 1, 0:TOK]), l)
                for lo, hi, rounds in ((0, P, CAP_P // 8), (P, TOK, CAP_S // 8)):
                    for _ in range(rounds):
                        apart(dve)
                        link(nc.vector.max(M8, WK[:, lo:hi]), l)
                        apart(dve)
                        link(nc.vector.match_replace(WK[:, lo:hi], M8, WK[:, lo:hi], -1.0), l)
                link(nc.vector.tensor_scalar(WK, WK, 0.0, None, ALU.is_lt), l)
                for lo, hi in ((0, P), (P, TOK)):
                    ins = nc.vector.tensor_tensor_scan(SN[:, lo:hi], AFT[:, lo:hi], WK[:, lo:hi], 0.0,
                                                       ALU.mult, ALU.add)
                link(ins, l)
                nc.vector.tensor_tensor(SN, SN, WK, ALU.mult).then_inc(pos_ok.s, 1)
                dve.wait_ge(pos_t.s, pos_t.at(l, 1))
                link(nc.vector.tensor_copy(POS, PS[:, 2, 0:NT * NE].rearrange("p (t e) -> p t e", t=NT)), l)
                for t in (1, 2, 0):
                    pos = POS[:, t].rearrange("p (e o) -> p e o", o=1).to_broadcast([P, NE, CAP_S])
                    iota = IOTA.rearrange("p (o s) -> p o s", o=1).to_broadcast([P, NE, CAP_S])
                    nc.vector.tensor_tensor(DD[:, t], pos, iota, ALU.is_equal).then_inc(disp_ok.s, 1)
                dve.wait_ge(disp_ok.s, disp_ok.at(l, NT))
                for t in range(NT):
                    aff = AFF[:, t].rearrange("p (e o) -> p e o", o=1).to_broadcast([P, NE, CAP_S])
                    ins = nc.vector.tensor_tensor(DG[:, t], DD[:, t], aff, ALU.mult)
                ins.then_inc(gated_ok.s, 1)
                for c in range(KC):
                    n = 2 * c + 1
                    dve.wait_ge(gather_mm.s, gather_mm.at(l, n + 1))
                    nc.vector.tensor_scalar(XE[:, c, :, CAP_S:CAP],
                                            gather_bank(c, 0)[:, 0:NE * CAP_P].rearrange("p (e s) -> p e s", e=NE),
                                            AA[:, 1, 0, c:c + 1], MODC[:, 0, 24 + c:25 + c],
                                            ALU.mult, ALU.add).then_inc(gather_dve.s, 1)
                    if c == 5:
                        dve.wait_ge(dgt_mm.s, dgt_mm.at(l, 1))
                        nc.vector.tensor_copy(DGT, PS[:, 4:7, :].rearrange("p a b -> p (a b)")
                                              .rearrange("p (g n) -> p g n", g=NG)).then_inc(dgt_ok.s, 1)
                nc.vector.memset(YS[:, 1], 0.0)
                dve.wait_ge(gather_act.s, gather_act.at(l, 8))
                dve.wait_ge(gather_dve.s, gather_dve.at(l, 8))
                dve.wait_ge(dgt_ok.s, dgt_ok.at(l, 1))
                dve.wait_ge(gb_ok.s, gb_ok.at(l, 2))
                apart(dve)
                with dve.Fori(0, NG) as g:
                    dve.wait_ge(comb_mm.s, comb_mm.in_group(l, g, 0))
                    nc.vector.tensor_copy(DGB, DGT.rearrange("p g n -> p (g n)")[:, bass.ds(g * (NT * P), NT * P)])\
                        .then_inc(dgb_ok.s, 1)

                    def tokens(e):
                        xe = XE[:, :, bass.ds(g * GE + e, 1), :].rearrange("p k e s -> p k (e s)")
                        nc.vector.tensor_copy(XB[:, e % 2, :, 0:CAP], xe).then_inc(xb_ok.s, 1)

                    tokens(0)
                    for e in range(GE):
                        if e + 1 < GE:
                            if e >= 1:
                                dve.wait_ge(gu_mm.s, gu_mm.in_group(l, g, 2 * e))
                            tokens(e + 1)
                        dve.wait_ge(sig_ok.s, sig_ok.in_group(l, g, e + 1))
                        dve.wait_ge(at_mm.s, at_mm.in_group(l, g, e))
                        nc.vector.tensor_tensor(AC, PS[:, e % 2], SGE, ALU.mult).then_inc(silu_ok.s, 1)
                        dve.wait_ge(silu_ok.s, silu_ok.in_group(l, g, e + 1))
                        dve.wait_ge(gu_mm.s, gu_mm.in_group(l, g, 2 * e + 2))
                        nc.vector.tensor_tensor(AC, AC, PS[:, 2 + e % 2], ALU.mult).then_inc(ac_ok.s, 1)
                    for n in range(6):
                        t, h = n // 2, n % 2
                        x = X[:, t, BF * h:BF * h + BF]
                        dve.wait_ge(comb_mm.s, comb_mm.in_group(l, g, n + 1))
                        nc.vector.tensor_tensor(CTMP[:, h], PS[:, 6 + h], G2[:, min(t, 1), BF * h:BF * h + BF],
                                                ALU.mult).then_inc(comb_ok.s, 1)
                        dve.wait_ge(comb_ok.s, comb_ok.in_group(l, g, n + 1))
                        ins = nc.vector.tensor_tensor(x, x, CTMP[:, h], ALU.add)
                        if h == 1:
                            ins.then_inc(xg_ok.s, 1)
                    dve.wait_ge(xg_ok.s, xg_ok.in_group(l, g, NT))
                assert links[0] == DVE_LINKS, ("DVE_LINKS", links[0])
            for t in range(NT):
                dve.wait_ge(fin_ss.s, t + 1)
                nc.vector.tensor_scalar(RS[:, t:t + 1], ST[:, t:t + 1], 1.0 / D, EPS, ALU.mult, ALU.add)\
                    .then_inc(fin_ms.s, 1)
            dve.wait_ge(fn_in.s, 16)
            for t in range(NT):
                dve.wait_ge(fin_root.s, t + 1)
                nc.vector.reciprocal(RS[:, t:t + 1], RS[:, t:t + 1]).then_inc(fin_rec.s, 1)
                dve.wait_ge(fin_rec.s, t + 1)
                nc.vector.scalar_tensor_tensor(out=XN[:, t], in0=X[:, t], scalar=RS[:, t:t + 1], in1=FNG,
                                               op0=ALU.mult, op1=ALU.mult).then_inc(fin_ok.s, 1)

        @block.tensor
        def _(pe):
            def arrived(l, n):
                pe.wait_ge(filled[n % SLOTS].s, filled[n % SLOTS].at(l, (n // SLOTS + 1) * 16))

            owed = []

            def settle(ins):
                if owed:
                    ins.then_inc(used[owed.pop()].s, 1)
                return ins

            def user_bank(l, key):
                n = USER_AT[key]
                if n >= 2:
                    freed = user_dve if USERS[n - 2][0] in BY_DVE else user_act
                    pe.wait_ge(freed.s, freed.at(l, evacuated(n - 2)))
                return PS[:, 6 + n % 2]

            def turn(out, src, rows=P):
                return pe.transpose(out, src, IDT[0:rows, 0:rows])

            def norm_turn(l):
                pe.wait_ge(xn_ok.s, xn_ok.at(l, NT))
                for c in range(KC):
                    if c >= 4:
                        freed = ht_dve if c % 2 else ht_act
                        pe.wait_ge(freed.s, freed.at(l, (c - 4) // 2 + 1))
                    for t in range(NT):
                        ins = turn(PS[:, 4 + c % 4, P * t:P * t + P], XN[:, t, P * c:P * c + P])
                        if (c, t) == (0, 0):
                            settle(ins)
                    ins.then_inc(ht_mm.s, 1)

            def h2_turn(l, n):
                pe.wait_ge(xn_t.s, xn_t.at(l, 2 if n == 0 else 3))
                for c, _, lo, hi, ps in h2_pieces(n):
                    ins = settle(turn(ps, XN2[:, lo // P, P * c:P * c + P]))
                ins.then_inc(h2_mm.s, 1)

            def router(l, tiles):
                for t in tiles:
                    for k in range(KC):
                        ins = pe.matmul(PS[:, 0, NE * t:NE * t + NE], hT[:, k, P * t:P * t + P], WR[:, k],
                                        start=k == 0, stop=k == KC - 1)
                return ins

            def ada(l, i, ps):
                for k in range(KC):
                    n = UNIT["ada", i, k]
                    arrived(l, n)
                    for j in range(4):
                        ins = pe.matmul(ps[32 * j:32 * j + 2], SC[:, k], ring[:, n % SLOTS, BF * j:BF * j + BF],
                                        start=k == 0, stop=k == KC - 1)
                        if j == 0:
                            settle(ins)
                    if k < KC - 1:
                        ins.then_inc(used[n % SLOTS].s, 1)
                owed.append(n % SLOTS)
                return ins

            def mod_turn(i, ps):
                for q in range(4):
                    ins = settle(turn(ps[:, P * q:P * q + P], MODR[:, BF * i + P * q:BF * i + P * q + P]))
                return ins

            def project(l, key, units, stride, width, col, t, last):
                ps = user_bank(l, key)
                for k in range(KC):
                    n = units[k // 2]
                    if k % 2 == 0:
                        arrived(l, n)
                    c0 = (k % 2) * stride + col
                    ins = pe.matmul(ps[:, 0:width], hT[:, k, P * t:P * t + P], ring[:, n % SLOTS, c0:c0 + width],
                                    start=k == 0, stop=k == KC - 1)
                    if k == 0:
                        settle(ins)
                    if last and k % 2 and k < KC - 1:
                        ins.then_inc(used[n % SLOTS].s, 1)
                ins.then_inc(user_mm.s, 1)
                if last:
                    owed.append(n % SLOTS)

            def gate(l, b, c):
                ps = user_bank(l, (f"gate{b}", c))
                n = UNIT[f"gate{b}", c // 2]
                arrived(l, n)
                w = ring[:, n % SLOTS].rearrange("p (k n) -> p k n", k=KC)
                for k in range(KC):
                    ins = pe.matmul(ps[:, 0:TOK], w[:, k, P * (c % 2):P * (c % 2) + P], hT[:, k], start=k == 0,
                                    stop=k == KC - 1)
                    if k == 0:
                        settle(ins)
                ins.then_inc(user_mm.s, 1)
                if c % 2:
                    owed.append(n % SLOTS)

            def branch(l, b, c):
                ps = user_bank(l, (f"br{b}", c))
                n = UNIT[f"br{b}", c // 4]
                arrived(l, n)
                if b < 2:
                    j = 7 if b == 0 else 11
                    pe.wait_ge(user_act.s, user_act.at(l, evacuated(USER_AT["pv", j])))
                else:
                    pe.wait_ge(ot2_ok.s, ot2_ok.at(l, 1))
                w = ring[:, n % SLOTS].rearrange("p (k n) -> p k n", k=4)
                o = (OT0, OT1, OT2)[b]
                for k in range(4):
                    ins = pe.matmul(ps[:, 0:TOK], w[:, k, P * (c % 4):P * (c % 4) + P], o[:, k], start=k == 0,
                                    stop=k == 3)
                    if k == 0:
                        settle(ins)
                ins.then_inc(user_mm.s, 1)
                if c % 4 == 3:
                    owed.append(n % SLOTS)

            def fill(l, key):
                kind = key[0]
                if kind == "c1":
                    project(l, key, [UNIT["c1", u] for u in range(4)], ZG_W, 384, 384 * key[2], key[1],
                            key[1:] == (2, 1))
                elif kind == "c2":
                    half, t, q = key[1] // 6, key[1] % 6 // 2, key[1] % 2
                    project(l, key, [UNIT["c2", 4 * half + u] for u in range(4)], 768, 384, 384 * q, t,
                            (t, q) == (2, 1))
                elif kind.startswith("gate"):
                    gate(l, int(kind[4]), key[1])
                elif kind == "ada":
                    ada(l, key[1], user_bank(l, key)).then_inc(user_mm.s, 1)
                elif kind == "adat":
                    ps = user_bank(l, key)
                    pe.wait_ge(user_dve.s, user_dve.at(l, evacuated(USER_AT["ada", key[1]])))
                    mod_turn(key[1], ps).then_inc(user_mm.s, 1)
                else:
                    branch(l, int(kind[2]), key[1])

            def prep(l, j):
                kind, i = JOBS[j]
                if j >= 2:
                    before = OUT_AT[j - 2, 1 if JOBS[j - 2][0] == "gqa" else 0] + 1
                    pe.wait_ge(pt_act.s, pt_act.at(l, before))
                    pe.wait_ge(pt_dve.s, pt_dve.at(l, before))
                if j == 1:
                    pe.wait_ge(prep_act.s, prep_act.at(l, 1))
                if kind == "mla":
                    if i % 2 == 0:
                        for c in range(2):
                            settle(pe.matmul(PS[:, 4], UKV[:, 0, c, NOPE * i:NOPE * (i + 2)], CKT[:, c],
                                             start=c == 0, stop=c == 1))
                    if i == 0:
                        pe.wait_ge(qrope_ok.s, qrope_ok.at(l, 1))
                    for t in range(NT):
                        ins = turn(PS[0:QD, 5, P * t:P * t + P], QQ[:, t, QD * i:QD * i + QD])
                elif kind == "gqa":
                    if i == 0:
                        pe.wait_ge(gq_ok.s, gq_ok.at(l, 1))
                        for kt, src in enumerate((ZG[:, 0, G_K:G_K + 128], CTX_GK, ZG[:, 1, G_K:G_K + 128],
                                                  ZG[:, 2, G_K:G_K + 128])):
                            settle(turn(PS[:, 4, P * kt:P * kt + P], src))
                    for t in range(NT):
                        ins = turn(PS[:, 5, P * t:P * t + P], ZG[:, t, P * i:P * i + P])
                        if t == 0:
                            settle(ins)
                else:
                    if i == 0:
                        pe.wait_ge(dq_ok.s, dq_ok.at(l, 1))
                    k0 = D_K + P * i
                    for kt, src in enumerate((ZD[:, 0, k0:k0 + P], CTX_DK[:, P * i:P * i + P], ZD[:, 1, k0:k0 + P],
                                              ZD[:, 2, k0:k0 + P])):
                        settle(turn(PS[:, 4, P * kt:P * kt + P], src))
                    for t in range(NT):
                        ins = turn(PS[:, 5, P * t:P * t + P], ZD[:, t, P * i:P * i + P])
                ins.then_inc(prep_mm.s, 1)

            def scores(l, j):
                kind, i = JOBS[j]
                pe.wait_ge(prep_act.s, prep_act.at(l, j + 1))
                pe.wait_ge(prep_dve.s, prep_dve.at(l, key_preps(j)))
                if j >= 1:
                    n = MAP_AT[j - 1, 0 if JOBS[j - 1][0] == "mla" else 1]
                    pe.wait_ge(exp_ok.s, exp_ok.at(l, n + 1))
                if (kind, i) == ("gqa", 0):
                    pe.wait_ge(zero_ok.s, zero_ok.at(l, 1))
                b = j % 2
                for m in range(1 if kind == "mla" else 2):
                    q = QM[0:QD, b] if kind == "mla" else QAB[:, b, m]
                    k = KT[0:QD, b] if kind == "mla" else KT[:, i // 2 if kind == "gqa" else b]
                    settle(pe.matmul(PS[:, 2 * m, 0:384], q[:, P:2 * P], k[:, P:NKEY], start=True, stop=True))
                    pe.matmul(PS[:, 2 * m, 384:512], q[:, 0:P], k[:, 0:P], start=True, stop=True)
                    pe.matmul(PS[:, 2 * m + 1, 0:384], q[:, 2 * P:TOK], k[:, P:NKEY], start=True, stop=True)\
                        .then_inc(score_mm.s, 1)

            def turn_probs(l, j):
                for m in range(2 if JOBS[j][0] == "gqa" else 1):
                    n = OUT_AT[j, m]
                    pe.wait_ge(prob_ok.s, prob_ok.at(l, n + 1))
                    if m == 0 and j + 1 < NJ:
                        pe.wait_ge(prep_act.s, prep_act.at(l, j + 2))
                        pe.wait_ge(prep_dve.s, prep_dve.at(l, key_preps(j + 1)))
                    elif n >= 1:
                        pe.wait_ge(pt_act.s, pt_act.at(l, n))
                        pe.wait_ge(pt_dve.s, pt_dve.at(l, n))
                    p = PB[:, MAP_AT[j, m] % 2]
                    settle(turn(PS[:, 4, 0:P], p[:, 384:512]))
                    for q, at_q in enumerate((0, 512)):
                        turn(PS[:, 4, P * (q + 1):P * (q + 2)], p[:, at_q:at_q + P])
                    for kt in range(1, 3):
                        for q, at_q in enumerate((0, 512)):
                            ins = turn(PS[:, 5, 256 * (kt - 1) + P * q:256 * (kt - 1) + P * q + P],
                                       p[:, at_q + P * kt:at_q + P * kt + P])
                    ins.then_inc(pt_mm.s, 1)

            def values(l, j):
                kind, i = JOBS[j]
                if not values_of(j):
                    return
                ps = user_bank(l, ("pv", j))
                n = OUT_AT[values_of(j)[-1]]
                pe.wait_ge(pt_act.s, pt_act.at(l, n + 1))
                pe.wait_ge(pt_dve.s, pt_dve.at(l, n + 1))
                heads = []
                for r, (job, m) in enumerate(values_of(j)):
                    if kind == "mla":
                        c = 64 * JOBS[job][1]
                        v = [VM[:, kt, c:c + 64] for kt in range(4)]
                    elif kind == "gqa":
                        kv = 64 * (i // 2)
                        c = G_V + kv
                        v = [ZG[:, 0, c:c + 64], CTX_GV[:, kv:kv + 64], ZG[:, 1, c:c + 64],
                             ZG[:, 2, c:c + 64]]
                    else:
                        c = D_V + P * i
                        v = [ZD[:, 0, c:c + P], CTX_DV[:, P * i:P * i + P], ZD[:, 1, c:c + P], ZD[:, 2, c:c + P]]
                    heads.append((ps if kind == "diff" else ps[64 * r:64 * r + 64], v, PT[:, OUT_AT[job, m] % 2]))
                for out, v, pt in heads:
                    settle(pe.matmul(out[:, 0:P], v[0], pt[:, 0:P], start=True, stop=True))
                for kt in range(3):
                    for out, v, pt in heads:
                        ins = pe.matmul(out[:, P:TOK], v[kt + 1], pt[:, P + 256 * kt:P + 256 * kt + 256],
                                        start=kt == 0, stop=kt == 2)
                ins.then_inc(user_mm.s, 1)

            def gate_rows(l, which, bank):
                for s in range(2):
                    for h in range(2):
                        row = 32 * (2 * which + h) + s
                        ins = pe.matmul(PS[:, bank + 2 * s + h], IDT[:, row:row + 1].to_broadcast([P, P]),
                                        MODR[:, BF * (1 + which):BF * (2 + which)], start=True, stop=True)
                        if (s, h) == (0, 0):
                            settle(ins)
                ins.then_inc(gb_mm.s, 1)

            for free in (*used, router_mm, at_mm, comb_mm):
                pe.sem_inc(free.s, 1)
            pe.wait_ge(const_in.s, 16)
            pe.wait_ge(cond_in.s, 32)
            turn(PS[:, 0, 0:16], CR, 16).then_inc(cond_t.s, 1)
            pe.wait_ge(cond_ok.s, 1)
            with pe.Fori(0, DEPTH) as l:
                pe.wait_ge(early_in.s, early_in.at(l, 96))
                apart(pe)
                turn(PS[:, 3, 0:16], NR, 16).then_inc(mod_t.s, 1)

                ada(l, 0, PS[:, 0]).then_inc(ada_mm.s, 1)
                pe.wait_ge(mod_row.s, mod_row.at(l, 1))
                pe.wait_ge(ncol_ok.s, ncol_ok.at(l, 1))
                mod_turn(0, PS[:, 3]).then_inc(mod_t.s, 1)
                norm_turn(l)
                pe.wait_ge(ht_act.s, ht_act.at(l, 4))
                pe.wait_ge(ht_dve.s, ht_dve.at(l, 4))
                units = [UNIT["c0", u] for u in range(4)]
                for t in range(NT):
                    for h in range(2):
                        project(l, ("c0", t, h), units, ZA_W, 336, 336 * h, t, (t, h) == (2, 1))
                for h in range(2):
                    fill(l, ("c1", 0, h))
                pe.wait_ge(za_ok.s, za_ok.at(l, 1))
                for c in range(3):
                    for t in range(NT):
                        ins = turn(PS[:, c, P * t:P * t + P], ZA[:, t, P * c:P * c + P])
                        if (c, t) == (0, 0):
                            settle(ins)
                ins.then_inc(tr_mm.s, 1)
                pe.wait_ge(late_in.s, late_in.at(l, 18 * 16))
                for c in range(2):
                    k0 = Z_KV + P * c
                    for kt, src in enumerate((ZA[:, 0, k0:k0 + P], CTX_CKV[:, P * c:P * c + P], ZA[:, 1, k0:k0 + P],
                                              ZA[:, 2, k0:k0 + P])):
                        ins = turn(PS[:, 3 + c, P * kt:P * kt + P], src)
                ins.then_inc(tr_mm.s, 1)
                pe.wait_ge(kpe_ok.s, kpe_ok.at(l, 1))
                for kt, src in enumerate((ZA[:, 0, Z_PE:Z_PE + ROPE], CTX_KPE, KPR[:, 0], KPR[:, 1])):
                    ins = turn(PS[0:ROPE, 5, P * kt:P * kt + P], src)
                ins.then_inc(tr_mm.s, 1)
                pe.wait_ge(tr_act.s, tr_act.at(l, 1))
                for t in range(NT):
                    for h in range(2):
                        ps = user_bank(l, ("q", t, h))
                        for k in range(3):
                            n = UNIT["uq", k // 2]
                            arrived(l, n)
                            c0 = (k % 2) * 768 + 384 * h
                            ins = pe.matmul(ps[:, 0:384], CQT[:, k, P * t:P * t + P],
                                            ring[:, n % SLOTS, c0:c0 + 384], start=k == 0, stop=k == 2)
                            if (t, h) == (2, 1) and k == 1:
                                ins.then_inc(used[n % SLOTS].s, 1)
                        ins.then_inc(user_mm.s, 1)
                owed.append(n % SLOTS)
                pe.wait_ge(tr_dve.s, tr_dve.at(l, 2))
                for kt in range(4):
                    ps = user_bank(l, ("v", kt))
                    for c in range(2):
                        ins = pe.matmul(ps, CKT[:, c, P * kt:P * kt + P], UKV[:, 1, c], start=c == 0, stop=c == 1)
                        if c == 0:
                            settle(ins)
                    ins.then_inc(user_mm.s, 1)
                prep(l, 0)
                for i in range(NJ + 1):
                    if i < NJ:
                        scores(l, i)
                    if i + 1 < NJ:
                        prep(l, i + 1)
                    if i >= 1:
                        values(l, i - 1)
                    for key in FILL[i]:
                        fill(l, key)
                    if i < NJ:
                        turn_probs(l, i)
                for c in range(KC):
                    gate(l, 2, c)
                    if c == 1:
                        pe.wait_ge(sqd_ok.s, sqd_ok.at(l, 1))
                        for h in range(4):
                            ins = pe.matmul(PS[:, h, 0:TOK], ONES, SQD[:, h], start=True, stop=True)
                            if h == 0:
                                settle(ins)
                        ins.then_inc(sqd_mm.s, 1)
                pe.wait_ge(msd_ok.s, msd_ok.at(l, 1))
                pe.wait_ge(stored_d.s, stored_d.at(l, 32))
                gate_rows(l, 0, 0)
                for c in range(KC):
                    branch(l, 2, c)
                pe.wait_ge(user_dve.s, user_dve.at(l, evacuated(USER_AT["br2", KC - 1])))
                for t in range(NT):
                    for h in range(2):
                        if (t, h) == (2, 1):
                            pe.wait_ge(gb_ok.s, gb_ok.at(l, 1))
                            h2_turn(l, 0)
                        ps = user_bank(l, ("out", t, h))
                        for k in range(KC):
                            n = UNIT["wout", k // 2]
                            arrived(l, n)
                            c0 = (k % 2) * D + BF * h
                            ins = pe.matmul(ps, MG[:, k, P * t:P * t + P], ring[:, n % SLOTS, c0:c0 + BF],
                                            start=k == 0, stop=k == KC - 1)
                            if k == 0:
                                settle(ins)
                            if (t, h) == (2, 1) and k % 2 and k < KC - 1:
                                ins.then_inc(used[n % SLOTS].s, 1)
                        ins.then_inc(user_mm.s, 1)
                owed.append(n % SLOTS)
                pe.wait_ge(h2_act.s, h2_act.at(l, 1))
                pe.wait_ge(h2_dve.s, h2_dve.at(l, 1))
                settle(router(l, (0, 1)))
                h2_turn(l, 1)
                pe.wait_ge(h2_act.s, h2_act.at(l, 2))
                pe.wait_ge(h2_dve.s, h2_dve.at(l, 2))
                router(l, (2,)).then_inc(router_mm.s, 1)
                pe.wait_ge(aff_ok.s, aff_ok.at(l, 1))
                for t in range(NT):
                    ins = turn(PS[0:NE, 1, P * t:P * t + P], AFF[:, t])
                ins.then_inc(aff_t.s, 1)
                gate_rows(l, 1, 4)
                pe.wait_ge(pos_ok.s, pos_ok.at(l, 1))
                apart(pe)
                for t in range(NT):
                    ins = turn(PS[:, 2, NE * t:NE * t + NE], SN[:, P * t:P * t + P], NE)
                ins.then_inc(pos_t.s, 1)
                def gather(c):
                    if c == 4:
                        pe.wait_ge(gated_ok.s, gated_ok.at(l, 1))
                        for n in range(NG * NT):
                            src = DG[:, n % NT, GE * (n // NT):GE * (n // NT) + GE].rearrange("p e s -> p (e s)")
                            ins = turn(PS[:, 4 + n // 4, P * (n % 4):P * (n % 4) + P], src)
                        ins.then_inc(dgt_mm.s, 1)
                    if c >= 2:
                        pe.wait_ge(gather_act.s, gather_act.at(l, c - 1))
                        pe.wait_ge(gather_dve.s, gather_dve.at(l, c - 1))
                    for t in range(1, 3):
                        ins = pe.matmul(gather_bank(c, 1), XN2[:, t, P * c:P * c + P],
                                        DD[:, t].rearrange("p e s -> p (e s)"), start=t == 1, stop=t == 2)
                    ins.then_inc(gather_mm.s, 1)
                    if c == 0:
                        pe.wait_ge(disp_ok.s, disp_ok.at(l, NT))
                    pe.matmul(gather_bank(c, 0)[:, 0:NE * CAP_P], XN2[:, 0, P * c:P * c + P],
                              DD[:, 0, :, 0:CAP_P], start=True, stop=True).then_inc(gather_mm.s, 1)

                def wide(g, e, first, u, lhs, bank, done):
                    i = first + u
                    pe.wait_ge(filled[i].s, (expert_use(l, i, g, e) + 1) * 16)
                    for k in range(2 * u, 2 * u + 2):
                        for h in range(2):
                            c0 = (k % 2) * D + BF * h
                            ins = pe.matmul(PS[64 * h:64 * h + 64, bank], lhs(k), slots[i][:, c0:c0 + BF],
                                            start=k == 0, stop=k == KC - 1)
                            if (k, h) == (0, 0):
                                settle(ins)
                    if u < 3:
                        ins.then_inc(used[i].s, 1)
                    else:
                        ins.then_inc(done.s, 1)
                        owed.append(i)

                def experts(g, opening):
                    for e in range(GE):
                        if opening and e == 0:
                            first_tokens = XE.rearrange("p k e s -> p k (e s)")[:, :, 0:XW]
                            for c in range(4):
                                gather(c)
                            for u in range(4):
                                pe.wait_ge(gather_act.s, gather_act.at(l, 2 * u + 2))
                                pe.wait_ge(gather_dve.s, gather_dve.at(l, 2 * u + 2))
                                wide(g, e, 0, u, lambda k: first_tokens[:, k], e % 2, gu_mm)
                                if u < 2:
                                    gather(2 * u + 4)
                                    gather(2 * u + 5)
                            for u in range(4):
                                wide(g, e, 4, u, lambda k: first_tokens[:, k], 2 + e % 2, gu_mm)
                        else:
                            pe.wait_ge(xb_ok.s, xb_ok.in_group(l, g, e + 1))
                            for u in range(4):
                                wide(g, e, 0, u, lambda k: XB[:, e % 2, k], e % 2, gu_mm)
                            for u in range(4):
                                wide(g, e, 4, u, lambda k: XB[:, e % 2, k], 2 + e % 2, gu_mm)
                        pe.wait_ge(ac_ok.s, ac_ok.in_group(l, g, e + 1))
                        for q in range(4):
                            ins = turn(PS[:, 4, P * q:P * q + P], AC[:, P * q:P * q + P])
                            if q == 0:
                                settle(ins)
                        ins.then_inc(at_mm.s, 1)
                        pe.wait_ge(at_ok.s, at_ok.in_group(l, g, e + 1))
                        pe.wait_ge(y_ok.s, y_ok.in_group(l, g, e))
                        for u in range(4):
                            wide(g, e, 8, u, lambda k: AT[:, k % 4, XW * (k // 4):XW * (k // 4) + XW], 5, y_mm)
                    pe.wait_ge(dgb_ok.s, dgb_ok.in_group(l, g, 1))
                    pe.wait_ge(y_ok.s, y_ok.in_group(l, g, GE))
                    for n in range(6):
                        t, h = n // 2, n % 2
                        pe.wait_ge(comb_ok.s, comb_ok.in_group(l, g, max(n - 1, 0)))
                        w = DGB[:, P * t:P * t + P]
                        for half in range(2):
                            y = YS[:, 0 if t else 1, BF * h + 256 * half:BF * h + 256 * half + 256]
                            ins = pe.matmul(PS[:, 6 + h, 256 * half:256 * half + 256], w, y, start=True, stop=True)
                            if half == 0:
                                settle(ins)
                        ins.then_inc(comb_mm.s, 1)
                    assert not owed

                pe.wait_ge(gb_ok.s, gb_ok.at(l, 2))
                pe.wait_ge(disp_ok.s, disp_ok.at(l, 2))
                experts(0, True)
                with pe.Fori(1, NG) as g:
                    experts(g, False)


_INS = ["x_prompt", "x_sample", "cache_mla_ckv", "cache_mla_kpe", "cache_gqa_k", "cache_gqa_v", "cache_diff_k",
        "cache_diff_v", "c", "c_ctx", "w_ada", "b_ada", "norm1", "norm2", "w_in", "mla_q_norm", "mla_kv_norm",
        "mla_w_uq", "mla_w_uk", "mla_w_uv", "gqa_q_norm", "gqa_k_norm", "diff_lam_q1", "diff_lam_k1",
        "diff_lam_q2", "diff_lam_k2", "diff_subln", "w_br_mla", "w_br_gqa", "w_br_diff", "w_out", "w_router",
        "w_gate", "w_up", "w_down", "final_norm"]
_OUTS = [("y_prompt", (1, 128, 1024)), ("y_sample", (1, 256, 1024)), ("new_ckv", (1, 2, 128, 256)),
         ("new_kpe", (1, 2, 128, 32)), ("new_gk", (1, 2, 128, 2, 64)), ("new_gv", (1, 2, 128, 2, 64)),
         ("new_dk", (1, 2, 128, 4, 128)), ("new_dv", (1, 2, 128, 4, 128))]


def kernel(**inputs):
    import concourse.bacc as bacc
    from concourse.bass_utils import run_bass_kernel_spmd

    nc = bacc.Bacc("TRN2", target_bir_lowering=False, num_devices=1)
    arrays, args = {}, {}
    for name in _INS:
        x = np.ascontiguousarray(inputs[name])
        arrays[f"in_{name}"] = x
        args[name] = nc.dram_tensor(f"in_{name}", x.shape, mybir.dt.from_np(x.dtype), kind="ExternalInput").ap()
    arrays["in_constants"] = constants()
    args["constants"] = nc.dram_tensor("in_constants", (P, C_W), F32, kind="ExternalInput").ap()
    for name, shape in _OUTS:
        args[name] = nc.dram_tensor(f"out_{name}", shape, F32, kind="ExternalOutput").ap()
    backbone(nc, args)
    r = run_bass_kernel_spmd(nc, [arrays], core_ids=[0])
    return tuple(r.results[0][f"out_{name}"] for name, _ in _OUTS)
```
